# Optimizing a Trainium2 kernel written in Bass

```python
import jax, jax.numpy as jnp
from jax import lax
import numpy as np

D_MODEL = 1024
BATCH = 1
SEQ = 512
DEPTH = 1

N_META = 16
EPS = 1e-6
ROPE_THETA = 10000.0
GLA_HEADS = 4
GLA_DK = 64
GLA_DV = 128
GLA_LOWRANK = 16
GLA_GATE_NORM = 16.0
GLA_CHUNK = 64
DSA_HEADS = 8
DSA_HD = 64
IDX_HEADS = 8
IDX_HD = 64
TOPK_MAX = 256
Q_BLOCK = 128
D_FF = 2816

GLA_WIDTH = GLA_HEADS * GLA_DV
DSA_WIDTH = DSA_HEADS * DSA_HD
MIX_WIDTH = GLA_WIDTH + DSA_WIDTH
IN_SIZES = (GLA_HEADS * GLA_DK, GLA_HEADS * GLA_DK, GLA_WIDTH, GLA_WIDTH, GLA_LOWRANK,
            DSA_WIDTH, DSA_WIDTH, DSA_WIDTH, IDX_HEADS * IDX_HD, IDX_HD, IDX_HEADS)
IN_COLS = sum(IN_SIZES)

kernel_name = "hymba_gla_dsa_macaron"

def rmsnorm(x, g):
    x32 = x.astype(jnp.float32)
    y = x32 * lax.rsqrt(jnp.mean(x32 * x32, axis=-1, keepdims=True) + EPS)
    return (y * g.astype(jnp.float32)).astype(x.dtype)

def swiglu(h, w_gate, w_up, w_down):
    return (jax.nn.silu(h @ w_gate) * (h @ w_up)) @ w_down

def rope_tables(L, dim):
    pos = jnp.arange(L, dtype=jnp.float32)
    inv_freq = 1.0 / (ROPE_THETA ** (jnp.arange(0, dim, 2, dtype=jnp.float32) / dim))
    ang = pos[:, None] * inv_freq[None, :]
    ang = jnp.concatenate([ang, ang], axis=-1)
    return jnp.cos(ang), jnp.sin(ang)

def apply_rope(x, cos, sin):
    half = x.shape[-1] // 2
    rot = jnp.concatenate([-x[..., half:], x[..., :half]], axis=-1)
    c = cos[None, :, None, :].astype(x.dtype)
    s = sin[None, :, None, :].astype(x.dtype)
    return x * c + rot * s

def gla_mixer(q, k, v, r, a_low, w_a2, b_a, head_norm):
    B, L, _ = q.shape
    dt = q.dtype
    f32 = jnp.float32
    q = q.reshape(B, L, GLA_HEADS, GLA_DK).astype(f32) * (GLA_DK ** -0.5)
    k = k.reshape(B, L, GLA_HEADS, GLA_DK).astype(f32)
    v = v.reshape(B, L, GLA_HEADS, GLA_DV).astype(f32)
    g = jax.nn.log_sigmoid((a_low @ w_a2 + b_a).astype(f32)) / GLA_GATE_NORM
    g = g.reshape(B, L, GLA_HEADS, GLA_DK)
    pad = GLA_CHUNK - N_META

    def to_chunks(t):
        t = jnp.pad(t, ((0, 0), (pad, 0), (0, 0), (0, 0)))
        nc = t.shape[1] // GLA_CHUNK
        return t.reshape(B, nc, GLA_CHUNK, GLA_HEADS, t.shape[-1]).transpose(1, 0, 3, 2, 4)

    qc, kc, vc, gc = to_chunks(q), to_chunks(k), to_chunks(v), to_chunks(g)
    causal = jnp.tril(jnp.ones((GLA_CHUNK, GLA_CHUNK), dtype=bool))

    def step(S, inp):
        qb, kb, vb, gb = inp
        b = jnp.cumsum(gb, axis=2)
        o_inter = jnp.einsum('bhcd,bhde->bhce', qb * jnp.exp(b), S)
        diff = b[:, :, :, None, :] - b[:, :, None, :, :]
        decay = jnp.exp(jnp.where(causal[None, None, :, :, None], diff, -jnp.inf))
        A = jnp.einsum('bhid,bhjd,bhijd->bhij', qb, kb, decay)
        o_intra = jnp.einsum('bhij,bhje->bhie', A, vb)
        b_last = b[:, :, -1:, :]
        S_new = jnp.exp(b_last[:, :, 0, :])[..., None] * S + \
            jnp.einsum('bhjd,bhje->bhde', kb * jnp.exp(b_last - b), vb)
        return S_new, o_inter + o_intra

    S0 = jnp.zeros((B, GLA_HEADS, GLA_DK, GLA_DV), f32)
    _, oc = lax.scan(step, S0, (qc, kc, vc, gc))
    o = oc.transpose(1, 0, 3, 2, 4).reshape(B, -1, GLA_HEADS, GLA_DV)[:, pad:]
    o = rmsnorm(o, head_norm)
    o = o.reshape(B, L, GLA_WIDTH) * jax.nn.silu(r.astype(f32))
    return o.astype(dt)

def dsa_mixer(q, k, v, iq, ik, iw, cos, sin, k_sel):
    B, L, _ = q.shape
    f32 = jnp.float32
    q = apply_rope(q.reshape(B, L, DSA_HEADS, DSA_HD), cos, sin)
    k = apply_rope(k.reshape(B, L, DSA_HEADS, DSA_HD), cos, sin)
    v = v.reshape(B, L, DSA_HEADS, DSA_HD)
    iq = apply_rope(iq.reshape(B, L, IDX_HEADS, IDX_HD), cos, sin)
    ik = apply_rope(ik.reshape(B, L, 1, IDX_HD), cos, sin)[:, :, 0]
    iw = iw * (IDX_HEADS ** -0.5)
    n_blk = -(-L // Q_BLOCK)
    Lp = n_blk * Q_BLOCK

    def to_blocks(t):
        t = jnp.pad(t, ((0, 0), (0, Lp - L)) + ((0, 0),) * (t.ndim - 2))
        t = t.reshape((B, n_blk, Q_BLOCK) + t.shape[2:])
        return jnp.moveaxis(t, 1, 0)

    key_pos = jnp.arange(L)
    q_pos = jnp.arange(Lp).reshape(n_blk, Q_BLOCK)

    def block(args):
        qb, iqb, iwb, tq = args
        idx_logits = jnp.einsum('bqhd,bsd->bqhs', iqb, ik) * (IDX_HD ** -0.5)
        score = jnp.einsum('bqh,bqhs->bqs', iwb, jax.nn.relu(idx_logits)).astype(f32)
        visible = key_pos[None, :] <= tq[:, None]
        score = jnp.where(visible[None], score, -jnp.inf)
        _, idx = lax.top_k(score, k_sel)
        ks = jax.vmap(lambda kk, ii: kk[ii])(k, idx)
        vs = jax.vmap(lambda vv, ii: vv[ii])(v, idx)
        logits = jnp.einsum('bqhd,bqkhd->bhqk', qb, ks).astype(f32) * (DSA_HD ** -0.5)
        valid = idx <= tq[None, :, None]
        logits = jnp.where(valid[:, None], logits, -jnp.inf)
        p = jax.nn.softmax(logits, axis=-1).astype(vs.dtype)
        return jnp.einsum('bhqk,bqkhd->bqhd', p, vs)

    out = lax.map(block, (to_blocks(q), to_blocks(iq), to_blocks(iw), q_pos))
    out = jnp.moveaxis(out, 0, 1).reshape(B, Lp, DSA_WIDTH)[:, :L]
    return out

def token_mixing(hn, w_in, gla_w_a2, gla_b_a, gla_head_norm, w_out, cos, sin, k_sel):
    proj = hn @ w_in
    split_points = np.cumsum(IN_SIZES)[:-1].tolist()
    gq, gk, gv, gr, ga, dq, dk, dv, iq, ik, iw = jnp.split(proj, split_points, axis=-1)
    o_gla = gla_mixer(gq, gk, gv, gr, ga, gla_w_a2, gla_b_a, gla_head_norm)
    o_dsa = dsa_mixer(dq, dk, dv, iq, ik, iw, cos, sin, k_sel)
    return jnp.concatenate([o_gla, o_dsa], axis=-1) @ w_out

def setup_inputs(seed: int = 0) -> dict:
    key = jax.random.key(seed)
    ks = jax.random.split(key, 20)
    f32 = jnp.float32

    def w(k, shape, fan_in):
        return jax.random.normal(k, shape, f32) * (fan_in ** -0.5)

    def gain(k, shape):
        return 1.0 + 0.02 * jax.random.normal(k, shape, f32)

    return {
        "x": jax.random.normal(ks[0], (BATCH, SEQ, D_MODEL), f32),
        "meta_tokens": jax.random.normal(ks[1], (N_META, D_MODEL), f32),
        "ffn1_norm": gain(ks[2], (DEPTH, D_MODEL)),
        "ffn1_w_gate": w(ks[3], (DEPTH, D_MODEL, D_FF), D_MODEL),
        "ffn1_w_up": w(ks[4], (DEPTH, D_MODEL, D_FF), D_MODEL),
        "ffn1_w_down": w(ks[5], (DEPTH, D_FF, D_MODEL), D_FF),
        "mix_norm": gain(ks[6], (DEPTH, D_MODEL)),
        "w_in": w(ks[7], (DEPTH, D_MODEL, IN_COLS), D_MODEL),
        "gla_w_a2": w(ks[8], (DEPTH, GLA_LOWRANK, GLA_HEADS * GLA_DK), GLA_LOWRANK),
        "gla_b_a": 0.01 * jax.random.normal(ks[9], (DEPTH, GLA_HEADS * GLA_DK), f32),
        "gla_head_norm": gain(ks[10], (DEPTH, GLA_DV)),
        "w_out": w(ks[11], (DEPTH, MIX_WIDTH, D_MODEL), MIX_WIDTH),
        "ffn2_norm": gain(ks[12], (DEPTH, D_MODEL)),
        "ffn2_w_gate": w(ks[13], (DEPTH, D_MODEL, D_FF), D_MODEL),
        "ffn2_w_up": w(ks[14], (DEPTH, D_MODEL, D_FF), D_MODEL),
        "ffn2_w_down": w(ks[15], (DEPTH, D_FF, D_MODEL), D_FF),
        "final_norm": gain(ks[16], (D_MODEL,)),
    }

def reference(x, meta_tokens, ffn1_norm, ffn1_w_gate, ffn1_w_up, ffn1_w_down, mix_norm, w_in,
              gla_w_a2, gla_b_a, gla_head_norm, w_out, ffn2_norm, ffn2_w_gate, ffn2_w_up,
              ffn2_w_down, final_norm):
    B, S, _ = x.shape
    k_sel = min(TOPK_MAX, S // 4)
    meta = jnp.broadcast_to(meta_tokens[None].astype(x.dtype), (B, N_META, D_MODEL))
    h = jnp.concatenate([meta, x], axis=1)
    L = h.shape[1]
    cos, sin = rope_tables(L, DSA_HD)
    for layer in range(DEPTH):
        h = h + 0.5 * swiglu(rmsnorm(h, ffn1_norm[layer]), ffn1_w_gate[layer], ffn1_w_up[layer], ffn1_w_down[layer])
        h = h + token_mixing(rmsnorm(h, mix_norm[layer]), w_in[layer], gla_w_a2[layer], gla_b_a[layer],
                             gla_head_norm[layer], w_out[layer], cos, sin, k_sel)
        h = h + 0.5 * swiglu(rmsnorm(h, ffn2_norm[layer]), ffn2_w_gate[layer], ffn2_w_up[layer], ffn2_w_down[layer])
    h = rmsnorm(h, final_norm)
    return h[:, N_META:]


_drawn_inputs = setup_inputs


def setup_inputs(seed=0):
    import zlib

    import numpy as np

    out = dict(_drawn_inputs(seed))
    spreads = {}
    factors = {'ffn1_norm': 4.279,
     'mix_norm': 2.689,
     'gla_b_a': 8.0,
     'gla_head_norm': 6.431,
     'ffn2_norm': 7.825,
     'final_norm': 2.857}
    for name, (base, spread) in spreads.items():
        noise = np.random.default_rng([zlib.crc32(name.encode()), seed]).standard_normal(out[name].shape)
        drawn = base * np.exp(spread * noise) if base else spread * noise
        out[name] = __import__('jax').numpy.asarray(drawn.astype(out[name].dtype))
    for name, factor in factors.items():
        out[name] = (out[name] * factor).astype(out[name].dtype)
    return out
```

```python
import math
from contextlib import ExitStack

import concourse.bass as bass
from concourse import mybir

F32 = mybir.dt.float32
F32R = mybir.dt.float32r
U8 = mybir.dt.uint8
ALU = mybir.AluOpType
ACT = mybir.ActivationFunctionType
AX_X = mybir.AxisListType.X

P = 128
D = 1024
KT = D // P
META, SEQ = 16, 512
TOK = META + SEQ
HALF = TOK // 2
D_FF = 2816
FT = D_FF // P
EPS = 1e-6
GLA_HEADS, DK, DV = 4, 64, 128
HD = 64
HEADS = 8
TOPK = min(256, SEQ // 4)
GATE_NORM = 16.0
RING = 4
UNIT = KT * P
ONE = 1
NEG = -1.0e30
TAKEN = -3.0e38

GROUPS = [(0, 8), (8, 8), (16, FT - 16)]
FFN_UNITS = 2 * FT + KT * len(GROUPS)

C_GQK, C_GV, C_GR, C_GA, C_DQK, C_DV, C_IQ, C_IK = 0, 512, 1024, 1536, 1552, 2576, 3088, 3600
N_GA, N_IKW = 16, HD + HEADS

M_IQ, M_IKW, M_GA, M_GV, M_RAW, M_DV, MIX_UNITS = 0, 4, 5, 6, 10, 26, 30
U_FFN1 = 0
U_MIX = U_FFN1 + FFN_UNITS
U_OUT = U_MIX + MIX_UNITS
U_FFN2 = U_OUT + KT
U_END = U_FFN2 + FFN_UNITS

BLK = [(0, TOPK)] + [(TOPK + 100 * i, 100) for i in range((TOK - TOPK) // 100)]
SEEN = [s + n for s, n in BLK]
MASK_AT = [sum(SEEN[:b]) for b in range(len(BLK))]
WIN = [(w, min(P, TOK - w)) for w in range(0, TOK, P)]
FULL_WIN = TOK // P
LEVELS = [1, 2, 4, 8, 16, 32, 64]
RC_WIN = [0, 1, 2, 3, 9]
RC_BLK = [4, 5, 6, 7, 8]


def at(i, step, base):
    return base if i is None else i * step + base


def halves(ap):
    return ap.rearrange("p (a n) -> p a n", a=2)


def build(nc, x, meta, ffn1, ffn2, mix_norm, w_in, w_a2, b_a, head_norm, w_out, final_norm,
          cos_t, sin_t, out, stop_after=None):
    ctx = ExitStack()
    with ctx:
        def sb(name, shape, dt=F32, scope=ctx):
            return scope.enter_context(nc.sbuf_tensor(name, shape, dt))

        def sem(name):
            return ctx.enter_context(nc.semaphore(name))

        ps = ctx.enter_context(nc.psum_tensor("ps", [P, 8, 512], F32))
        h = sb("h", [P, KT, TOK])
        xh = sb("xh", [P, KT, TOK], F32R)
        xl = sb("xl", [P, KT, TOK], F32R)
        raw = sb("raw", [P, RING, UNIT])
        wh = sb("wh", [P, RING, UNIT], F32R)
        wl = sb("wl", [P, RING, UNIT], F32R)
        rstd = sb("rstd", [P, TOK])
        ss = sb("ss", [P, TOK])
        t0 = sb("t0", [P, TOK])
        t1 = sb("t1", [P, TOK])
        ident = sb("ident", [P, P])
        ones = sb("ones", [P, P])
        vec_rows = sb("vec_rows", [4 * KT + 3, P])
        vecs = sb("vecs", [P, 4 * KT + 3])
        gains = vecs[:, 0:4 * KT].rearrange("p (n k) -> p n k", k=KT)
        ba = vecs[:, 4 * KT:4 * KT + 2]
        hn = vecs[:, 4 * KT + 2:4 * KT + 3]
        scrap = sb("scrap", [P, 1])
        ffn_scope = ExitStack()
        ah = sb("ah", [P, KT, TOK], F32R, ffn_scope)
        al = sb("al", [P, KT, TOK], F32R, ffn_scope)
        xin = sb("xin", [P, 5, D], F32, ffn_scope)
        ffn_scope.close()
        pja = sb("pja", [P, 8, TOK])
        iq = sb("iq", [P, 4, TOK])
        sw = sb("sw", [P, 4, TOK])
        pjb = sb("pjb", [P, 8, TOK])
        dv = sb("dv", [P, 5, 512])
        mask = sb("mask", [P, sum(SEEN)])
        cosr = sb("cosr", [P, TOK])
        sinr = sb("sinr", [P, TOK])
        ik = sb("ik", [P, TOK])
        ga = sb("ga", [P, TOK])
        gb = sb("gb", [P, 2, TOK])
        tri = sb("tri", [P, P])
        lvm = sb("lvm", [P, len(LEVELS), P], U8)
        S = t1[:, 0:GLA_HEADS * DV].rearrange("p (g n) -> p g n", g=GLA_HEADS)
        small = sb("small", [P, 96])
        rcol = small[:, 0:10]
        iwt = small[:, 16:48]
        top8 = small[:, 48:56]
        elast = small[:, 56:66]
        wa2 = sb("wa2", [N_GA, 2, P])
        gla_scope = ExitStack()
        xa = sb("xa", [P, 2, TOK], F32, gla_scope)
        xb = sb("xb", [P, 2, TOK], F32, gla_scope)
        gv = sb("gv", [P, 5, 512], F32, gla_scope)
        gla_scope.close()
        lg = sb("lg", [P, 2, TOK])
        pr = sb("pr", [P, 2, TOK])
        pt = sb("pt", [P, 2, 512])
        otok = sb("otok", [P, 5, P])
        qst, kst = ik, gb[:, 0, :]
        stat = small[:, 66:76]
        AT = iq[:, :, :].rearrange("p a n -> p (a n)")
        oT = sw

        def at_win(w):
            width = WIN[w][1]
            base = w * GLA_HEADS * P
            return AT[0:width, base:base + GLA_HEADS * width].rearrange("p (e t n) -> p e t n", e=2, t=2)

        w_in_slot = [sem(f"w_in_slot{i}") for i in range(RING)]
        w_hi = sem("w_hi")
        w_split = sem("w_split")
        w_used = sem("w_used")
        x_loaded, const_loaded, mix_loaded = sem("x_loaded"), sem("const_loaded"), sem("mix_loaded")
        vecs_turned, vecs_kept = sem("vecs_turned"), sem("vecs_kept")
        c_zero, consts, lv_step = sem("c_zero"), sem("consts"), sem("lv_step")
        x_turned, x_kept = sem("x_turned"), sem("x_kept")
        h_done, sq_done, ss_zero, ss_done = sem("h_done"), sem("sq_done"), sem("ss_zero"), sem("ss_done")
        x_hi, x_lo = sem("x_hi"), sem("x_lo")
        norm_sum, var_done, inv_done, rstd_done = sem("norm_sum"), sem("var_done"), sem("inv_done"), sem("rstd_done")
        gate_scaled, up_scaled, silu_done = sem("gate_scaled"), sem("up_scaled"), sem("silu_done")
        a_prod, a_hi, a_lo = sem("a_prod"), sem("a_hi"), sem("a_lo")
        tables_done, pj_kept = sem("tables_done"), sem("pj_kept")
        iw_scaled, ga_scaled = sem("iw_scaled"), sem("ga_scaled")
        swapped = [sem(f"swapped{i}") for i in range(13)]
        rope_sin, rope_cos, rope_done = sem("rope_sin"), sem("rope_cos"), sem("rope_done")
        ik_copied = sem("ik_copied")
        tok_turned, tok_kept, v_kept = sem("tok_turned"), sem("tok_kept"), sem("v_kept")
        idx_done, relu_done, acc_done = sem("idx_done"), sem("relu_done"), sem("acc_done")
        top_found, top_taken, mask_done = sem("top_found"), sem("top_taken"), sem("mask_done")
        q_sin, q_cos, q_roped = sem("q_sin"), sem("q_cos"), sem("q_roped")
        z_done, gate_y, gate_abs, gate_exp, gate_ln, gate_g, gate_cum = (
            sem("z_done"), sem("gate_y"), sem("gate_abs"), sem("gate_exp"), sem("gate_ln"), sem("gate_g"),
            sem("gate_cum"))
        gqk_scaled, lv_diff, lv_exp, lv_x, lv_mm, at_done = (
            sem("gqk_scaled"), sem("lv_diff"), sem("lv_exp"), sem("lv_x"), sem("lv_mm"), sem("at_done"))
        kd_turned, kd_kept, s_mm, s_new, o_mm, o_kept = (
            sem("kd_turned"), sem("kd_kept"), sem("s_mm"), sem("s_new"), sem("o_mm"), sem("o_kept"))
        o_sq, o_sum, o_var, o_inv, o_rstd, gr_scaled, gr_silu, o_step, m_hi, m_lo = (
            sem("o_sq"), sem("o_sum"), sem("o_var"), sem("o_inv"), sem("o_rstd"), sem("gr_scaled"),
            sem("gr_silu"), sem("o_step"), sem("m_hi"), sem("m_lo"))
        staged, qk_done, lg_done, max_done, exp_done, sum_inv, pt_done, pt_kept, pv_done, pv_kept, ot_turned = (
            sem("staged"), sem("qk_done"), sem("lg_done"), sem("max_done"), sem("exp_done"), sem("sum_inv"),
            sem("pt_done"), sem("pt_kept"), sem("pv_done"), sem("pv_kept"), sem("ot_turned"))
        kd_ready, qe_ready, kd_diff, kd_exp, qe_exp, el_exp, s_zero = (
            sem("kd_ready"), sem("qe_ready"), sem("kd_diff"), sem("kd_exp"), sem("qe_exp"), sem("el_exp"),
            sem("s_zero"))
        o_out, o_normed, tri_done, pt_first, m_first = (
            sem("o_out"), sem("o_normed"), sem("tri_done"), sem("pt_first"), sem("m_first"))
        passed = sem("passed")
        y_done, y_turned, y_kept, y_kept_act, stored = (
            sem("y_done"), sem("y_turned"), sem("y_kept"), sem("y_kept_act"), sem("stored"))

        H_FFN = [KT, KT + KT * len(GROUPS) + KT]
        H_OUT = KT + KT * len(GROUPS)
        H_END = H_FFN[1] + KT * len(GROUPS)
        FFNS = [(ffn1, U_FFN1, 0), (ffn2, U_FFN2, 1)]

        scrap_done = sem("scrap_done")

        def x_cols(n):
            t = n // 2
            return (META + t * P, P) if t < 4 else (0, META)

        def keep_x(eng, n):
            c, w = x_cols(n)
            eng.wait_ge(x_turned, n + 1)
            src = ps[:, n % 8, 0:4 * w].rearrange("p (k n) -> p k n", k=4)
            dst = h[:, 4 * (n % 2):4 * (n % 2) + 4, c:c + w]
            if n % 2 == 1:
                eng.activation(dst, src, ACT.Copy).then_inc(x_kept_act, 1)
            else:
                eng.tensor_copy(dst, src).then_inc(x_kept, 1)

        x_kept_act = sem("x_kept_act")

        def keep_y(eng, parity):
            for n in range(8):
                if n % 2 != parity:
                    continue
                eng.wait_ge(y_turned, n + 1)
                src = ps[:, n % 8, :]
                dst = xin[:, n // 2, 512 * (n % 2):512 * (n % 2) + 512]
                if parity:
                    eng.activation(dst, src, ACT.Copy).then_inc(y_kept_act, 1)
                else:
                    eng.tensor_copy(dst, src).then_inc(y_kept, 1)

        def swap_r(sp, swap, r):
            n = r - 8
            sp.wait_ge(pj_kept, 5 + r + 1)
            if n < 4:
                sp.wait_ge(rope_done, 5)
            else:
                sp.wait_ge(q_roped, n - 3)
            swap(5 + n, pjb[:, n, :], sw[:, n % 4, :])

        V_BANKS = {M_GV: [4, 5, 6, 7, 0], M_DV: [0, 1, 2, 3, 4]}
        INDEX = [(b, hd) for b in range(1, len(BLK)) for hd in range(HEADS)]
        RC = [(RC_WIN[w], s, n) for w, (s, n) in enumerate(WIN)] + [(RC_BLK[b], s, n) for b, (s, n) in enumerate(BLK)]
        NLV = len(LEVELS) + 1

        def lv_views(g):
            return 1 if TOK % (2 * LEVELS[g - 1]) == 0 else 2

        def views_before(g):
            return sum(lv_views(k) for k in range(1, g))

        def lv_ap(ap, g, v):
            s = LEVELS[g - 1]
            if lv_views(g) == 1:
                flat = ap.rearrange("p t n -> p (t n)")
            else:
                flat = ap[:, v, 0:FULL_WIN * P]
            return flat.rearrange("p (m a b) -> p m a b", a=2, b=s)

        def lv_wins(g):
            return len(WIN) if g == 0 or LEVELS[g - 1] < WIN[-1][1] else FULL_WIN

        STEPS = [(g, w) for g in range(NLV) for w in range(lv_wins(g))]

        def steps_before(g):
            return sum(lv_wins(k) for k in range(g))

        xbuf = [xa, xb]
        kdt = t0[:, 0:2 * P].rearrange("p (t n) -> p t n", t=2)

        def pe_mixer(pe, product):
            for m in range(6):
                if m == 3:
                    pe.wait_ge(var_done, 2)
                if m >= 4:
                    pe.wait_ge(pj_kept, m - 3)
                rows = N_IKW if m == M_IKW else N_GA if m == M_GA else P
                product(U_MIX + m, 2 * (m % 4), rows, xh, xl, KT,
                        before_k=(lambda k: pe.wait_ge(x_lo, KT + k + 1)) if m == 0 else None)

            def v_unit(m0, q, blocks):
                u = U_MIX + m0 + q
                slot = u % RING
                pe.wait_ge(w_split, u + RING + 1)
                for b, (s, n) in enumerate(blocks):
                    for k in range(2):
                        for c, (xx, ww) in enumerate(((xh, wh), (xl, wh), (xh, wl))):
                            mm = pe.matmul(ps[0:n, V_BANKS[m0][b], :], xx[:, 2 * q + k, s:s + n],
                                           ww[:, slot, k * 512:(k + 1) * 512], start=(q == 0 and k == 0 and c == 0),
                                           stop=(q == 3 and k == 1 and c == 2))
                mm.then_inc(w_used, 1)

            pe.wait_ge(pj_kept, 5)
            pe.wait_ge(iw_scaled, 1)
            v_unit(M_GV, 0, WIN)
            pe.wait_ge(ga_scaled, 1)
            pe.wait_ge(rstd_done, 2)
            for c, s, n in RC:
                pe.matmul(ps[0:n, 3, c:c + 1], rstd[0:1, s:s + n], ones[0:1, 0:1], start=True, stop=True)
            for b in range(1, len(BLK)):
                s, n = BLK[b]
                mm = pe.transpose(ps[0:n, 1, 8 * b:8 * b + 8], ga[64:64 + HEADS, s:s + n],
                                  ident[64:64 + HEADS, 64:64 + HEADS])
            mm.then_inc(tok_turned, 1)
            for q in range(1, 4):
                v_unit(M_GV, q, WIN)

            pe.wait_ge(rope_done, 5)
            pe.wait_ge(ik_copied, 16)
            for n, (b, hd) in enumerate(INDEX):
                q = (n + 1) % 4
                if n == 0:
                    pe.wait_ge(tok_kept, 4)
                elif n < 4:
                    pe.wait_ge(v_kept, [2, 4, 5][n - 1])
                else:
                    pe.wait_ge(relu_done, n - 3)
                s, w = BLK[b]
                e = 64 * (hd % 2)
                for a, (k0, kn) in enumerate(key_parts(b)):
                    mm = pe.matmul(ps[0:w, 2 * q + a, 0:kn], iq[e:e + HD, hd // 2, s:s + w],
                                   ik[e:e + HD, k0:k0 + kn], start=True, stop=True)
                mm.then_inc(idx_done, 1)
            for t in range(2):
                q = 1 + t
                pe.wait_ge(relu_done, 29 + t)
                for a in range(2):
                    mm = pe.matmul(ps[:, 2 * q + a, 0:HALF], wa2[:, t, :], ga[0:N_GA, a * HALF:(a + 1) * HALF],
                                   start=True, stop=True)
                mm.then_inc(z_done, 1)
            with pe.Fori(0, 4) as i:
                for j in range(4):
                    if j in (1, 2):
                        pe.wait_ge(gate_y, j)
                    else:
                        pe.wait_ge(relu_done, 32)
                    pe.wait_ge(pj_kept, at(i, 4, j + 2))
                    product(U_MIX + M_RAW + j, 2 * j, P, xh, xl, KT, i)
            pe.wait_ge(pj_kept, 5 + 15)
            for q in range(4):
                v_unit(M_DV, q, BLK)

            pe.wait_ge(pj_kept, 5 + 16)
            pe.wait_ge(gqk_scaled, 4)
            for n, (g, w) in enumerate(STEPS):
                if w == 0 and g:
                    pe.wait_ge(lv_x, 2 * (views_before(g) + lv_views(g)))
                if n == 1:
                    pe.wait_ge(v_kept, 10)
                if n >= 4:
                    pe.wait_ge(at_done, n - 3)
                s, width = WIN[w]
                for hd in range(GLA_HEADS):
                    t, e = hd // 2, 64 * (hd % 2)
                    if g == 0:
                        kk, qq = pja[e:e + DK, 2 + t, s:s + width], pja[e:e + DK, t, s:s + width]
                    else:
                        kk = qq = xbuf[g % 2][e:e + DK, t, s:s + width]
                    mm = pe.matmul(ps[0:width, 2 * ((n + 3) % 4) + hd % 2, t * width:(t + 1) * width], kk, qq,
                                   start=True, stop=True)
                mm.then_inc(lv_mm, 1)
            for w, (s, width) in enumerate(WIN):
                last = w == len(WIN) - 1
                if not last:
                    if w == 0:
                        pe.wait_ge(kd_ready, 2)
                        pe.wait_ge(v_kept, 10)
                    if w:
                        pe.wait_ge(kd_kept, w)
                    for t in range(2):
                        mm = pe.transpose(ps[0:width, 2, t * P:(t + 1) * P], xb[:, t, s:s + width], ident[:, :])
                    mm.then_inc(kd_turned, 1)
                pe.wait_ge(at_done, len(STEPS))
                pe.wait_ge(qe_ready, 1)
                if w >= 2:
                    pe.wait_ge(o_kept, w - 1)
                if w:
                    pe.wait_ge(s_new, GLA_HEADS * w)
                for hd in range(GLA_HEADS):
                    t, e = hd // 2, 64 * (hd % 2)
                    o = ps[:, w % 2, hd * width:(hd + 1) * width]
                    mm = pe.matmul(o, gv[0:width, w, hd * DV:(hd + 1) * DV], at_win(w)[:, hd % 2, t, :], start=True,
                                   stop=(w == 0))
                    if w:
                        mm = pe.matmul(o, S[:, hd, :], xa[:, t, s:s + width], start=False, stop=True)
                mm.then_inc(o_mm, 1)
                if not last:
                    pe.wait_ge(kd_kept, w + 1)
                    for hd in range(GLA_HEADS):
                        t, e = hd // 2, 64 * (hd % 2)
                        mm = pe.matmul(ps[e:e + DK, 3, t * DV:(t + 1) * DV], kdt[0:width, t, e:e + DK],
                                       gv[0:width, w, hd * DV:(hd + 1) * DV], start=True, stop=True)
                    mm.then_inc(s_mm, 1)
            for hd in range(GLA_HEADS):
                pe.wait_ge(o_sq, hd + 1)
                if hd == 0:
                    pe.wait_ge(o_kept, len(WIN))
                if hd == 1:
                    pe.wait_ge(s_new, GLA_HEADS * FULL_WIN)
                for a in range(2):
                    mm = pe.matmul(ps[:, 2 * hd + a, 0:HALF], ones[:, :], o_square(hd)[:, a * HALF:(a + 1) * HALF],
                                   start=True, stop=True)
                mm.then_inc(o_sum, 1)

            pe.wait_ge(o_var, GLA_HEADS)
            with pe.Fori(0, HEADS // 2) as i:
                pe.wait_ge(staged, at(i, 2, 2))

                def logits(n):
                    e, b = divmod(n, 5)
                    s, w = BLK[b]
                    pe.wait_ge(lg_done, at(i, 10, n + 1))
                    for a, (k0, kn) in enumerate(key_parts(b)):
                        mm = pe.matmul(ps[0:w, 2 * (n % 2) + a, 0:kn], qst[64 * e:64 * e + HD, s:s + w],
                                       kst[64 * e:64 * e + HD, k0:k0 + kn], start=True, stop=True)
                    mm.then_inc(qk_done, 1)

                logits(0)
                logits(1)
                for n in range(10):
                    e, b = divmod(n, 5)
                    w = BLK[b][1]
                    pe.wait_ge(exp_done, ONE + at(i, 10, n + 1))
                    pe.wait_ge(pt_kept, at(i, 10, n + 1))
                    for c in range(b + 1):
                        s, wc = BLK[c]
                        mm = pe.transpose(ps[0:wc, 4 + n % 2, c * w:(c + 1) * w], pr[0:w, n % 2, s:s + wc],
                                          ident[0:w, 0:w])
                    mm.then_inc(pt_done, 1)
                    if n + 2 < 10:
                        logits(n + 2)
                    pe.wait_ge(pt_kept, at(i, 10, n + 3))
                    pe.wait_ge(pv_kept, at(i, 10, n + 1))
                    pe.wait_ge(m_lo, at(i, 1, GLA_HEADS))
                    for c in range(b + 1):
                        wc = BLK[c][1]
                        mm = pe.matmul(ps[0:w, 6 + n % 2, 0:HD], pt[0:wc, n % 2, c * w:(c + 1) * w],
                                       dv[0:wc, c, bass.ds(i * P + HD * e, HD)], start=(c == 0), stop=(c == b))
                    mm.then_inc(pv_done, 1)
                pe.wait_ge(pv_kept, at(i, 10, 12))
                for b, (s, w) in enumerate(BLK):
                    bank, c = (6, s) if s + w <= 512 else (7, 0)
                    mm = pe.transpose(ps[:, bank, c:c + w], otok[0:w, b, :], ident[0:w, 0:w])
                mm.then_inc(ot_turned, 1)

            pe.wait_ge(m_lo, KT)
            with pe.Fori(0, KT // 4) as i:
                for j in range(4):
                    pe.wait_ge(h_done, at(i, 4, H_OUT + j - 3))
                    product(U_OUT + j, 2 * j, P, ah, al, KT, i)

        def key_parts(b):
            n = SEEN[b]
            return [(0, n)] if n <= 512 else [(0, HALF), (HALF, n - HALF)]

        def key_view(ap, b):
            return ap if SEEN[b] <= 512 else halves(ap)

        def key_psum(b, w, bank):
            return ps[0:w, bank, 0:SEEN[b]] if SEEN[b] <= 512 else ps[0:w, bank:bank + 2, 0:HALF]

        def o_square(hd):
            return xbuf[hd // 2][:, hd % 2, :]

        def act_mixer(act, hi, prep_hi):
            def keep(bank, dst, rows, u, i=None):
                act.wait_ge(w_used, at(i, 4, u + RING + 1))
                act.activation(halves(dst), ps[0:rows, bank:bank + 2, 0:HALF], ACT.Copy).then_inc(pj_kept, 1)

            def keep_v(dst, m0, blocks, cols):
                act.wait_ge(w_used, U_MIX + m0 + 3 + RING + 1)
                act.wait_ge(tok_kept, 4)
                for b, (s, n) in enumerate(blocks):
                    act.activation(dst[0:n, b, :], ps[0:n, V_BANKS[m0][b], :], ACT.Copy,
                                   scale=rcol[0:n, cols[b]:cols[b] + 1]).then_inc(v_kept, 1)

            for m in range(6):
                hi(U_MIX + m + 2)
                if m < 4:
                    keep(2 * m, iq[:, m, :], P, U_MIX + m)
                elif m == 4:
                    keep(0, ik[0:HD, :], HD, U_MIX + m)
            for q in range(4):
                hi(U_MIX + M_GV + q + 2)
            keep_v(gv, M_GV, WIN, RC_WIN)
            for n, (b, hd) in enumerate(INDEX):
                w = BLK[b][1]
                act.wait_ge(idx_done, n + 1)
                if n >= 2:
                    act.wait_ge(acc_done, n - 1)
                act.activation(key_view(gb[0:w, n % 2, 0:SEEN[b]], b), key_psum(b, w, 2 * ((n + 1) % 4)),
                               ACT.Relu).then_inc(relu_done, 1)
            act.wait_ge(gate_y, 2)
            act.activation(gb[:, :, :], xa[:, :, :], ACT.Abs).then_inc(gate_abs, 1)
            act.wait_ge(gate_abs, 1)
            act.activation(gb[:, :, :], gb[:, :, :], ACT.Exp, scale=-1.0).then_inc(gate_exp, 1)
            act.wait_ge(gate_exp, 1)
            act.activation(gb[:, :, :], gb[:, :, :], ACT.Ln, bias=1.0).then_inc(gate_ln, 1)
            u = U_MIX + M_RAW
            for half, dst in enumerate((pja, pjb)):
                with act.Fori(0, 2) as i:
                    for j in range(4):
                        hi(u + 8 * half + j + 2, i)
                        keep(2 * j, dst[:, i * 4 + j, :], P, u + 8 * half + j, i)
            for q in range(4):
                hi(U_MIX + M_DV + q + 2)
            keep_v(dv, M_DV, BLK, RC_BLK)
            for g in range(1, NLV):
                for v in range(lv_views(g)):
                    n = views_before(g) + v
                    act.wait_ge(lv_diff, 2 * (n + 1))
                    ap = lv_ap(xbuf[g % 2][:, :, :], g, v)
                    act.activation(ap, ap, ACT.Exp, scale=1.0 / GATE_NORM).then_inc(lv_exp, 1)
            act.wait_ge(lv_mm, steps_before(NLV - 1))
            act.activation(xa[:, :, :], gb[:, :, :], ACT.Exp, scale=1.0 / GATE_NORM).then_inc(qe_exp, 1)
            act.activation(elast.rearrange("p (t w) -> p t w", t=2)[:, :, 0:FULL_WIN],
                           gb[:, :, P - 1:FULL_WIN * P:P], ACT.Exp, scale=1.0 / GATE_NORM).then_inc(el_exp, 1)
            act.wait_ge(kd_diff, 2)
            act.activation(xb[:, :, 0:FULL_WIN * P], xb[:, :, 0:FULL_WIN * P], ACT.Exp,
                           scale=1.0 / GATE_NORM).then_inc(kd_exp, 1)
            act.wait_ge(gr_scaled, GLA_HEADS)
            act.activation(pja[:, 4:8, :], pja[:, 4:8, :], ACT.Silu).then_inc(gr_silu, 1)
            act.wait_ge(o_kept, len(WIN))
            for hd in range(GLA_HEADS):
                act.activation(o_square(hd), oT[:, hd, :], ACT.Square).then_inc(o_sq, 1)
            for hd in range(GLA_HEADS):
                act.wait_ge(o_inv, hd + 1)
                act.activation(o_square(hd), o_square(hd), ACT.Sqrt).then_inc(o_rstd, 1)
            for hd in range(GLA_HEADS):
                act.wait_ge(o_out, hd + 1)
                act.activation(ah[:, hd, :], oT[:, hd, :], ACT.Copy).then_inc(m_hi, 1)
            act.activation(scrap[:, :], scrap[:, :], ACT.Exp).then_inc(scrap_done, 1)
            with act.Fori(0, HEADS // 2) as i:
                act.wait_ge(qk_done, ONE + at(i, 10, 0))
                act.activation(qst[:, :], pjb[:, i, :], ACT.Copy).then_inc(staged, 1)
                act.activation(kst[:, :], pjb[:, i + 4, :], ACT.Copy).then_inc(staged, 1)

                def keep_pv(n):
                    e, b = divmod(n, 5)
                    w = BLK[b][1]
                    act.wait_ge(pv_done, ONE + at(i, 10, n + 1))
                    act.wait_ge(sum_inv, at(i, 10, n + 1))
                    act.activation(otok[0:w, b, 64 * e:64 * e + HD], ps[0:w, 6 + n % 2, 0:HD], ACT.Copy,
                                   scale=stat[0:w, 8 + n % 2:9 + n % 2]).then_inc(pv_kept, 1)

                for n in range(10):
                    e, b = divmod(n, 5)
                    w = BLK[b][1]
                    if n == 0:
                        act.wait_ge(ot_turned, ONE + at(i, 1, 0))
                    act.wait_ge(max_done, at(i, 10, n + 1))
                    if n >= 2:
                        act.wait_ge(pt_done, at(i, 10, n - 1))
                    act.activation(pr[0:w, n % 2, 0:SEEN[b]], lg[0:w, n % 2, 0:SEEN[b]], ACT.Exp, scale=HD ** -0.5,
                                   bias=stat[0:w, 4 + n % 2:5 + n % 2],
                                   accum_out=stat[0:w, 6 + n % 2:7 + n % 2]).then_inc(exp_done, 1)
                    if n >= 1:
                        keep_pv(n - 1)
                keep_pv(9)
                act.wait_ge(ot_turned, ONE + at(i, 1, 1))
                act.activation(ah[:, i + 4, 0:428], ps[:, 6, 0:428], ACT.Copy).then_inc(m_hi, 1)
                act.activation(ah[:, i + 4, 428:TOK], ps[:, 7, 0:TOK - 428], ACT.Copy).then_inc(m_hi, 1)
            for d in range(KT):
                hi(U_OUT + d + 2)
                prep_hi(2, d, H_OUT + d)

        def dve_mixer(dve, prep, prep_lo):
            dve.wait_ge(rstd_done, 2)
            dve.wait_ge(mix_loaded, 48)
            dve.tensor_tensor(cosr[:, :], cosr[:, :], rstd[:, :], ALU.mult).then_inc(tables_done, 1)
            dve.tensor_tensor(sinr[:, :], sinr[:, :], rstd[:, :], ALU.mult).then_inc(tables_done, 1)
            dve.wait_ge(tables_done, 2)

            def rope(n, x, s, rows):
                dve.wait_ge(swapped[n], 64 if rows == P else 32)
                dve.tensor_tensor(s[0:rows, :], s[0:rows, :], sinr[0:rows, :], ALU.mult).then_inc(rope_sin, 1)
                dve.tensor_tensor(x[0:rows, :], x[0:rows, :], cosr[0:rows, :], ALU.mult).then_inc(rope_cos, 1)
                dve.wait_ge(rope_sin, n + 1)
                dve.wait_ge(rope_cos, n + 1)
                dve.tensor_tensor(x[0:rows, :], x[0:rows, :], s[0:rows, :], ALU.add).then_inc(rope_done, 1)

            for m in range(4):
                rope(m, iq[:, m, :], sw[:, m, :], P)
            dve.wait_ge(w_used, U_MIX + M_IKW + RING + 1)
            dve.scalar_tensor_tensor(out=halves(ga[64:64 + HEADS, :]), in0=ps[64:64 + HEADS, 0:2, 0:HALF],
                                     scalar=HEADS ** -0.5 * HD ** -0.5, in1=halves(rstd[64:64 + HEADS, :]),
                                     op0=ALU.mult, op1=ALU.mult).then_inc(iw_scaled, 1)
            dve.wait_ge(w_used, U_MIX + M_GA + RING + 1)
            dve.tensor_tensor(halves(ga[0:N_GA, :]), ps[0:N_GA, 2:4, 0:HALF], halves(rstd[0:N_GA, :]),
                              ALU.mult).then_inc(ga_scaled, 1)
            rope(4, ik, sw[:, 0, :], HD)
            dve.wait_ge(tok_turned, 1)
            dve.tensor_copy(rcol[:, 0:5], ps[:, 3, 0:5]).then_inc(tok_kept, 1)
            dve.tensor_copy(rcol[0:100, 5:9], ps[0:100, 3, 5:9]).then_inc(tok_kept, 1)
            dve.tensor_copy(rcol[0:WIN[-1][1], 9:10], ps[0:WIN[-1][1], 3, 9:10]).then_inc(tok_kept, 1)
            dve.tensor_copy(iwt[0:100, :], ps[0:100, 1, 8:40]).then_inc(tok_kept, 1)
            dve.wait_ge(tok_kept, 4)
            dve.wait_ge(consts, 3)
            for n, (b, hd) in enumerate(INDEX):
                w = BLK[b][1]
                sc = mask[0:w, MASK_AT[b]:MASK_AT[b] + SEEN[b]]
                weight = iwt[0:w, 8 * (b - 1) + hd:8 * (b - 1) + hd + 1]
                r = gb[0:w, n % 2, 0:SEEN[b]]
                dve.wait_ge(relu_done, n + 1)
                if hd == 0:
                    dve.tensor_scalar(sc, r, weight, None, ALU.mult).then_inc(acc_done, 1)
                else:
                    dve.wait_ge(acc_done, n)
                    dve.scalar_tensor_tensor(out=sc, in0=r, scalar=weight, in1=sc, op0=ALU.mult,
                                             op1=ALU.add).then_inc(acc_done, 1)
            dve.wait_ge(acc_done, 32)
            for b in range(len(BLK)):
                s, w = BLK[b]
                own = mask[0:w, MASK_AT[b] + s:MASK_AT[b] + s + w]
                if b == 0:
                    dve.tensor_copy(own, tri[0:w, 0:w]).then_inc(mask_done, 1)
                else:
                    dve.tensor_tensor(own, own, tri[0:w, 0:w], ALU.add).then_inc(tri_done, 1)
            for t in range(2):
                dve.wait_ge(z_done, t + 1)
                dve.tensor_scalar(halves(xa[:, t, :]), ps[:, 2 + 2 * t:4 + 2 * t, 0:HALF], ba[:, t:t + 1], None,
                                  ALU.add).then_inc(gate_y, 1)
            dve.wait_ge(tri_done, 4)
            rounds = TOPK // 8
            for b in range(1, len(BLK)):
                w = BLK[b][1]
                sc = mask[0:w, MASK_AT[b]:MASK_AT[b] + SEEN[b]]
                base = (b - 1) * rounds
                with dve.Fori(0, rounds // 4) as i:
                    for j in range(4):
                        dve.wait_ge(top_taken, ONE + at(i, 4, base + j))
                        dve.sem_inc(passed, 1)
                        dve.max(top8[0:w, :], sc).then_inc(top_found, 1)
                        dve.wait_ge(top_found, at(i, 4, base + j + 1))
                        dve.sem_inc(passed, 1)
                        dve.match_replace(sc, top8[0:w, :], sc, TAKEN).then_inc(top_taken, 1)
                dve.wait_ge(top_taken, ONE + base + rounds)
                dve.tensor_scalar(sc, sc, TAKEN * 0.5, NEG, ALU.is_gt, ALU.mult).then_inc(mask_done, 1)

            dve.wait_ge(pj_kept, 5 + 8)
            for t in range(4):
                dve.scalar_tensor_tensor(out=pja[:, t, :], in0=pja[:, t, :], scalar=DK ** -0.5 if t < 2 else 1.0,
                                         in1=rstd[:, :], op0=ALU.mult, op1=ALU.mult).then_inc(gqk_scaled, 1)
            for t in range(4):
                dve.tensor_tensor(pja[:, 4 + t, :], pja[:, 4 + t, :], rstd[:, :], ALU.mult).then_inc(gr_scaled, 1)
            dve.wait_ge(gate_ln, 1)
            dve.scalar_tensor_tensor(out=xa[:, :, :], in0=xa[:, :, :], scalar=0.0, in1=gb[:, :, :], op0=ALU.min,
                                     op1=ALU.subtract).then_inc(gate_g, 1)
            dve.wait_ge(gate_g, 1)
            for t in range(2):
                for s, w in WIN:
                    dve.tensor_tensor_scan(gb[:, t, s:s + w], ones[:, 0:w], xa[:, t, s:s + w], 0.0, ALU.mult,
                                           ALU.add).then_inc(gate_cum, 1)
            dve.wait_ge(gate_cum, 2 * len(WIN))
            dve.wait_ge(gqk_scaled, 4)

            def level_diff(g):
                if g >= 3:
                    dve.wait_ge(lv_mm, steps_before(g - 1))
                for v in range(lv_views(g)):
                    b4, x4 = lv_ap(gb[:, :, :], g, v), lv_ap(xbuf[g % 2][:, :, :], g, v)
                    s = LEVELS[g - 1]
                    ref = b4[:, :, 0, s - 1:s].broadcast_to([P, b4.shape[1], s])
                    dve.tensor_tensor(x4[:, :, 0, :], ref, b4[:, :, 0, :], ALU.subtract).then_inc(lv_diff, 1)
                    dve.tensor_tensor(x4[:, :, 1, :], b4[:, :, 1, :], ref, ALU.subtract).then_inc(lv_diff, 1)

            def level_x(g):
                for v in range(lv_views(g)):
                    n = views_before(g) + v
                    dve.wait_ge(lv_exp, n + 1)
                    x4 = lv_ap(xbuf[g % 2][:, :, :], g, v)
                    k4, q4 = lv_ap(pja[:, 2:4, :], g, v), lv_ap(pja[:, 0:2, :], g, v)
                    dve.tensor_tensor(x4[:, :, 0, :], x4[:, :, 0, :], k4[:, :, 0, :], ALU.mult).then_inc(lv_x, 1)
                    dve.tensor_tensor(x4[:, :, 1, :], x4[:, :, 1, :], q4[:, :, 1, :], ALU.mult).then_inc(lv_x, 1)

            def level_take(g):
                for w in range(lv_wins(g)):
                    n = steps_before(g) + w
                    width = WIN[w][1]
                    dve.wait_ge(lv_mm, n + 1)
                    bank = 2 * ((n + 3) % 4)
                    src = ps[0:width, bank:bank + 2, 0:2 * width].rearrange("p e (t n) -> p e t n", t=2)
                    sel = (ident[0:width, 0:width] if g == 0 else lvm[0:width, g - 1, 0:width])
                    sel = sel.unsqueeze(1).unsqueeze(1).broadcast_to([width, 2, 2, width])
                    if g == 0:
                        dve.tensor_tensor(at_win(w), src, sel, ALU.mult).then_inc(at_done, 1)
                    else:
                        dve.wait_ge(at_done, n)
                        dve.copy_predicated(at_win(w), sel, src).then_inc(at_done, 1)

            dve.wait_ge(lv_step, 5 * len(LEVELS))
            level_diff(1)
            for g in range(1, NLV):
                level_x(g)
                level_take(g - 1)
                if g + 1 < NLV:
                    level_diff(g + 1)
            level_take(NLV - 1)
            for t in range(2):
                b3 = gb[:, t, 0:FULL_WIN * P].rearrange("p (w n) -> p w n", n=P)
                x3 = xb[:, t, 0:FULL_WIN * P].rearrange("p (w n) -> p w n", n=P)
                dve.tensor_tensor(x3, b3[:, :, P - 1:P].broadcast_to([P, FULL_WIN, P]), b3,
                                  ALU.subtract).then_inc(kd_diff, 1)
            dve.wait_ge(qe_exp, 1)
            dve.tensor_tensor(xa[:, :, :], xa[:, :, :], pja[:, 0:2, :], ALU.mult).then_inc(qe_ready, 1)
            dve.wait_ge(kd_exp, 1)
            for t in range(2):
                dve.tensor_tensor(xb[:, t, 0:FULL_WIN * P], xb[:, t, 0:FULL_WIN * P], pja[:, 2 + t, 0:FULL_WIN * P],
                                  ALU.mult).then_inc(kd_ready, 1)
            dve.memset(S[:, :, :], 0.0).then_inc(s_zero, 1)
            dve.wait_ge(s_zero, 1)
            for w, (s, width) in enumerate(WIN):
                last = w == len(WIN) - 1
                if not last:
                    dve.wait_ge(kd_turned, w + 1)
                    if w:
                        dve.wait_ge(s_mm, w)
                    dve.tensor_copy(kdt, ps[:, 2, 0:2 * P].rearrange("p (t n) -> p t n", t=2)).then_inc(kd_kept, 1)
                if w:
                    dve.wait_ge(s_mm, w)
                if not last:
                    dve.wait_ge(s_mm, w + 1)
                    if w == 1:
                        dve.wait_ge(el_exp, 1)
                    if w:
                        dve.wait_ge(s_new, GLA_HEADS * w)
                    for hd in range(GLA_HEADS):
                        t, e = hd // 2, 64 * (hd % 2)
                        new, old = ps[e:e + DK, 3, t * DV:(t + 1) * DV], S[e:e + DK, hd, :]
                        if w == 0:
                            dve.tensor_copy(old, new).then_inc(s_new, 1)
                        else:
                            dve.scalar_tensor_tensor(out=old, in0=old,
                                                     scalar=elast[e:e + DK, 5 * t + w:5 * t + w + 1], in1=new,
                                                     op0=ALU.mult, op1=ALU.add).then_inc(s_new, 1)
                dve.wait_ge(o_mm, w + 1)
                dve.tensor_copy(oT[:, :, s:s + width], ps[:, w % 2, 0:GLA_HEADS * width].rearrange(
                    "p (g n) -> p g n", g=GLA_HEADS)).then_inc(o_kept, 1)
            for hd in range(GLA_HEADS):
                dve.wait_ge(o_sum, hd + 1)
                dve.tensor_scalar(halves(o_square(hd)), ps[:, 2 * hd:2 * hd + 2, 0:HALF], 1.0 / DV, EPS, ALU.mult,
                                  ALU.add).then_inc(o_var, 1)
                dve.wait_ge(o_var, hd + 1)
                dve.reciprocal(o_square(hd), o_square(hd)).then_inc(o_inv, 1)
            dve.wait_ge(gr_silu, 1)
            for hd in range(GLA_HEADS):
                dve.wait_ge(o_rstd, hd + 1)
                dve.wait_ge(o_kept, len(WIN))
                dve.scalar_tensor_tensor(out=oT[:, hd, :], in0=oT[:, hd, :], scalar=hn, in1=o_square(hd),
                                         op0=ALU.mult, op1=ALU.mult).then_inc(o_normed, 1)
                dve.wait_ge(o_normed, hd + 1)
                dve.tensor_tensor(oT[:, hd, :], oT[:, hd, :], pja[:, 4 + hd, :], ALU.mult).then_inc(o_out, 1)
            for hd in range(GLA_HEADS):
                dve.wait_ge(m_hi, hd + 1)
                dve.tensor_tensor(al[:, hd, :], oT[:, hd, :], ah[:, hd, :].bitcast(F32),
                                  ALU.subtract).then_inc(m_lo, 1)
            dve.wait_ge(mask_done, 5)
            with dve.Fori(0, HEADS // 2) as i:
                def masked(n):
                    b = n % 5
                    w = BLK[b][1]
                    dve.wait_ge(qk_done, ONE + at(i, 10, n + 1))
                    dve.wait_ge(exp_done, ONE + at(i, 10, max(n - 1, 0)))
                    dve.sem_inc(passed, 1)
                    dve.tensor_tensor_reduce(out=key_view(lg[0:w, n % 2, 0:SEEN[b]], b), in0=key_psum(b, w, 2 * (n % 2)),
                                             in1=key_view(mask[0:w, MASK_AT[b]:MASK_AT[b] + SEEN[b]], b), scale=1.0,
                                             scalar=-3.0e38, op0=ALU.add, op1=ALU.max,
                                             accum_out=stat[0:w, 2 + n % 2:3 + n % 2]).then_inc(lg_done, 1)
                    dve.wait_ge(lg_done, at(i, 10, n + 3))
                    dve.tensor_scalar(stat[0:w, 4 + n % 2:5 + n % 2], stat[0:w, 2 + n % 2:3 + n % 2], -HD ** -0.5, None,
                                      ALU.mult).then_inc(max_done, 1)

                def keep_pt(n):
                    b = n % 5
                    w = BLK[b][1]
                    dve.wait_ge(exp_done, ONE + at(i, 10, n + 1))
                    dve.wait_ge(pv_kept, at(i, 10, n + 1))
                    dve.reciprocal(stat[0:w, 8 + n % 2:9 + n % 2], stat[0:w, 6 + n % 2:7 + n % 2]).then_inc(sum_inv, 1)
                    dve.wait_ge(pt_done, at(i, 10, n + 1))
                    dve.wait_ge(pv_done, ONE + at(i, 10, max(n - 1, 0)))
                    if b == 0:
                        dve.tensor_copy(pt[:, n % 2, 0:w], ps[:, 4 + n % 2, 0:w]).then_inc(pt_kept, 1)
                    else:
                        dve.tensor_copy(pt[:, n % 2, 0:w], ps[:, 4 + n % 2, 0:w]).then_inc(pt_first, 1)
                        dve.tensor_copy(pt[0:100, n % 2, w:(b + 1) * w],
                                        ps[0:100, 4 + n % 2, w:(b + 1) * w]).then_inc(pt_kept, 1)

                masked(0)
                masked(1)
                for n in range(10):
                    keep_pt(n)
                    if n + 2 < 10:
                        masked(n + 2)
                dve.wait_ge(m_hi, at(i, 2, GLA_HEADS + 2))
                dve.tensor_tensor(al[:, i + 4, 0:428], ps[:, 6, 0:428], ah[:, i + 4, 0:428].bitcast(F32),
                                  ALU.subtract).then_inc(m_first, 1)
                dve.tensor_tensor(al[:, i + 4, 428:TOK], ps[:, 7, 0:TOK - 428], ah[:, i + 4, 428:TOK].bitcast(F32),
                                  ALU.subtract).then_inc(m_lo, 1)
            for d in range(KT):
                bank = 2 * (d % 4)
                dve.wait_ge(w_used, U_OUT + d + RING + 1)
                dve.wait_ge(h_done, H_OUT - KT + d + 1)
                dve.tensor_tensor(halves(h[:, d, :]), ps[:, bank:bank + 2, 0:HALF], halves(h[:, d, :]),
                                  ALU.add).then_inc(h_done, 1)
                prep(2, d, H_OUT + d)
                prep_lo(2, d)

        block = ctx.enter_context(nc.Block())

        @block.sync
        def _(sp):
            def load(u, src, dst_view, i=None):
                slot = u % RING
                sp.wait_ge(w_split, at(i, RING, u + 1))
                sp.dma_start(dst_view(raw[:, slot, :]), src).then_inc(w_in_slot[slot], 16)

            def cols(n=P):
                return lambda s: s.rearrange("p (k n) -> p k n", k=KT)[:, :, 0:n]

            sp.dma_start(xin[:, 0:4, :], x.rearrange("(t p) d -> p t d", p=P)).then_inc(x_loaded, 16)
            sp.dma_start(xin[0:META, 4, :], meta).then_inc(x_loaded, 16)
            for n, g in enumerate([ffn1[0], mix_norm, ffn2[0], final_norm]):
                sp.dma_start(vec_rows[KT * n:KT * (n + 1), :], g.rearrange("(k p) -> k p", p=P)).then_inc(const_loaded, 16)
            sp.dma_start(vec_rows[4 * KT:4 * KT + 2, :], b_a.rearrange("(k p) -> k p", p=P)).then_inc(const_loaded, 16)
            sp.dma_start(vec_rows[4 * KT + 2:4 * KT + 3, :], head_norm.rearrange("(k p) -> k p", p=P)).then_inc(const_loaded, 16)

            def ffn_loads(weights, u0):
                _, w_gate, w_up, w_down = weights
                gate_v = w_gate.rearrange("(k p) f -> p k f", p=P)
                up_v = w_up.rearrange("(k p) f -> p k f", p=P)
                down_v = w_down.rearrange("(k p) d -> p k d", p=P)
                u = u0
                for f0, cnt in GROUPS:
                    with sp.Fori(0, cnt // 2) as i:
                        for j in range(2):
                            c = (i * 2 + (f0 + j)) * P
                            load(u + 2 * j, gate_v[:, :, bass.ds(c, P)], cols(), i)
                            load(u + 2 * j + 1, up_v[:, :, bass.ds(c, P)], cols(), i)
                    u += 2 * cnt
                    with sp.Fori(0, KT // RING) as i:
                        for j in range(RING):
                            c = (i * RING + j) * P
                            load(u + j, down_v[:, f0:f0 + cnt, bass.ds(c, P)],
                                 lambda s: s.rearrange("p (k n) -> p k n", k=KT)[:, 0:cnt, :], i)
                    u += KT

            ffn_loads(ffn1, U_FFN1)
            if stop_after != "ffn1":
                win_v = w_in.rearrange("(k p) n -> p k n", p=P)

                def load_mix(m):
                    u = U_MIX + m
                    if m < M_IKW:
                        load(u, win_v[:, :, C_IQ + m * P:C_IQ + (m + 1) * P], cols())
                    elif m == M_IKW:
                        load(u, win_v[:, :, C_IK:C_IK + N_IKW], cols(N_IKW))
                    elif m == M_GA:
                        load(u, win_v[:, :, C_GA:C_GA + N_GA], cols(N_GA))
                    elif M_RAW <= m < M_DV:
                        r = m - M_RAW
                        c = C_GQK + r * P if r < 4 else C_GR + (r - 4) * P if r < 8 else C_DQK + (r - 8) * P
                        load(u, win_v[:, :, c:c + P], cols())
                    else:
                        c, q = (C_GV, m - M_GV) if m < M_RAW else (C_DV, m - M_DV)
                        load(u, win_v[:, 2 * q:2 * q + 2, c:c + 512], lambda s: s.rearrange("p (k n) -> p k n", k=2))

                def swap(n, tile, dst, rows=P):
                    for a in range(0, rows, 32):
                        b = a ^ 32
                        sp.dma_start(dst[a:a + 32, :], tile[b:b + 32, :]).then_inc(swapped[n], 16)

                for m in range(4):
                    load_mix(m)
                sp.wait_ge(h_done, H_OUT)
                for dst, src in ((cosr, cos_t), (sinr, sin_t)):
                    sp.dma_start(dst[:, :], src).then_inc(mix_loaded, 16)
                sp.dma_start(wa2[:, :, :], w_a2.rearrange("k (t n) -> k t n", n=P)).then_inc(mix_loaded, 16)
                load_mix(4)
                load_mix(5)
                for m in range(5):
                    sp.wait_ge(pj_kept, m + 1)
                    if m < 4:
                        swap(m, iq[:, m, :], sw[:, m, :])
                    else:
                        sp.wait_ge(rope_done, 1)
                        swap(m, ik[:, :], sw[:, 0, :], HD)
                    load_mix(6 + m)
                sp.wait_ge(rope_done, 5)
                sp.dma_start(ik[HD:2 * HD, :], ik[0:HD, :]).then_inc(ik_copied, 16)
                for m in range(11, MIX_UNITS):
                    load_mix(m)
                    r = m - M_RAW - 5
                    if 8 <= r < 16:
                        swap_r(sp, swap, r)
                for r in range(MIX_UNITS - M_RAW - 5, 16):
                    swap_r(sp, swap, r)
                out_v = w_out.rearrange("(k p) d -> p k d", p=P)
                with sp.Fori(0, KT // RING) as i:
                    for j in range(RING):
                        load(U_OUT + j, out_v[:, :, bass.ds((i * RING + j) * P, P)], cols(), i)
                ffn_loads(ffn2, U_FFN2)
            for t in range(SEQ // P):
                sp.wait_ge(y_kept, t + 1)
                sp.wait_ge(y_kept_act, t + 1)
                sp.dma_start(out[t * P:(t + 1) * P, :], xin[:, t, :]).then_inc(stored, 16)
            sp.wait_ge(stored, 16 * (SEQ // P))

        @block.gpsimd
        def _(pool):
            pool.sem_inc(w_split, RING)
            pool.memset(ident[:, :], 0.0).then_inc(c_zero, 1)
            pool.memset(ones[:, :], 1.0).then_inc(consts, 1)
            pool.wait_ge(c_zero, 1)
            pool.affine_select(out=ident[:, :], in_=ident[:, :], compare_op=ALU.not_equal, fill=1.0, base=0,
                               pattern=[[-1, P]], channel_multiplier=1).then_inc(consts, 1)

            def lo(u, i=None):
                slot = u % RING
                pool.wait_ge(w_hi, at(i, RING, u + 1))
                pool.tensor_tensor(wl[:, slot, :], raw[:, slot, :], wh[:, slot, :].bitcast(F32),
                                   ALU.subtract).then_inc(w_split, 1)

            def run(u0, n):
                if n >= RING:
                    with pool.Fori(0, n // RING) as i:
                        for j in range(RING):
                            lo(u0 + j, i)
                for j in range(n - n % RING, n):
                    lo(u0 + j)

            run(0, U_MIX)
            if stop_after != "ffn1":
                run(U_MIX, 6)
                pool.wait_ge(h_done, H_OUT)
                pool.memset(tri[:, :], 0.0).then_inc(c_zero, 1)
                pool.wait_ge(c_zero, 2)
                pool.affine_select(out=tri[:, :], in_=tri[:, :], compare_op=ALU.is_ge, fill=NEG, base=0,
                                   pattern=[[-1, P]], channel_multiplier=1).then_inc(consts, 1)
                run(U_MIX + 6, M_RAW - 6)
                steps = 0
                for n, s in enumerate(LEVELS):
                    scratch = xb[:, 0, 0:P]
                    blk = scratch.rearrange("p (m a b) -> p m a b", a=2, b=s)
                    if n:
                        pool.wait_ge(lv_step, steps)
                    pool.memset(scratch, 0.0).then_inc(lv_step, 1)
                    steps += 1
                    pool.wait_ge(lv_step, steps)
                    pool.memset(blk[:, :, 1, :], 1.0).then_inc(lv_step, 1)
                    steps += 1
                    pool.wait_ge(lv_step, steps)
                    pool.affine_select(out=blk[:, :, 1, :], in_=blk[:, :, 1, :], compare_op=ALU.is_ge, fill=0.0,
                                       base=0, pattern=[[-2 * s, P // (2 * s)], [0, s]],
                                       channel_multiplier=1).then_inc(lv_step, 1)
                    steps += 1
                    pool.wait_ge(lv_step, steps)
                    pool.affine_select(out=blk[:, :, 1, :], in_=blk[:, :, 1, :], compare_op=ALU.is_ge, fill=0.0,
                                       base=s - 1, pattern=[[2 * s, P // (2 * s)], [0, s]],
                                       channel_multiplier=-1).then_inc(lv_step, 1)
                    steps += 1
                    pool.wait_ge(lv_step, steps)
                    pool.tensor_copy(lvm[:, n, :], scratch).then_inc(lv_step, 1)
                    steps += 1
                run(U_MIX + M_RAW, M_DV - M_RAW)
                for q in range(4):
                    lo(U_MIX + M_DV + q)
                    if q == 1:
                        for n in range(8):
                            pool.wait_ge(swapped[5 + n], 64)
                            s = sw[:, n % 4, :]
                            pool.tensor_tensor(s, s, sinr[:, :], ALU.mult).then_inc(q_sin, 1)
                            pool.tensor_tensor(pjb[:, n, :], pjb[:, n, :], cosr[:, :], ALU.mult).then_inc(q_cos, 1)
                            pool.wait_ge(q_sin, n + 1)
                            pool.wait_ge(q_cos, n + 1)
                            pool.tensor_tensor(pjb[:, n, :], pjb[:, n, :], s, ALU.add).then_inc(q_roped, 1)
                run(U_OUT, U_END - U_OUT)

        @block.scalar
        def _(act):
            def hi(u, i=None):
                slot = u % RING
                if i is None and u >= last_unit:
                    return
                act.wait_ge(w_in_slot[slot], at(i, 16, 16 * (u // RING + 1)))
                act.wait_ge(w_used, at(i, RING, u + 1))
                act.activation(wh[:, slot, :], raw[:, slot, :], ACT.Copy).then_inc(w_hi, 1)

            act.sem_inc(pv_kept, 2)
            act.sem_inc(exp_done, ONE)
            last_unit = U_MIX if stop_after == "ffn1" else U_END

            def prep_hi(norm, d, h_count):
                act.wait_ge(h_done, h_count + 1)
                act.activation(xh[:, d, :], h[:, d, :], ACT.Copy, scale=gains[:, norm, d:d + 1]).then_inc(x_hi, 1)

            def root(norm):
                act.wait_ge(inv_done, norm + 1)
                act.activation(rstd[:, :], rstd[:, :], ACT.Sqrt).then_inc(rstd_done, 1)

            def ffn(u0, number, norm):
                u = u0
                hd = H_FFN[number]
                ft = number * FT
                for f0, cnt in GROUPS:
                    last_body = cnt // 2 - 1
                    act.activation(scrap[:, :], scrap[:, :], ACT.Silu).then_inc(scrap_done, 1)
                    scrap_n[0] += 1
                    act.wait_ge(scrap_done, scrap_n[0])
                    with act.Fori(0, cnt // 2) as i:
                        for j in range(2):
                            hi(u + 2 * j + 2, i)
                            hi(u + 2 * j + 3, i)
                            act.wait_ge(gate_scaled, at(i, 2, ft + f0 + j + 1))
                            act.activation(t0[:, :], t0[:, :], ACT.Silu).then_inc(silu_done, 1)
                    u += 2 * cnt
                    prep = f0 == GROUPS[-1][0] and number == 0
                    final = f0 == GROUPS[-1][0] and u + KT >= last_unit
                    for d in range(KT):
                        if not (final and d >= KT - 2):
                            hi(u + d + 2)
                        if prep:
                            prep_hi(1, d, hd + d)
                    u += KT
                    hd += KT

            scrap_n = [1]
            act.wait_ge(scrap_done, 1)

            act.wait_ge(vecs_kept, 1)
            for n in range(10):
                if n % 2 == 1:
                    keep_x(act, n)
            for d in range(KT):
                prep_hi(0, d, d)
                if d < 2:
                    hi(d)
            root(0)
            ffn(U_FFN1, 0, 0)
            if stop_after == "ffn1":
                root(1)
            else:
                root(1)
                act_mixer(act, hi, prep_hi)
                root(2)
                ffn(U_FFN2, 1, 2)
                root(3)
            keep_y(act, 1)

        @block.vector
        def _(dve):
            dve.memset(scrap[:, :], 0.0).then_inc(scrap_done, 1)
            for free in (up_scaled, lg_done, pt_kept):
                dve.sem_inc(free, 2)
            for start in (a_prod, a_lo, top_taken):
                dve.sem_inc(start, ONE)

            def prep(norm, d, h_count):
                n = norm * KT + d
                if d == 0:
                    if norm:
                        dve.wait_ge(var_done, norm)
                    dve.memset(ss[:, :], 0.0).then_inc(ss_zero, 1)
                dve.wait_ge(h_done, h_count + 1)
                if n:
                    dve.wait_ge(ss_done, n)
                dve.tensor_tensor(t1[:, :], h[:, d, :], h[:, d, :], ALU.mult).then_inc(sq_done, 1)
                dve.wait_ge(sq_done, n + 1)
                dve.wait_ge(ss_zero, norm + 1)
                dve.tensor_tensor(ss[:, :], ss[:, :], t1[:, :], ALU.add).then_inc(ss_done, 1)

            def prep_lo(norm, d):
                n = norm * KT + d
                dve.wait_ge(x_hi, n + 1)
                dve.scalar_tensor_tensor(out=xl[:, d, :], in0=h[:, d, :], scalar=gains[:, norm, d:d + 1],
                                         in1=xh[:, d, :].bitcast(F32), op0=ALU.mult,
                                         op1=ALU.subtract).then_inc(x_lo, 1)

            def invert(norm):
                dve.wait_ge(norm_sum, norm + 1)
                dve.tensor_scalar(halves(rstd[:, :]), ps[:, 6:8, 0:HALF], 1.0 / D, EPS, ALU.mult,
                                  ALU.add).then_inc(var_done, 1)
                dve.wait_ge(var_done, norm + 1)
                dve.reciprocal(rstd[:, :], rstd[:, :]).then_inc(inv_done, 1)

            def ffn(u0, number, norm):
                u = u0
                hd = H_FFN[number]
                ft = number * FT
                dve.wait_ge(rstd_done, norm + 1)
                for f0, cnt in GROUPS:
                    with dve.Fori(0, cnt // 2) as i:
                        for j in range(2):
                            F = ft + f0 + j
                            bank = 4 * j
                            dve.wait_ge(w_used, at(i, 4, u + 2 * j + RING + 1))
                            dve.wait_ge(a_prod, ONE + at(i, 2, F))
                            dve.tensor_tensor(halves(t0[:, :]), ps[:, bank:bank + 2, 0:HALF], halves(rstd[:, :]),
                                              ALU.mult).then_inc(gate_scaled, 1)
                            dve.wait_ge(w_used, at(i, 4, u + 2 * j + 1 + RING + 1))
                            dve.wait_ge(a_lo, ONE + at(i, 2, F))
                            dve.tensor_tensor(halves(t1[:, :]), ps[:, bank + 2:bank + 4, 0:HALF],
                                              halves(rstd[:, :]), ALU.mult).then_inc(up_scaled, 1)
                            dve.wait_ge(silu_done, at(i, 2, F + 1))
                            dve.wait_ge(up_scaled, at(i, 2, F + 3))
                            dve.tensor_tensor(t1[:, :], t0[:, :], t1[:, :], ALU.mult).then_inc(a_prod, 1)
                            dve.wait_ge(a_prod, ONE + at(i, 2, F + 1))
                            dve.tensor_copy(ah[:, i * 2 + j, :], t1[:, :]).then_inc(a_hi, 1)
                            dve.wait_ge(a_hi, at(i, 2, F + 1))
                            dve.tensor_tensor(al[:, i * 2 + j, :], t1[:, :], ah[:, i * 2 + j, :].bitcast(F32),
                                              ALU.subtract).then_inc(a_lo, 1)
                    u += 2 * cnt
                    last = f0 == GROUPS[-1][0]
                    for d in range(KT):
                        bank = 2 * (d % 4)
                        dve.wait_ge(w_used, u + d + RING + 1)
                        dve.wait_ge(h_done, hd - KT + d + 1)
                        dve.scalar_tensor_tensor(out=halves(h[:, d, :]), in0=ps[:, bank:bank + 2, 0:HALF], scalar=0.5,
                                                 in1=halves(h[:, d, :]), op0=ALU.mult, op1=ALU.add).then_inc(h_done, 1)
                        if last:
                            prep(norm + 1, d, hd + d)
                            if number == 0:
                                prep_lo(norm + 1, d)
                    u += KT
                    hd += KT

            dve.wait_ge(vecs_turned, 1)
            dve.tensor_copy(vecs[:, :], ps[:, 7, 0:4 * KT + 3]).then_inc(vecs_kept, 1)
            for n in range(0, 10, 2):
                keep_x(dve, n)
            dve.wait_ge(x_kept, 5)
            dve.wait_ge(x_kept_act, 5)
            dve.sem_inc(h_done, KT)
            dve.wait_ge(vecs_kept, 1)
            for d in range(KT):
                prep(0, d, d)
                prep_lo(0, d)
            invert(0)
            ffn(U_FFN1, 0, 0)
            invert(1)
            if stop_after != "ffn1":
                dve_mixer(dve, prep, prep_lo)
                invert(2)
                ffn(U_FFN2, 1, 2)
                invert(3)
            final_n = 1 if stop_after == "ffn1" else 3
            dve.wait_ge(rstd_done, final_n + 1)
            for d in range(KT):
                dve.scalar_tensor_tensor(out=h[:, d, :], in0=h[:, d, :], scalar=gains[:, 3, d:d + 1], in1=rstd[:, :],
                                         op0=ALU.mult, op1=ALU.mult).then_inc(y_done, 1)
            keep_y(dve, 0)

        @block.tensor
        def _(pe):
            pe.sem_inc(w_used, RING)
            for start in (qk_done, pv_done, ot_turned):
                pe.sem_inc(start, ONE)

            def product(u, bank, m, rh, rl, kts, i=None, before_k=None):
                slot = u % RING
                pe.wait_ge(w_split, at(i, RING, u + RING + 1))
                for k in range(kts):
                    if before_k:
                        before_k(k)
                    for n, (w, r) in enumerate(((wh, rh), (wh, rl), (wl, rh))):
                        for a in range(2):
                            mm = pe.matmul(ps[0:m, bank + a, 0:HALF], w[:, slot, k * P:k * P + m],
                                           r[:, k, a * HALF:(a + 1) * HALF], start=(k == 0 and n == 0),
                                           stop=(k == kts - 1 and n == 2))
                mm.then_inc(w_used, 1)

            def norm_product(norm):
                pe.wait_ge(ss_done, KT * (norm + 1))
                for a in range(2):
                    mm = pe.matmul(ps[:, 6 + a, 0:HALF], ones[:, :], ss[:, a * HALF:(a + 1) * HALF], start=True,
                                   stop=True)
                mm.then_inc(norm_sum, 1)

            def ffn(u0, number, norm):
                u = u0
                hd = H_FFN[number]
                ft = number * FT
                norm_product(norm)
                for f0, cnt in GROUPS:
                    def x_ready(k):
                        pe.wait_ge(x_lo, KT * norm + k + 1)

                    with pe.Fori(0, cnt // 2) as i:
                        for j in range(2):
                            pe.wait_ge(h_done, hd - 2 + 2 * j)
                            if j == 1:
                                pe.wait_ge(var_done, norm + 1)
                            pe.wait_ge(up_scaled, at(i, 2, ft + f0 + j + 1))
                            product(u + 2 * j, 4 * j, P, xh, xl, KT, i, x_ready if j == 0 else None)
                            product(u + 2 * j + 1, 4 * j + 2, P, xh, xl, KT, i)
                    u += 2 * cnt
                    F = ft + f0

                    def a_ready(k):
                        pe.wait_ge(a_lo, ONE + F + k + 1)

                    with pe.Fori(0, KT // 4) as i:
                        for j in range(4):
                            pe.wait_ge(up_scaled, F + cnt + (1 if j == 0 else 2))
                            pe.wait_ge(h_done, at(i, 4, hd + j - 3))
                            product(u + j, 2 * j, P, ah, al, cnt, i, a_ready if j == 0 else None)
                    u += KT
                    hd += KT

            pe.wait_ge(consts, 2)
            pe.wait_ge(const_loaded, 96)
            pe.transpose(ps[:, 7, 0:4 * KT + 3], vec_rows[:, :], ident[0:4 * KT + 3, 0:4 * KT + 3]).then_inc(vecs_turned, 1)
            pe.wait_ge(x_loaded, 32)
            pe.wait_ge(vecs_kept, 1)
            for n in range(10):
                t, half = n // 2, n % 2
                w = x_cols(n)[1]
                if n >= 8:
                    pe.wait_ge(x_kept, 5 - 4 if n == 8 else 1)
                    pe.wait_ge(x_kept_act, 1)
                for k in range(4):
                    c = (4 * half + k) * P
                    mm = pe.transpose(ps[:, n % 8, k * w:(k + 1) * w], xin[0:w, t, c:c + P], ident[0:w, 0:w])
                mm.then_inc(x_turned, 1)
            ffn(U_FFN1, 0, 0)
            norm_product(1)
            if stop_after != "ffn1":
                pe_mixer(pe, product)
                ffn(U_FFN2, 1, 2)
                norm_product(3)
            pe.wait_ge(y_done, KT)
            for n in range(8):
                t, half = n // 2, n % 2
                for k in range(4):
                    mm = pe.transpose(ps[:, n, k * P:(k + 1) * P],
                                      h[:, 4 * half + k, META + t * P:META + (t + 1) * P], ident[:, :])
                mm.then_inc(y_turned, 1)


INPUTS = ["x", "meta_tokens", "ffn1_norm", "ffn1_w_gate", "ffn1_w_up", "ffn1_w_down", "mix_norm", "w_in", "gla_w_a2",
          "gla_b_a", "gla_head_norm", "w_out", "ffn2_norm", "ffn2_w_gate", "ffn2_w_up", "ffn2_w_down", "final_norm"]
STOP = None


def rope_tables():
    import numpy as np
    f32 = np.float32
    inv = (f32(1.0) / (f32(10000.0) ** (np.arange(0, HD, 2, dtype=f32) / f32(HD)))).astype(f32)
    ang = (inv[:, None] * np.arange(TOK, dtype=f32)[None, :]).astype(f32)
    cos, sin = np.cos(ang).astype(f32), np.sin(ang).astype(f32)
    return np.concatenate([cos] * 4), np.concatenate([-sin, sin] * 2)


def kernel(**inputs):
    import numpy as np
    import concourse.bacc as bacc
    from concourse.bass_utils import run_bass_kernel_spmd as run

    nc = bacc.Bacc("TRN2", target_bir_lowering=False, num_devices=1)
    arrays, a = {}, {}
    given = {n: np.ascontiguousarray(inputs[n]) for n in INPUTS}
    given["cos_t"], given["sin_t"] = rope_tables()
    for name, v in given.items():
        if name != "meta_tokens" and v.ndim > 1 and v.shape[0] == 1:
            v = v[0]
        arrays[f"in_{name}"] = np.ascontiguousarray(v)
        a[name] = nc.dram_tensor(f"in_{name}", v.shape, F32, kind="ExternalInput").ap()
    out = nc.dram_tensor("out_0", (SEQ, D), F32, kind="ExternalOutput").ap()
    build(nc, a["x"], a["meta_tokens"],
          (a["ffn1_norm"], a["ffn1_w_gate"], a["ffn1_w_up"], a["ffn1_w_down"]),
          (a["ffn2_norm"], a["ffn2_w_gate"], a["ffn2_w_up"], a["ffn2_w_down"]),
          a["mix_norm"], a["w_in"], a["gla_w_a2"], a["gla_b_a"], a["gla_head_norm"], a["w_out"], a["final_norm"],
          a["cos_t"], a["sin_t"], out, STOP)
    r = run(nc, [arrays], core_ids=[0])
    return r.results[0]["out_0"].reshape(1, SEQ, D)
```

```python
import math
from contextlib import ExitStack

import concourse.bass as bass
from concourse import mybir

F32 = mybir.dt.float32
F32R = mybir.dt.float32r
U8 = mybir.dt.uint8
ALU = mybir.AluOpType
ACT = mybir.ActivationFunctionType
AX_X = mybir.AxisListType.X

P = 128
D = 1024
KT = D // P
META, SEQ = 16, 512
TOK = META + SEQ
HALF = TOK // 2
D_FF = 2816
FT = D_FF // P
EPS = 1e-6
GLA_HEADS, DK, DV = 4, 64, 128
HD = 64
HEADS = 8
TOPK = min(256, SEQ // 4)
GATE_NORM = 16.0
RING = 4
UNIT = KT * P
ONE = 1
NEG = -1.0e30
TAKEN = -3.0e38

GROUPS = [(0, 8), (8, 8), (16, FT - 16)]
FFN_UNITS = 2 * FT + KT * len(GROUPS)

C_GQK, C_GV, C_GR, C_GA, C_DQK, C_DV, C_IQ, C_IK = 0, 512, 1024, 1536, 1552, 2576, 3088, 3600
N_GA, N_IKW = 16, HD + HEADS

M_IQ, M_IKW, M_GA, M_GV, M_RAW, M_DV, MIX_UNITS = 0, 4, 5, 6, 10, 26, 30
R_Q, R_GR = 4, 12
U_FFN1 = 0
U_MIX = U_FFN1 + FFN_UNITS
U_OUT = U_MIX + MIX_UNITS
U_FFN2 = U_OUT + KT
U_END = U_FFN2 + FFN_UNITS

BLK = [(0, TOPK)] + [(TOPK + 100 * i, 100) for i in range((TOK - TOPK) // 100)]
SEEN = [s + n for s, n in BLK]
MASK_AT = [sum(SEEN[:b]) for b in range(len(BLK))]
WIN = [(w, min(P, TOK - w)) for w in range(0, TOK, P)]
FULL_WIN = TOK // P
LEVELS = [1, 2, 4, 8, 16, 32, 64]
NLV = len(LEVELS) + 1
GR_BEFORE = {0: 0, 2: 1, 5: 2, NLV: 3}
DV_BEFORE = {0: 0, 1: 1, 2: 2}
RC_WIN = [0, 1, 2, 3, 9]
RC_BLK = [4, 5, 6, 7, 8]


def at(i, step, base):
    return base if i is None else i * step + base


def halves(ap):
    return ap.rearrange("p (a n) -> p a n", a=2)


def build(nc, x, meta, ffn1, ffn2, mix_norm, w_in, w_a2, b_a, head_norm, w_out, final_norm,
          cos_t, sin_t, out):
    ctx = ExitStack()
    with ctx:
        def sb(name, shape, dt=F32, scope=ctx):
            return scope.enter_context(nc.sbuf_tensor(name, shape, dt))

        def sem(name):
            return ctx.enter_context(nc.semaphore(name))

        ps = ctx.enter_context(nc.psum_tensor("ps", [P, 8, 512], F32))
        h = sb("h", [P, KT, TOK])
        xh = sb("xh", [P, KT, TOK], F32R)
        xl = sb("xl", [P, KT, TOK], F32R)
        raw = sb("raw", [P, RING, UNIT])
        wh = sb("wh", [P, RING, UNIT], F32R)
        wl = sb("wl", [P, RING, UNIT], F32R)
        rstd = sb("rstd", [P, TOK])
        ss = sb("ss", [P, TOK])
        t01 = sb("t01", [P, 2, TOK])
        t0, t1 = t01[:, 0, :], t01[:, 1, :]
        ident = sb("ident", [P, P])
        ones = sb("ones", [P, P])
        vec_rows = sb("vec_rows", [4 * KT + 3, P])
        vecs = sb("vecs", [P, 4 * KT + 3])
        gains = vecs[:, 0:4 * KT].rearrange("p (n k) -> p n k", k=KT)
        ba = vecs[:, 4 * KT:4 * KT + 2]
        hn = vecs[:, 4 * KT + 2:4 * KT + 3]
        scrap = sb("scrap", [P, 1])
        n_orow = len(WIN) * GLA_HEADS
        pick = sb("pick", [P, 2 * n_orow - 1])
        ffn_scope = ExitStack()
        ah = sb("ah", [P, KT, TOK], F32R, ffn_scope)
        al = sb("al", [P, KT, TOK], F32R, ffn_scope)
        xin = sb("xin", [P, 5, D], F32, ffn_scope)
        ffn_scope.close()
        pja = sb("pja", [P, 8, TOK])
        iq = sb("iq", [P, 4, TOK])
        sw = sb("sw", [P, 4, TOK])
        pjb = sb("pjb", [P, 8, TOK])
        dv = sb("dv", [P, 5, 512])
        mask = sb("mask", [P, sum(SEEN)])
        cosr = sb("cosr", [P, TOK])
        sinr = sb("sinr", [P, TOK])
        ikga = sb("ikga", [P, 2, TOK])
        ik, ga = ikga[:, 0, :], ikga[:, 1, :]
        gb = sb("gb", [P, 2, TOK])
        tri = sb("tri", [P, P])
        lvm = sb("lvm", [P, len(LEVELS), P], U8)
        S = t1[:, 0:GLA_HEADS * DV].rearrange("p (g n) -> p g n", g=GLA_HEADS)
        small = sb("small", [P, 112])
        rcol = small[:, 0:10]
        iwt = small[:, 16:48]
        orow = t0[0:len(WIN) * GLA_HEADS, 0:P]
        rout = small[:, 76:80]
        top8 = [small[:, 96:104], small[:, 104:112]]
        elast = small[:, 56:66]
        wa2 = sb("wa2", [N_GA, 2, P])
        gla_scope = ExitStack()
        xa = sb("xa", [P, 2, TOK], F32, gla_scope)
        xb = sb("xb", [P, 2, TOK], F32, gla_scope)
        gv = sb("gv", [P, 5, 512], F32, gla_scope)
        gla_scope.close()
        lg = sb("lg", [P, 2, TOK])
        pr = sb("pr", [P, 2, TOK])
        pt = sb("pt", [P, 2, 512])
        vst0 = sb("vst0", [P, 5, P])
        ikz = [ik, xa[:, 1, :]]
        dg = sb("dg", [P, 2, P])
        qst = [ik, cosr]
        kst = [[gb[:, 0, :], gb[:, 1, :]], [sinr, ga]]
        vst = [vst0, t01[:, :, :].rearrange("p a n -> p (a n)")[:, 0:5 * P].rearrange("p (c n) -> p c n", c=5)]
        stat = small[:, 66:76]
        AT = iq[:, :, :].rearrange("p a n -> p (a n)")
        oT = sw

        def at_win(w):
            width = WIN[w][1]
            base = w * GLA_HEADS * P
            return AT[0:width, base:base + GLA_HEADS * width].rearrange("p (t e n) -> p t e n", t=2, e=2)

        w_in_slot = [sem(f"w_in_slot{i}") for i in range(RING)]
        w_hi = sem("w_hi")
        w_split = sem("w_split")
        w_used = sem("w_used")
        x_loaded = [sem(f"x_loaded{t}") for t in range(5)]
        const_loaded, mix_loaded = sem("const_loaded"), sem("mix_loaded")
        vecs_turned, vecs_kept = sem("vecs_turned"), sem("vecs_kept")
        c_zero, consts, lv_step = sem("c_zero"), sem("consts"), sem("lv_step")
        x_turned, x_kept = sem("x_turned"), sem("x_kept")
        h_done, sq_done, ss_zero, ss_done = sem("h_done"), sem("sq_done"), sem("ss_zero"), sem("ss_done")
        x_hi, x_lo = sem("x_hi"), sem("x_lo")
        norm_sum, var_done, inv_done, rstd_done = sem("norm_sum"), sem("var_done"), sem("inv_done"), sem("rstd_done")
        gate_scaled, up_scaled, silu_done = sem("gate_scaled"), sem("up_scaled"), sem("silu_done")
        a_prod, a_hi, a_lo = sem("a_prod"), sem("a_hi"), sem("a_lo")
        tables_done, pj_kept = sem("tables_done"), sem("pj_kept")
        iw_scaled, ga_scaled = sem("iw_scaled"), sem("ga_scaled")
        swapped = [sem(f"swapped{i}") for i in range(13)]
        rope_sin, rope_cos, rope_done = sem("rope_sin"), sem("rope_cos"), sem("rope_done")
        ik_copied, ik_zero, kst_zero = sem("ik_copied"), sem("ik_zero"), sem("kst_zero")
        tok_turned, tok_kept, v_kept = sem("tok_turned"), sem("tok_kept"), sem("v_kept")
        idx_done, relu_done, acc_done = sem("idx_done"), sem("relu_done"), sem("acc_done")
        top_found, top_taken, mask_done = sem("top_found"), sem("top_taken"), sem("mask_done")
        q_sin, q_cos, q_roped = sem("q_sin"), sem("q_cos"), sem("q_roped")
        z_done, gate_y, gate_abs, gate_exp, gate_ln, gate_g, gate_cum = (
            sem("z_done"), sem("gate_y"), sem("gate_abs"), sem("gate_exp"), sem("gate_ln"), sem("gate_g"),
            sem("gate_cum"))
        zq_zero, picked = sem("zq_zero"), sem("picked")
        gqk_scaled, lv_diff, lv_exp, lv_x, lv_mm, at_done = (
            sem("gqk_scaled"), sem("lv_diff"), sem("lv_exp"), sem("lv_x"), sem("lv_mm"), sem("at_done"))
        kd_turned, kd_kept, s_mm, s_new, o_mm, o_kept = (
            sem("kd_turned"), sem("kd_kept"), sem("s_mm"), sem("s_new"), sem("o_mm"), sem("o_kept"))
        o_sq, o_sum, o_var, o_inv, o_rstd, gr_scaled, gr_silu, o_spread, m_hi, m_lo = (
            sem("o_sq"), sem("o_sum"), sem("o_var"), sem("o_inv"), sem("o_rstd"), sem("gr_scaled"),
            sem("gr_silu"), sem("o_spread"), sem("m_hi"), sem("m_lo"))
        diag_done = sem("diag_done")
        staged, qk_done, lg_done, exp_done, sum_inv, pt_done, pt_kept, pv_done, pv_kept, ot_turned = (
            sem("staged"), sem("qk_done"), sem("lg_done"), sem("exp_done"), sem("sum_inv"),
            sem("pt_done"), sem("pt_kept"), sem("pv_done"), sem("pv_kept"), sem("ot_turned"))
        kd_ready, qe_ready, kd_diff, kd_exp, qe_exp, el_exp, s_zero = (
            sem("kd_ready"), sem("qe_ready"), sem("kd_diff"), sem("kd_exp"), sem("qe_exp"), sem("el_exp"),
            sem("s_zero"))
        g_hi, g_lo = sem("g_hi"), sem("g_lo")
        o_out, o_normed, tri_done, pt_first, m_first = (
            sem("o_out"), sem("o_normed"), sem("tri_done"), sem("pt_first"), sem("m_first"))
        passed = sem("passed")
        y_done, y_turned, y_kept, y_kept_act, stored = (
            sem("y_done"), sem("y_turned"), sem("y_kept"), sem("y_kept_act"), sem("stored"))

        H_FFN = [KT, KT + KT * len(GROUPS) + KT]
        H_OUT = KT + KT * len(GROUPS)
        H_END = H_FFN[1] + KT * len(GROUPS)
        FFNS = [(ffn1, U_FFN1, 0), (ffn2, U_FFN2, 1)]

        scrap_done = sem("scrap_done")

        def x_cols(n):
            t = n // 2
            return (META + t * P, P) if t < 4 else (0, META)

        def keep_x(eng, n):
            c, w = x_cols(n)
            eng.wait_ge(x_turned, n + 1)
            src = ps[:, n % 8, 0:4 * w].rearrange("p (k n) -> p k n", k=4)
            dst = h[:, 4 * (n % 2):4 * (n % 2) + 4, c:c + w]
            if n % 2 == 1:
                eng.activation(dst, src, ACT.Copy).then_inc(x_kept_act, 1)
            else:
                eng.tensor_copy(dst, src).then_inc(x_kept, 1)

        x_kept_act, sq0_done = sem("x_kept_act"), sem("sq0_done")

        def keep_y(eng, half):
            eng.wait_ge(rstd_done, 4)
            for t in range(4):
                eng.wait_ge(y_turned, 4 * half + t + 1)
                src, dst = ps[:, 4 * half + t, :], xin[:, t, 512 * half:512 * half + 512]
                if half:
                    eng.activation(dst, src, ACT.Copy, scale=rout[:, t:t + 1]).then_inc(y_kept_act, 1)
                else:
                    eng.tensor_scalar(dst, src, rout[:, t:t + 1], None, ALU.mult).then_inc(y_kept, 1)

        def swap_r(sp, swap, r):
            n = r - R_Q
            sp.wait_ge(pj_kept, 5 + r + 1)
            if n < 4:
                sp.wait_ge(rope_done, 5)
            else:
                sp.wait_ge(q_roped, n - 3)
            swap(5 + n, pjb[:, n, :], sw[:, n % 4, :])

        V_BANKS = {M_GV: [4, 5, 6, 7, 0], M_DV: [3, 4, 5, 6, 7]}
        INDEX = [(b, hd) for b in range(1, len(BLK)) for hd in range(HEADS)]
        RC = [(RC_WIN[w], s, n) for w, (s, n) in enumerate(WIN)] + [(RC_BLK[b], s, n) for b, (s, n) in enumerate(BLK)]

        def lv_ap(ap, g):
            n = TOK if TOK % (2 * LEVELS[g - 1]) == 0 else FULL_WIN * P
            return ap[:, :, 0:n].rearrange("p t (m a b) -> p t m a b", a=2, b=LEVELS[g - 1])

        def lv_steps(g):
            if g == 0:
                return [[w] for w in range(len(WIN))]
            pairs = [[w, w + 1] for w in range(0, FULL_WIN, 2)]
            return pairs + [[FULL_WIN]] if LEVELS[g - 1] < WIN[-1][1] else pairs

        STEPS = [(g, ws) for g in range(NLV) for ws in lv_steps(g)]

        def steps_before(g):
            return sum(len(lv_steps(k)) for k in range(g))

        zq = [t01[:, :, :].rearrange("p t (e n) -> p t e n", e=2), ikga[:, :, :].rearrange("p t (e n) -> p t e n", e=2)]
        xbuf = [xa, xb]
        kdt = pja[:, 2:4, :].rearrange("p t n -> p (t n)")[:, 0:FULL_WIN * 2 * P].rearrange(
            "p (w t n) -> p w t n", w=FULL_WIN, t=2)

        def pe_mixer(pe, product, norm_product):
            for m in range(6):
                if m == 3:
                    pe.wait_ge(var_done, 2)
                if m >= 4:
                    pe.wait_ge(pj_kept, m - 3)
                rows = N_IKW if m == M_IKW else N_GA if m == M_GA else P
                product(U_MIX + m, 2 * (m % 4), rows, xh, xl, KT,
                        before_k=(lambda k: pe.wait_ge(x_lo, KT + k + 1)) if m == 0 else None)
                if m == 0:
                    norm_product(1)

            def v_unit(m0, q, blocks):
                u = U_MIX + m0 + q
                slot = u % RING
                pe.wait_ge(w_split, u + RING + 1)
                for b, (s, n) in enumerate(blocks):
                    for k in range(2):
                        for c, (xx, ww) in enumerate(((xh, wh), (xl, wh), (xh, wl))):
                            mm = pe.matmul(ps[0:n, V_BANKS[m0][b], :], xx[:, 2 * q + k, s:s + n],
                                           ww[:, slot, k * 512:(k + 1) * 512], start=(q == 0 and k == 0 and c == 0),
                                           stop=(q == 3 and k == 1 and c == 2))
                mm.then_inc(w_used, 1)

            pe.wait_ge(pj_kept, 5)
            pe.wait_ge(iw_scaled, 1)
            v_unit(M_GV, 0, WIN)
            pe.wait_ge(ga_scaled, 1)
            pe.wait_ge(rstd_done, 2)
            for c, s, n in RC:
                pe.matmul(ps[0:n, 3, c:c + 1], rstd[0:1, s:s + n], ones[0:1, 0:1], start=True, stop=True)
            for b in range(1, len(BLK)):
                s, n = BLK[b]
                mm = pe.transpose(ps[0:n, 1, 8 * b:8 * b + 8], ga[64:64 + HEADS, s:s + n],
                                  ident[64:64 + HEADS, 64:64 + HEADS])
            mm.then_inc(tok_turned, 1)
            for q in range(1, 4):
                v_unit(M_GV, q, WIN)

            pe.wait_ge(rope_done, 5)
            pe.wait_ge(ik_copied, 16)
            pe.wait_ge(ik_zero, 2)
            for n, (b, hd) in enumerate(INDEX):
                q = (n + 1) % 4
                if n == 0:
                    pe.wait_ge(tok_kept, 4)
                elif n < 4:
                    pe.wait_ge(v_kept, [2, 4, 5][n - 1])
                else:
                    pe.wait_ge(relu_done, n - 3)
                s, w = BLK[b]
                for a, (k0, kn) in enumerate(key_parts(b)):
                    mm = pe.matmul(ps[0:w, 2 * q + a, 0:kn], iq[:, hd // 2, s:s + w],
                                   ikz[hd % 2][:, k0:k0 + kn], start=True, stop=True)
                mm.then_inc(idx_done, 1)
            for t in range(2):
                q = 1 + t
                pe.wait_ge(relu_done, 29 + t)
                for a in range(2):
                    mm = pe.matmul(ps[:, 2 * q + a, 0:HALF], wa2[:, t, :], ga[0:N_GA, a * HALF:(a + 1) * HALF],
                                   start=True, stop=True)
                mm.then_inc(z_done, 1)
            with pe.Fori(0, R_GR // 4) as i:
                for j in range(4):
                    if j in (1, 2):
                        pe.wait_ge(gate_y, j)
                    else:
                        pe.wait_ge(relu_done, 32)
                    pe.wait_ge(pj_kept, at(i, 4, j + 2))
                    product(U_MIX + M_RAW + j, 2 * j, P, xh, xl, KT, i)

            def gr_unit(n):
                pe.wait_ge(pj_kept, 5 + (R_GR - 3 if n == 0 else R_GR + n))
                product(U_MIX + M_RAW + R_GR + n, 0, P, xh, xl, KT)

            n = 0
            for g in range(NLV):
                if g in GR_BEFORE:
                    gr_unit(GR_BEFORE[g])
                if g == 0:
                    pe.wait_ge(pj_kept, 5 + R_GR)
                    pe.wait_ge(gqk_scaled, 4)
                    pe.wait_ge(zq_zero, 4)
                else:
                    pe.wait_ge(lv_x, 3 * g)
                for ws in lv_steps(g):
                    if n >= 3:
                        pe.wait_ge(at_done, n - 2)
                    for w in ws:
                        s, width = WIN[w]
                        if g == 0:
                            for hd in range(GLA_HEADS):
                                t, e = hd // 2, 64 * (hd % 2)
                                mm = pe.matmul(ps[0:width, lv_bank(n) + hd % 2, t * width:(t + 1) * width],
                                               pja[e:e + DK, 2 + t, s:s + width], pja[e:e + DK, t, s:s + width],
                                               start=True, stop=True)
                        else:
                            for t in range(2):
                                c = 2 * P * (w - ws[0]) + t * width
                                mm = pe.matmul(ps[0:width, lv_bank(n), c:c + width], xbuf[g % 2][:, t, s:s + width],
                                               zq[g % 2][:, t, :, s // 2:(s + width) // 2], start=True, stop=True)
                    mm.then_inc(lv_mm, 1)
                    n += 1
            gr_unit(GR_BEFORE[NLV])
            pe.wait_ge(at_done, len(STEPS))
            v_unit(M_DV, DV_BEFORE[0], BLK)
            pe.wait_ge(pj_kept, 5 + 16)
            pe.wait_ge(kd_ready, 2)
            for w, (s, width) in enumerate(WIN[0:FULL_WIN]):
                for t in range(2):
                    c = (2 * (w % 2) + t) * P
                    mm = pe.transpose(ps[:, w // 2, c:c + P], xb[:, t, s:s + width], ident[:, :])
                if w % 2:
                    mm.then_inc(kd_turned, 1)
            pe.wait_ge(qe_ready, 1)
            pe.wait_ge(kd_kept, 2)
            for w, (s, width) in enumerate(WIN):
                if w and w in DV_BEFORE:
                    v_unit(M_DV, DV_BEFORE[w], BLK)
                if w:
                    pe.wait_ge(s_new, GLA_HEADS * w)
                if w < FULL_WIN:
                    for hd in range(GLA_HEADS):
                        t, e = hd // 2, 64 * (hd % 2)
                        mm = pe.matmul(ps[e:e + DK, 2, t * DV:(t + 1) * DV], kdt[0:width, w, t, e:e + DK],
                                       gv[0:width, w, hd * DV:(hd + 1) * DV], start=True, stop=True)
                    mm.then_inc(s_mm, 1)
                if w >= 2:
                    pe.wait_ge(o_sq, 2 * (w - 1))
                for hd in range(GLA_HEADS):
                    t, e = hd // 2, 64 * (hd % 2)
                    o = ps[:, w % 2, hd * width:(hd + 1) * width]
                    mm = pe.matmul(o, gv[0:width, w, hd * DV:(hd + 1) * DV], at_win(w)[:, t, hd % 2, :], start=True,
                                   stop=(w == 0))
                    if w:
                        mm = pe.matmul(o, S[:, hd, :], xa[:, t, s:s + width], start=False, stop=True)
                mm.then_inc(o_mm, 1)
            pe.wait_ge(s_new, GLA_HEADS * FULL_WIN)
            pe.wait_ge(picked, 2)
            for w, (s, width) in enumerate(WIN):
                pe.wait_ge(o_sq, 2 * (w + 1))
                for hd in range(GLA_HEADS):
                    c = GLA_HEADS * w + hd
                    mm = pe.matmul(ps[0:n_orow, 2, 0:width], pick[:, n_orow - 1 - c:2 * n_orow - 1 - c],
                                   o_square[hd // 2][:, hd % 2, s:s + width], start=(c == 0), stop=(c == n_orow - 1))
            mm.then_inc(o_sum, 1)
            v_unit(M_DV, 3, BLK)
            pe.wait_ge(o_rstd, 1)
            pe.wait_ge(o_kept, len(WIN))
            for w, (s, width) in enumerate(WIN):
                if w >= 3:
                    pe.wait_ge(v_kept, 5 + w - 2)
                for hd in range(GLA_HEADS):
                    c = GLA_HEADS * w + hd
                    mm = pe.matmul(ps[:, w, hd * width:(hd + 1) * width],
                                   ident[0:n_orow, c:c + 1].broadcast_to([n_orow, P]), orow[:, 0:width],
                                   start=True, stop=True)
                mm.then_inc(o_spread, 1)

            pe.wait_ge(o_normed, len(WIN))
            pe.wait_ge(v_kept, 10)
            pe.wait_ge(kst_zero, 4)
            with pe.Fori(0, HEADS // 4) as i:
                def logits(n):
                    pair, e, b, s, w = att_step(n)
                    if n % 10 == 0:
                        pe.wait_ge(staged, at(i, 10, 5 * (pair + 1)))
                    pe.wait_ge(lg_done, at(i, N_ATT, n + 1))
                    for a, (k0, kn) in enumerate(key_parts(b)):
                        mm = pe.matmul(ps[0:w, QK_BANK[b] + a, 0:kn], qst[pair][:, s:s + w],
                                       kst[pair][e][:, k0:k0 + kn], start=True, stop=True)
                    mm.then_inc(qk_done, 1)

                def values(n):
                    pair, e, b, s, w = att_step(n)
                    pe.wait_ge(pt_kept, at(i, N_ATT, n + 3))
                    pe.wait_ge(m_lo, at(i, N_ATT, n + 1))
                    for c in range(b + 1):
                        wc = BLK[c][1]
                        mm = pe.matmul(ps[HD * e:HD * (e + 1), 6 + n % 2, 0:w], vst[pair][0:wc, c, HD * e:HD * (e + 1)],
                                       pt[0:wc, n % 2, c * w:(c + 1) * w], start=(c == 0), stop=(c == b))
                    mm.then_inc(pv_done, 1)

                logits(0)
                logits(1)
                for n in range(N_ATT):
                    pair, e, b, s, w = att_step(n)
                    if n + 2 < N_ATT:
                        logits(n + 2)
                    pe.wait_ge(diag_done, at(i, N_ATT, n + 1))
                    pe.wait_ge(pt_kept, at(i, N_ATT, n + 1))
                    for c in range(b + 1):
                        sc, wc = BLK[c]
                        mm = pe.matmul(ps[0:wc, 4 + n % 2, c * w:(c + 1) * w], pr[0:w, n % 2, sc:sc + wc],
                                       dg[0:w, n % 2, 0:w], start=True, stop=True)
                    mm.then_inc(pt_done, 1)
                    if n:
                        values(n - 1)
                values(N_ATT - 1)

            pe.wait_ge(g_lo, GLA_HEADS)
            pe.wait_ge(m_lo, 2 + HEADS // 4 * N_ATT)
            with pe.Fori(0, KT // 4) as i:
                for j in range(4):
                    pe.wait_ge(h_done, at(i, 4, H_OUT + j - 3))
                    product(U_OUT + j, 2 * j, P, ah, al, KT, i, tiles=MIX_TILE)

        def key_parts(b):
            n = SEEN[b]
            return [(0, n)] if n <= 512 else [(0, HALF), (HALF, n - HALF)]

        def key_view(ap, b):
            return ap if SEEN[b] <= 512 else halves(ap)

        def key_psum(b, w, bank):
            return ps[0:w, bank, 0:SEEN[b]] if SEEN[b] <= 512 else ps[0:w, bank:bank + 2, 0:HALF]

        o_square = [xb, pja[:, 0:2, :]]

        N_ATT = 4 * len(BLK)
        QK_BANK = [0, 1, 2, 0, 1]
        MIX_TILE = [4, 5, 6, 7, 0, 1, 2, 3]

        def att_step(n):
            pair, rest = divmod(n, 2 * len(BLK))
            e, b = divmod(rest, len(BLK))
            return (pair, e, b) + BLK[b]

        def lv_bank(n):
            return 2 + 2 * (n % 3)

        def act_mixer(act, hi, prep_hi, root):
            def keep(bank, dst, rows, u, i=None):
                act.wait_ge(w_used, at(i, 4, u + RING + 1))
                act.activation(halves(dst), ps[0:rows, bank:bank + 2, 0:HALF], ACT.Copy).then_inc(pj_kept, 1)

            def keep_v(dst, m0, blocks, cols):
                act.wait_ge(w_used, U_MIX + m0 + 3 + RING + 1)
                act.wait_ge(tok_kept, 4)
                for b, (s, n) in enumerate(blocks):
                    act.activation(dst[0:n, b, :], ps[0:n, V_BANKS[m0][b], :], ACT.Copy,
                                   scale=rcol[0:n, cols[b]:cols[b] + 1]).then_inc(v_kept, 1)

            for m in range(6):
                hi(U_MIX + m + 2)
                if m == 1:
                    root(1)
                if m < 4:
                    keep(2 * m, iq[:, m, :], P, U_MIX + m)
                elif m == 4:
                    keep(0, ik[0:HD, :], HD, U_MIX + m)
            for q in range(4):
                hi(U_MIX + M_GV + q + 2)
            keep_v(gv, M_GV, WIN, RC_WIN)
            for n, (b, hd) in enumerate(INDEX):
                w = BLK[b][1]
                act.wait_ge(idx_done, n + 1)
                if n >= 2:
                    act.wait_ge(acc_done, n - 1)
                act.activation(key_view(gb[0:w, n % 2, 0:SEEN[b]], b), key_psum(b, w, 2 * ((n + 1) % 4)),
                               ACT.Relu).then_inc(relu_done, 1)
            act.wait_ge(gate_y, 2)
            act.activation(gb[:, :, :], xa[:, :, :], ACT.Abs).then_inc(gate_abs, 1)
            act.wait_ge(gate_abs, 1)
            act.activation(gb[:, :, :], gb[:, :, :], ACT.Exp, scale=-1.0).then_inc(gate_exp, 1)
            act.wait_ge(gate_exp, 1)
            act.activation(gb[:, :, :], gb[:, :, :], ACT.Ln, bias=1.0).then_inc(gate_ln, 1)
            u = U_MIX + M_RAW
            for part, n in ((pja, 1), (pjb, 2)):
                with act.Fori(0, n) as i:
                    for j in range(4):
                        hi(u + j + 2, i)
                        keep(2 * j, part[:, i * 4 + j, :], P, u + j, i)
                u += 4 * n
            for g in range(NLV + 1):
                if 0 < g < NLV:
                    act.wait_ge(lv_diff, 2 * g)
                    part = xbuf[g % 2][:, :, 0:TOK if TOK % (2 * LEVELS[g - 1]) == 0 else FULL_WIN * P]
                    act.activation(part, part, ACT.Exp,
                                   scale=1.0 / GATE_NORM).then_inc(lv_exp, 1)
                if g == NLV:
                    act.wait_ge(lv_mm, steps_before(NLV - 1))
                    act.activation(xa[:, :, :], gb[:, :, :], ACT.Exp, scale=1.0 / GATE_NORM).then_inc(qe_exp, 1)
                    act.activation(elast.rearrange("p (t w) -> p t w", t=2)[:, :, 0:FULL_WIN],
                                   gb[:, :, P - 1:FULL_WIN * P:P], ACT.Exp, scale=1.0 / GATE_NORM).then_inc(el_exp, 1)
                    act.wait_ge(kd_diff, 2)
                    act.activation(xb[:, :, 0:FULL_WIN * P], xb[:, :, 0:FULL_WIN * P], ACT.Exp,
                                   scale=1.0 / GATE_NORM).then_inc(kd_exp, 1)
                if g in GR_BEFORE:
                    hi(u + 2 if GR_BEFORE[g] < 3 else u + 3)
                    if GR_BEFORE[g] == 2:
                        hi(u + 3)
                    if GR_BEFORE[g] < 3:
                        keep(0, pja[:, 4 + GR_BEFORE[g], :], P, u)
                    u += 1
            hi(u + 3)
            keep(0, pja[:, 7, :], P, u - 1)
            for w, (s, n) in enumerate(WIN):
                act.wait_ge(o_mm, w + 1)
                if w == 0:
                    act.wait_ge(q_roped, 8)
                    act.wait_ge(kd_turned, 2)
                o = ps[:, w % 2, 0:GLA_HEADS * n].rearrange("p (g n) -> p g n", g=GLA_HEADS)
                act.activation(oT[:, :, s:s + n], o, ACT.Copy).then_inc(o_kept, 1)
                for pair in range(2):
                    act.activation(o_square[pair][:, :, s:s + n], o[:, 2 * pair:2 * pair + 2, :],
                                   ACT.Square).then_inc(o_sq, 1)
                if w == 0:
                    hi(U_OUT)
                elif w == 1:
                    hi(U_OUT + 1)
                elif w == 2:
                    act.wait_ge(gr_scaled, 4)
                    act.activation(pja[:, 4:8, :], pja[:, 4:8, :], ACT.Silu).then_inc(gr_silu, 1)
            act.wait_ge(o_inv, 1)
            act.activation(orow, orow, ACT.Sqrt).then_inc(o_rstd, 1)
            keep_v(dv, M_DV, BLK, RC_BLK)
            act.activation(scrap[:, :], scrap[:, :], ACT.Exp).then_inc(scrap_done, 1)
            with act.Fori(0, HEADS // 4) as i:
                def probs(n):
                    pair, e, b, s, w = att_step(n)
                    act.wait_ge(lg_done, at(i, N_ATT, n + 3))
                    act.wait_ge(pt_done, at(i, N_ATT, n + 1))
                    act.activation(pr[0:w, n % 2, 0:SEEN[b]], lg[0:w, n % 2, 0:SEEN[b]], ACT.Exp, scale=-1.0,
                                   bias=stat[0:w, 4 + n % 2:5 + n % 2],
                                   accum_out=stat[0:w, 6 + n % 2:7 + n % 2]).then_inc(exp_done, 1)
                    act.wait_ge(sum_inv, at(i, N_ATT, n + 1))
                    act.activation(dg[0:w, n % 2, 0:w], ident[0:w, 0:w], ACT.Copy,
                                   scale=stat[0:w, 8 + n % 2:9 + n % 2]).then_inc(diag_done, 1)

                def keep_hi(n):
                    pair, e, b, s, w = att_step(n)
                    rows = slice(HD * e, HD * (e + 1))
                    act.wait_ge(pv_done, at(i, N_ATT, n + 1))
                    act.activation(ah[rows, 2 * i + pair, s:s + w], ps[rows, 6 + n % 2, 0:w],
                                   ACT.Copy).then_inc(m_hi, 1)

                probs(0)
                for n in range(N_ATT):
                    if n + 1 < N_ATT:
                        probs(n + 1)
                    if n:
                        keep_hi(n - 1)
                keep_hi(N_ATT - 1)
            for d in range(KT):
                hi(U_OUT + d + 2)
                prep_hi(2, d, H_OUT + d)

        def dve_mixer(dve, prep, prep_lo):
            dve.wait_ge(rstd_done, 2)
            dve.wait_ge(mix_loaded, 48)
            dve.tensor_tensor(cosr[:, :], cosr[:, :], rstd[:, :], ALU.mult).then_inc(tables_done, 1)
            dve.tensor_tensor(sinr[:, :], sinr[:, :], rstd[:, :], ALU.mult).then_inc(tables_done, 1)
            dve.wait_ge(tables_done, 2)

            def rope(n, x, s, rows):
                dve.wait_ge(swapped[n], 64 if rows == P else 32)
                dve.tensor_tensor(s[0:rows, :], s[0:rows, :], sinr[0:rows, :], ALU.mult).then_inc(rope_sin, 1)
                dve.tensor_tensor(x[0:rows, :], x[0:rows, :], cosr[0:rows, :], ALU.mult).then_inc(rope_cos, 1)
                dve.wait_ge(rope_sin, n + 1)
                dve.wait_ge(rope_cos, n + 1)
                dve.tensor_tensor(x[0:rows, :], x[0:rows, :], s[0:rows, :], ALU.add).then_inc(rope_done, 1)

            for m in range(4):
                rope(m, iq[:, m, :], sw[:, m, :], P)
            dve.wait_ge(w_used, U_MIX + M_IKW + RING + 1)
            dve.scalar_tensor_tensor(out=halves(ga[64:64 + HEADS, :]), in0=ps[64:64 + HEADS, 0:2, 0:HALF],
                                     scalar=HEADS ** -0.5 * HD ** -0.5, in1=halves(rstd[64:64 + HEADS, :]),
                                     op0=ALU.mult, op1=ALU.mult).then_inc(iw_scaled, 1)
            dve.wait_ge(w_used, U_MIX + M_GA + RING + 1)
            dve.tensor_tensor(halves(ga[0:N_GA, :]), ps[0:N_GA, 2:4, 0:HALF], halves(rstd[0:N_GA, :]),
                              ALU.mult).then_inc(ga_scaled, 1)
            rope(4, ik, sw[:, 0, :], HD)
            dve.wait_ge(tok_turned, 1)
            dve.tensor_copy(rcol[:, 0:5], ps[:, 3, 0:5]).then_inc(tok_kept, 1)
            dve.tensor_copy(rcol[0:100, 5:9], ps[0:100, 3, 5:9]).then_inc(tok_kept, 1)
            dve.tensor_copy(rcol[0:WIN[-1][1], 9:10], ps[0:WIN[-1][1], 3, 9:10]).then_inc(tok_kept, 1)
            dve.tensor_copy(iwt[0:100, :], ps[0:100, 1, 8:40]).then_inc(tok_kept, 1)
            dve.wait_ge(tok_kept, 4)
            dve.wait_ge(consts, 3)
            for n, (b, hd) in enumerate(INDEX):
                w = BLK[b][1]
                sc = mask[0:w, MASK_AT[b]:MASK_AT[b] + SEEN[b]]
                weight = iwt[0:w, 8 * (b - 1) + hd:8 * (b - 1) + hd + 1]
                r = gb[0:w, n % 2, 0:SEEN[b]]
                dve.wait_ge(relu_done, n + 1)
                if hd == 0:
                    dve.tensor_scalar(sc, r, weight, None, ALU.mult).then_inc(acc_done, 1)
                else:
                    dve.wait_ge(acc_done, n)
                    dve.scalar_tensor_tensor(out=sc, in0=r, scalar=weight, in1=sc, op0=ALU.mult,
                                             op1=ALU.add).then_inc(acc_done, 1)
            dve.wait_ge(acc_done, 32)
            for b in range(len(BLK)):
                s, w = BLK[b]
                own = mask[0:w, MASK_AT[b] + s:MASK_AT[b] + s + w]
                if b == 0:
                    dve.tensor_copy(own, tri[0:w, 0:w]).then_inc(mask_done, 1)
                else:
                    dve.tensor_tensor(own, own, tri[0:w, 0:w], ALU.add).then_inc(tri_done, 1)
            for t in range(2):
                dve.wait_ge(z_done, t + 1)
                dve.tensor_scalar(halves(xa[:, t, :]), ps[:, 2 + 2 * t:4 + 2 * t, 0:HALF], ba[:, t:t + 1], None,
                                  ALU.add).then_inc(gate_y, 1)
            for z in zq:
                for e in range(2):
                    dve.memset(z[64 * (1 - e):64 * (1 - e) + DK, :, e, :], 0.0).then_inc(zq_zero, 1)
            dve.wait_ge(tri_done, 4)
            rounds = TOPK // 8
            for pair in range(2):
                def blocks():
                    for c in range(2):
                        b = 1 + 2 * pair + c
                        w = BLK[b][1]
                        yield c, top8[c][0:w, :], mask[0:w, MASK_AT[b]:MASK_AT[b] + SEEN[b]]

                base = 2 * pair * rounds
                with dve.Fori(0, rounds // 4) as i:
                    for j in range(4):
                        for c, top, sc in blocks():
                            dve.wait_ge(top_taken, at(i, 8, base + 2 * j + c + 1))
                            dve.sem_inc(passed, 1)
                            dve.max(top, sc).then_inc(top_found, 1)
                        for c, top, sc in blocks():
                            dve.wait_ge(top_found, at(i, 8, base + 2 * j + c + 1))
                            dve.sem_inc(passed, 1)
                            dve.match_replace(sc, top, sc, TAKEN).then_inc(top_taken, 1)
                for c, top, sc in blocks():
                    dve.wait_ge(top_taken, base + 2 * rounds + c + 1)
                    dve.tensor_scalar(sc, sc, TAKEN * 0.5, NEG, ALU.is_gt, ALU.mult).then_inc(mask_done, 1)

            dve.wait_ge(pj_kept, 5 + 4)
            for t in range(4):
                dve.scalar_tensor_tensor(out=pja[:, t, :], in0=pja[:, t, :], scalar=DK ** -0.5 if t < 2 else 1.0,
                                         in1=rstd[:, :], op0=ALU.mult, op1=ALU.mult).then_inc(gqk_scaled, 1)
            dve.wait_ge(gate_ln, 1)
            dve.scalar_tensor_tensor(out=xa[:, :, :], in0=xa[:, :, :], scalar=0.0, in1=gb[:, :, :], op0=ALU.min,
                                     op1=ALU.subtract).then_inc(gate_g, 1)
            dve.wait_ge(gate_g, 1)
            for t in range(2):
                for s, w in WIN:
                    dve.tensor_tensor_scan(gb[:, t, s:s + w], ones[:, 0:w], xa[:, t, s:s + w], 0.0, ALU.mult,
                                           ALU.add).then_inc(gate_cum, 1)
            dve.wait_ge(gate_cum, 2 * len(WIN))
            dve.wait_ge(gqk_scaled, 4)

            def level_diff(g):
                if g >= 3:
                    dve.wait_ge(lv_mm, steps_before(g - 1))
                b5, x5 = lv_ap(gb, g), lv_ap(xbuf[g % 2], g)
                s = LEVELS[g - 1]
                ref = b5[:, :, :, 0, s - 1:s].broadcast_to([P, 2, b5.shape[2], s])
                dve.tensor_tensor(x5[:, :, :, 0, :], ref, b5[:, :, :, 0, :], ALU.subtract).then_inc(lv_diff, 1)
                dve.tensor_tensor(x5[:, :, :, 1, :], b5[:, :, :, 1, :], ref, ALU.subtract).then_inc(lv_diff, 1)

            def level_x(g):
                dve.wait_ge(lv_exp, g)
                x5, k5, q5 = lv_ap(xbuf[g % 2], g), lv_ap(pja[:, 2:4, :], g), lv_ap(pja[:, 0:2, :], g)
                m, b = x5.shape[2], LEVELS[g - 1]
                for e in range(2):
                    rows = slice(64 * e, 64 * e + DK)
                    z = zq[g % 2][rows, :, e, 0:m * b].rearrange("p t (m b) -> p t m b", b=b)
                    dve.tensor_tensor(z, x5[rows, :, :, 1, :], q5[rows, :, :, 1, :], ALU.mult).then_inc(lv_x, 1)
                dve.tensor_tensor(x5[:, :, :, 0, :], x5[:, :, :, 0, :], k5[:, :, :, 0, :], ALU.mult).then_inc(lv_x, 1)

            def level_take(g):
                for k, ws in enumerate(lv_steps(g)):
                    n = steps_before(g) + k
                    w, width = ws[0], WIN[ws[0]][1]
                    dve.wait_ge(lv_mm, n + 1)
                    bank = lv_bank(n)
                    if g == 0:
                        src = ps[0:width, bank:bank + 2, 0:2 * width].rearrange("p e (t n) -> p t e n", t=2)
                        sel = ident[0:width, 0:width].unsqueeze(1).unsqueeze(1).broadcast_to([width, 2, 2, width])
                        dve.tensor_tensor(at_win(w), src, sel, ALU.mult).then_inc(at_done, 1)
                    else:
                        b, g4 = LEVELS[g - 1], GLA_HEADS * len(ws)
                        dve.wait_ge(at_done, n)
                        src = ps[0:width, bank, 0:g4 * width // 2].rearrange("p (g m b) -> p g m b", g=g4, b=b)
                        sel = lvm[0:width, g - 1, 0:width].rearrange("p (m a b) -> p m a b", a=2, b=b)[:, :, 1, :]
                        sel = sel.unsqueeze(1).broadcast_to([width, g4, width // (2 * b), b])
                        c = w * GLA_HEADS * P
                        dst = AT[0:width, c:c + g4 * width].rearrange("p (g m a b) -> p g m a b", g=g4, a=2, b=b)
                        dve.copy_predicated(dst[:, :, :, 1, :], sel, src).then_inc(at_done, 1)

            dve.wait_ge(lv_step, 5 * len(LEVELS))
            level_diff(1)
            for g in range(1, NLV):
                level_x(g)
                if g + 1 < NLV:
                    level_diff(g + 1)
                level_take(g - 1)
            level_take(NLV - 1)
            for t in range(2):
                b3 = gb[:, t, 0:FULL_WIN * P].rearrange("p (w n) -> p w n", n=P)
                x3 = xb[:, t, 0:FULL_WIN * P].rearrange("p (w n) -> p w n", n=P)
                dve.tensor_tensor(x3, b3[:, :, P - 1:P].broadcast_to([P, FULL_WIN, P]), b3,
                                  ALU.subtract).then_inc(kd_diff, 1)
            dve.wait_ge(qe_exp, 1)
            dve.tensor_tensor(xa[:, :, :], xa[:, :, :], pja[:, 0:2, :], ALU.mult).then_inc(qe_ready, 1)
            dve.wait_ge(kd_exp, 1)
            for t in range(2):
                dve.tensor_tensor(xb[:, t, 0:FULL_WIN * P], xb[:, t, 0:FULL_WIN * P], pja[:, 2 + t, 0:FULL_WIN * P],
                                  ALU.mult).then_inc(kd_ready, 1)
            dve.memset(S[:, :, :], 0.0).then_inc(s_zero, 1)
            dve.wait_ge(kd_ready, 2)
            for c in range(2):
                dve.wait_ge(kd_turned, c + 1)
                dve.tensor_copy(kdt[:, 2 * c:2 * c + 2, :, :], ps[:, c, :].rearrange(
                    "p (w t n) -> p w t n", w=2, t=2)).then_inc(kd_kept, 1)
            dve.wait_ge(s_zero, 1)
            dve.wait_ge(el_exp, 1)
            for w in range(FULL_WIN):
                dve.wait_ge(s_mm, w + 1)
                if w:
                    dve.wait_ge(s_new, GLA_HEADS * w)
                    dve.wait_ge(o_mm, w + 1)
                for hd in range(GLA_HEADS):
                    t, e = hd // 2, 64 * (hd % 2)
                    new, old = ps[e:e + DK, 2, t * DV:(t + 1) * DV], S[e:e + DK, hd, :]
                    if w == 0:
                        dve.tensor_copy(old, new).then_inc(s_new, 1)
                    else:
                        dve.scalar_tensor_tensor(out=old, in0=old,
                                                 scalar=elast[e:e + DK, 5 * t + w:5 * t + w + 1], in1=new,
                                                 op0=ALU.mult, op1=ALU.add).then_inc(s_new, 1)
            dve.wait_ge(o_sum, 1)
            dve.tensor_scalar(orow, ps[0:n_orow, 2, 0:P], 1.0 / DV, EPS, ALU.mult, ALU.add).then_inc(o_var, 1)
            dve.wait_ge(o_var, 1)
            dve.reciprocal(orow, orow).then_inc(o_inv, 1)
            dve.wait_ge(o_kept, len(WIN))
            for w, (s, width) in enumerate(WIN):
                dve.wait_ge(o_spread, w + 1)
                o = oT[:, :, s:s + width]
                dve.scalar_tensor_tensor(out=o, in0=o, scalar=hn, in1=ps[:, w, 0:GLA_HEADS * width].rearrange(
                    "p (g n) -> p g n", g=GLA_HEADS), op0=ALU.mult, op1=ALU.mult).then_inc(o_normed, 1)
            dve.wait_ge(mask_done, 5)
            with dve.Fori(0, HEADS // 4) as i:
                def masked(n):
                    pair, e, b, s, w = att_step(n)
                    dve.wait_ge(qk_done, at(i, N_ATT, n + 1))
                    dve.wait_ge(exp_done, at(i, N_ATT, n + 1))
                    dve.sem_inc(passed, 1)
                    dve.tensor_tensor_reduce(out=key_view(lg[0:w, n % 2, 0:SEEN[b]], b),
                                             in0=key_psum(b, w, QK_BANK[b]),
                                             in1=key_view(mask[0:w, MASK_AT[b]:MASK_AT[b] + SEEN[b]], b), scale=-HD ** -0.5,
                                             scalar=3.0e38, op0=ALU.add, op1=ALU.min,
                                             accum_out=stat[0:w, 4 + n % 2:5 + n % 2]).then_inc(lg_done, 1)

                def inverse(n):
                    w = att_step(n)[-1]
                    dve.wait_ge(exp_done, at(i, N_ATT, n + 3))
                    dve.wait_ge(diag_done, at(i, N_ATT, n))
                    dve.reciprocal(stat[0:w, 8 + n % 2:9 + n % 2], stat[0:w, 6 + n % 2:7 + n % 2]).then_inc(sum_inv, 1)

                def keep_pt(n):
                    pair, e, b, s, w = att_step(n)
                    dve.wait_ge(pt_done, at(i, N_ATT, n + 3))
                    dve.wait_ge(pv_done, at(i, N_ATT, n))
                    if b == 0:
                        dve.tensor_copy(pt[:, n % 2, 0:w], ps[:, 4 + n % 2, 0:w]).then_inc(pt_kept, 1)
                    else:
                        dve.tensor_copy(pt[:, n % 2, 0:w], ps[:, 4 + n % 2, 0:w]).then_inc(pt_first, 1)
                        dve.tensor_copy(pt[0:100, n % 2, w:(b + 1) * w],
                                        ps[0:100, 4 + n % 2, w:(b + 1) * w]).then_inc(pt_kept, 1)

                def keep_lo(n):
                    pair, e, b, s, w = att_step(n)
                    rows = slice(HD * e, HD * (e + 1))
                    dve.wait_ge(m_hi, at(i, N_ATT, n + 1))
                    dve.tensor_tensor(al[rows, 2 * i + pair, s:s + w], ps[rows, 6 + n % 2, 0:w],
                                      ah[rows, 2 * i + pair, s:s + w].bitcast(F32), ALU.subtract).then_inc(m_lo, 1)

                masked(0)
                masked(1)
                inverse(0)
                for n in range(N_ATT):
                    if n + 1 < N_ATT:
                        inverse(n + 1)
                    if n + 2 < N_ATT:
                        masked(n + 2)
                    keep_pt(n)
                    if n:
                        keep_lo(n - 1)
                keep_lo(N_ATT - 1)
            for d in range(KT):
                bank = 2 * (d % 4)
                dve.wait_ge(w_used, U_OUT + d + RING + 1)
                dve.wait_ge(h_done, H_OUT - KT + d + 1)
                dve.tensor_tensor(halves(h[:, d, :]), ps[:, bank:bank + 2, 0:HALF], halves(h[:, d, :]),
                                  ALU.add).then_inc(h_done, 1)
                prep(2, d, H_OUT + d)
                prep_lo(2, d)

        block = ctx.enter_context(nc.Block())

        @block.sync
        def _(sp):
            def load(u, src, dst_view, i=None):
                slot = u % RING
                sp.wait_ge(w_split, at(i, RING, u + 1))
                sp.dma_start(dst_view(raw[:, slot, :]), src).then_inc(w_in_slot[slot], 16)

            def cols(n=P):
                return lambda s: s.rearrange("p (k n) -> p k n", k=KT)[:, :, 0:n]

            for t in range(4):
                sp.dma_start(xin[:, t, :], x[t * P:(t + 1) * P, :]).then_inc(x_loaded[t], 16)
            sp.dma_start(xin[0:META, 4, :], meta).then_inc(x_loaded[4], 16)
            for n, g in enumerate([ffn1[0], mix_norm, ffn2[0], final_norm]):
                sp.dma_start(vec_rows[KT * n:KT * (n + 1), :], g.rearrange("(k p) -> k p", p=P)).then_inc(const_loaded, 16)
            sp.dma_start(vec_rows[4 * KT:4 * KT + 2, :], b_a.rearrange("(k p) -> k p", p=P)).then_inc(const_loaded, 16)
            sp.dma_start(vec_rows[4 * KT + 2:4 * KT + 3, :], head_norm.rearrange("(k p) -> k p", p=P)).then_inc(const_loaded, 16)

            def ffn_loads(weights, u0):
                _, w_gate, w_up, w_down = weights
                gate_v = w_gate.rearrange("(k p) f -> p k f", p=P)
                up_v = w_up.rearrange("(k p) f -> p k f", p=P)
                down_v = w_down.rearrange("(k p) d -> p k d", p=P)
                u = u0
                for f0, cnt in GROUPS:
                    with sp.Fori(0, cnt // 2) as i:
                        for j in range(2):
                            c = (i * 2 + (f0 + j)) * P
                            load(u + 2 * j, gate_v[:, :, bass.ds(c, P)], cols(), i)
                            load(u + 2 * j + 1, up_v[:, :, bass.ds(c, P)], cols(), i)
                    u += 2 * cnt
                    with sp.Fori(0, KT // RING) as i:
                        for j in range(RING):
                            c = (i * RING + j) * P
                            load(u + j, down_v[:, f0:f0 + cnt, bass.ds(c, P)],
                                 lambda s: s.rearrange("p (k n) -> p k n", k=KT)[:, 0:cnt, :], i)
                    u += KT

            ffn_loads(ffn1, U_FFN1)
            win_v = w_in.rearrange("(k p) n -> p k n", p=P)

            def load_mix(m):
                u = U_MIX + m
                if m < M_IKW:
                    load(u, win_v[:, :, C_IQ + m * P:C_IQ + (m + 1) * P], cols())
                elif m == M_IKW:
                    load(u, win_v[:, :, C_IK:C_IK + N_IKW], cols(N_IKW))
                elif m == M_GA:
                    load(u, win_v[:, :, C_GA:C_GA + N_GA], cols(N_GA))
                elif M_RAW <= m < M_DV:
                    r = m - M_RAW
                    c = (C_GQK + r * P if r < R_Q else C_DQK + (r - R_Q) * P if r < R_GR
                         else C_GR + (r - R_GR) * P)
                    load(u, win_v[:, :, c:c + P], cols())
                else:
                    c, q = (C_GV, m - M_GV) if m < M_RAW else (C_DV, m - M_DV)
                    load(u, win_v[:, 2 * q:2 * q + 2, c:c + 512], lambda s: s.rearrange("p (k n) -> p k n", k=2))

            def swap(n, tile, dst, rows=P):
                for a in range(0, rows, 32):
                    b = a ^ 32
                    sp.dma_start(dst[a:a + 32, :], tile[b:b + 32, :]).then_inc(swapped[n], 16)

            for m in range(4):
                load_mix(m)
            sp.wait_ge(h_done, H_OUT)
            for dst, src in ((cosr, cos_t), (sinr, sin_t)):
                sp.dma_start(dst[:, :], src).then_inc(mix_loaded, 16)
            sp.dma_start(wa2[:, :, :], w_a2.rearrange("k (t n) -> k t n", n=P)).then_inc(mix_loaded, 16)
            load_mix(4)
            load_mix(5)
            for m in range(5):
                sp.wait_ge(pj_kept, m + 1)
                if m < 4:
                    swap(m, iq[:, m, :], sw[:, m, :])
                else:
                    sp.wait_ge(rope_done, 1)
                    swap(m, ik[:, :], sw[:, 0, :], HD)
                load_mix(6 + m)
            sp.wait_ge(rope_done, 5)
            sp.dma_start(ikz[1][HD:2 * HD, :], ik[0:HD, :]).then_inc(ik_copied, 16)
            for m in range(11, MIX_UNITS):
                load_mix(m)
                r = m - M_RAW - 5
                if R_Q <= r < R_GR:
                    swap_r(sp, swap, r)
            out_v = w_out.rearrange("(k p) d -> p k d", p=P)
            with sp.Fori(0, KT // RING) as i:
                for j in range(RING):
                    load(U_OUT + j, out_v[:, :, bass.ds((i * RING + j) * P, P)], cols(), i)
            ffn_loads(ffn2, U_FFN2)
            for t in range(SEQ // P):
                sp.wait_ge(y_kept, t + 1)
                sp.wait_ge(y_kept_act, t + 1)
                sp.dma_start(out[t * P:(t + 1) * P, :], xin[:, t, :]).then_inc(stored, 16)
            sp.wait_ge(stored, 16 * (SEQ // P))

        @block.gpsimd
        def _(pool):
            pool.sem_inc(w_split, RING)
            for e in range(2):
                pool.memset(ikz[e][64 * (1 - e):64 * (1 - e) + HD, :], 0.0).then_inc(ik_zero, 1)
                pool.wait_ge(ik_zero, e + 1)
            pool.memset(ident[:, :], 0.0).then_inc(c_zero, 1)
            pool.memset(ones[:, :], 1.0).then_inc(consts, 1)
            pool.memset(pick[:, :], 0.0).then_inc(picked, 1)
            pool.wait_ge(picked, 1)
            pool.memset(pick[:, n_orow - 1:n_orow], 1.0).then_inc(picked, 1)
            pool.wait_ge(c_zero, 1)
            pool.affine_select(out=ident[:, :], in_=ident[:, :], compare_op=ALU.not_equal, fill=1.0, base=0,
                               pattern=[[-1, P]], channel_multiplier=1).then_inc(consts, 1)

            def lo(u, i=None):
                slot = u % RING
                pool.wait_ge(w_hi, at(i, RING, u + 1))
                pool.tensor_tensor(wl[:, slot, :], raw[:, slot, :], wh[:, slot, :].bitcast(F32),
                                   ALU.subtract).then_inc(w_split, 1)

            def run(u0, n):
                if n >= RING:
                    with pool.Fori(0, n // RING) as i:
                        for j in range(RING):
                            lo(u0 + j, i)
                for j in range(n - n % RING, n):
                    lo(u0 + j)

            run(0, U_MIX)
            run(U_MIX, 6)
            pool.wait_ge(h_done, H_OUT)
            pool.memset(tri[:, :], 0.0).then_inc(c_zero, 1)
            pool.wait_ge(c_zero, 2)
            pool.affine_select(out=tri[:, :], in_=tri[:, :], compare_op=ALU.is_ge, fill=NEG, base=0,
                               pattern=[[-1, P]], channel_multiplier=1).then_inc(consts, 1)
            run(U_MIX + 6, M_RAW - 6)
            steps = 0
            for n, s in enumerate(LEVELS):
                scratch = xb[:, 0, 0:P]
                blk = scratch.rearrange("p (m a b) -> p m a b", a=2, b=s)
                if n:
                    pool.wait_ge(lv_step, steps)
                pool.memset(scratch, 0.0).then_inc(lv_step, 1)
                steps += 1
                pool.wait_ge(lv_step, steps)
                pool.memset(blk[:, :, 1, :], 1.0).then_inc(lv_step, 1)
                steps += 1
                pool.wait_ge(lv_step, steps)
                pool.affine_select(out=blk[:, :, 1, :], in_=blk[:, :, 1, :], compare_op=ALU.is_ge, fill=0.0,
                                   base=0, pattern=[[-2 * s, P // (2 * s)], [0, s]],
                                   channel_multiplier=1).then_inc(lv_step, 1)
                steps += 1
                pool.wait_ge(lv_step, steps)
                pool.affine_select(out=blk[:, :, 1, :], in_=blk[:, :, 1, :], compare_op=ALU.is_ge, fill=0.0,
                                   base=s - 1, pattern=[[2 * s, P // (2 * s)], [0, s]],
                                   channel_multiplier=-1).then_inc(lv_step, 1)
                steps += 1
                pool.wait_ge(lv_step, steps)
                pool.tensor_copy(lvm[:, n, :], scratch).then_inc(lv_step, 1)
                steps += 1
            run(U_MIX + M_RAW, 8)
            for n in range(8):
                lo(U_MIX + M_RAW + 8 + n)
                pool.wait_ge(swapped[5 + n], 64)
                s = sw[:, n % 4, :]
                pool.tensor_tensor(s, s, sinr[:, :], ALU.mult).then_inc(q_sin, 1)
                pool.tensor_tensor(pjb[:, n, :], pjb[:, n, :], cosr[:, :], ALU.mult).then_inc(q_cos, 1)
                pool.wait_ge(q_sin, n + 1)
                pool.wait_ge(q_cos, n + 1)
                pool.tensor_tensor(pjb[:, n, :], pjb[:, n, :], s, ALU.add).then_inc(q_roped, 1)
            for q in range(4):
                lo(U_MIX + M_DV + q)
            pool.wait_ge(pj_kept, 5 + 16)
            for t in range(4):
                pool.tensor_tensor(pja[:, 4 + t, :], pja[:, 4 + t, :], rstd[:, :], ALU.mult).then_inc(gr_scaled, 1)
            pool.wait_ge(q_roped, 8)
            pool.wait_ge(w_split, U_OUT + RING)
            pool.wait_ge(gr_scaled, 4)
            pool.wait_ge(lv_mm, len(STEPS))
            pool.wait_ge(kd_diff, 2)
            pool.wait_ge(el_exp, 1)
            pool.wait_ge(qe_exp, 1)
            for n, (pair, e) in enumerate(((0, 0), (0, 1), (1, 0), (1, 1))):
                pool.memset(kst[pair][e][64 * (1 - e):64 * (1 - e) + HD, :], 0.0).then_inc(kst_zero, 1)
                pool.wait_ge(kst_zero, n + 1)
            lo(U_OUT)
            lo(U_OUT + 1)
            pool.wait_ge(w_split, U_OUT + 2 + RING)

            def stage(p):
                k = p % 2
                if p >= 2:
                    pool.wait_ge(qk_done, 10 * (p - 1))
                pool.tensor_copy(qst[k][:, :], pjb[:, p, :]).then_inc(staged, 1)
                for e in range(2):
                    rows = slice(HD * e, HD * (e + 1))
                    pool.wait_ge(staged, 5 * p + 1 + e)
                    pool.tensor_copy(kst[k][e][rows, :], pjb[rows, p + 4, :]).then_inc(staged, 1)
                if p >= 2:
                    pool.wait_ge(pv_done, 10 * (p - 1))
                else:
                    pool.wait_ge(v_kept, 10)
                if p == 1:
                    pool.wait_ge(o_normed, len(WIN))
                pool.wait_ge(staged, 5 * p + 3)
                pool.tensor_copy(vst[k][:, 0, :], dv[:, 0, p * P:(p + 1) * P]).then_inc(staged, 1)
                pool.wait_ge(staged, 5 * p + 4)
                pool.tensor_copy(vst[k][0:100, 1:5, :], dv[0:100, 1:5, p * P:(p + 1) * P]).then_inc(staged, 1)
                pool.wait_ge(staged, 5 * p + 5)

            stage(0)
            stage(1)
            pool.wait_ge(o_normed, len(WIN))
            pool.wait_ge(gr_silu, 1)
            for hd in range(GLA_HEADS):
                pool.tensor_tensor(oT[:, hd, :], oT[:, hd, :], pja[:, 4 + hd, :], ALU.mult).then_inc(o_out, 1)
            for hd in range(GLA_HEADS):
                pool.wait_ge(o_out, hd + 1)
                pool.tensor_copy(ah[:, 4 + hd, :], oT[:, hd, :]).then_inc(g_hi, 1)
            for hd in range(GLA_HEADS):
                pool.wait_ge(g_hi, hd + 1)
                pool.tensor_tensor(al[:, 4 + hd, :], oT[:, hd, :], ah[:, 4 + hd, :].bitcast(F32),
                                   ALU.subtract).then_inc(g_lo, 1)
            pool.wait_ge(g_lo, GLA_HEADS)
            stage(2)
            stage(3)
            run(U_OUT + 2, U_END - U_OUT - 2)

        @block.scalar
        def _(act):
            def hi(u, i=None):
                slot = u % RING
                if i is None and u >= U_END:
                    return
                act.wait_ge(w_in_slot[slot], at(i, 16, 16 * (u // RING + 1)))
                act.wait_ge(w_used, at(i, RING, u + 1))
                act.activation(wh[:, slot, :], raw[:, slot, :], ACT.Copy).then_inc(w_hi, 1)

            act.sem_inc(exp_done, 2)

            def prep_hi(norm, d, h_count):
                act.wait_ge(h_done, h_count + 1)
                act.activation(xh[:, d, :], h[:, d, :], ACT.Copy, scale=gains[:, norm, d:d + 1]).then_inc(x_hi, 1)

            def root(norm):
                act.wait_ge(inv_done, norm + 1)
                act.activation(rstd[:, :], rstd[:, :], ACT.Sqrt).then_inc(rstd_done, 1)

            def ffn(u0, number, norm):
                u = u0
                hd = H_FFN[number]
                ft = number * FT
                for f0, cnt in GROUPS:
                    def body(i, b):
                        for j in range(2):
                            hi(u + 4 * b + 2 * j + 2, i)
                            hi(u + 4 * b + 2 * j + 3, i)
                            if i is None and j == 0:
                                root(norm)
                            act.wait_ge(gate_scaled, at(i, 2, ft + f0 + 2 * b + j + 1))
                            act.activation(t0[:, :], t0[:, :], ACT.Silu).then_inc(silu_done, 1)

                    first = 1 if f0 == 0 else 0
                    if first:
                        body(None, 0)
                    else:
                        act.activation(scrap[:, :], scrap[:, :], ACT.Silu).then_inc(scrap_done, 1)
                        scrap_n[0] += 1
                        act.wait_ge(scrap_done, scrap_n[0])
                    with act.Fori(0, cnt // 2 - first) as i:
                        body(i, first)
                    u += 2 * cnt
                    last = f0 == GROUPS[-1][0]
                    for d in range(KT):
                        hi(u + d + 2)
                        if last and number == 0:
                            prep_hi(1, d, hd + d)
                        elif last:
                            act.wait_ge(sq_done, 3 * KT + d + 1)
                            act.activation(h[:, d, :], h[:, d, :], ACT.Copy,
                                           scale=gains[:, 3, d:d + 1]).then_inc(y_done, 1)
                    u += KT
                    hd += KT

            scrap_n = [1]
            act.wait_ge(scrap_done, 1)

            act.wait_ge(vecs_kept, 1)
            for n in range(10):
                if n % 2 == 1:
                    keep_x(act, n)
            hi(0)
            for d in range(KT):
                prep_hi(0, d, d)
                if d == 3:
                    hi(1)
            for d in range(KT):
                if d >= 2:
                    act.wait_ge(ss_done, d - 1)
                act.activation(t01[:, 1 - d % 2, :], h[:, d, :], ACT.Square).then_inc(sq0_done, 1)
            ffn(U_FFN1, 0, 0)
            act_mixer(act, hi, prep_hi, root)
            ffn(U_FFN2, 1, 2)
            act.wait_ge(inv_done, 4)
            act.activation(rout, rout, ACT.Sqrt).then_inc(rstd_done, 1)
            keep_y(act, 1)

        @block.vector
        def _(dve):
            dve.memset(scrap[:, :], 0.0).then_inc(scrap_done, 1)
            for free in (up_scaled, lg_done, pt_kept, m_lo):
                dve.sem_inc(free, 2)
            dve.sem_inc(top_taken, 2)
            for start in (a_prod, a_lo):
                dve.sem_inc(start, ONE)

            def prep(norm, d, h_count):
                n = norm * KT + d
                if d == 0:
                    if norm:
                        dve.wait_ge(var_done, norm)
                    dve.memset(ss[:, :], 0.0).then_inc(ss_zero, 1)
                dve.wait_ge(h_done, h_count + 1)
                if n:
                    dve.wait_ge(ss_done, n)
                dve.tensor_tensor(t1[:, :], h[:, d, :], h[:, d, :], ALU.mult).then_inc(sq_done, 1)
                dve.wait_ge(sq_done, n + 1)
                dve.wait_ge(ss_zero, norm + 1)
                dve.tensor_tensor(ss[:, :], ss[:, :], t1[:, :], ALU.add).then_inc(ss_done, 1)

            def prep_lo(norm, d):
                n = norm * KT + d
                dve.wait_ge(x_hi, n + 1)
                dve.scalar_tensor_tensor(out=xl[:, d, :], in0=h[:, d, :], scalar=gains[:, norm, d:d + 1],
                                         in1=xh[:, d, :].bitcast(F32), op0=ALU.mult,
                                         op1=ALU.subtract).then_inc(x_lo, 1)

            def invert(norm):
                dve.wait_ge(norm_sum, norm + 1)
                dve.tensor_scalar(halves(rstd[:, :]), ps[:, 6:8, 0:HALF], 1.0 / D, EPS, ALU.mult,
                                  ALU.add).then_inc(var_done, 1)
                dve.wait_ge(var_done, norm + 1)
                dve.reciprocal(rstd[:, :], rstd[:, :]).then_inc(inv_done, 1)

            def ffn(u0, number, norm):
                u = u0
                hd = H_FFN[number]
                ft = number * FT
                dve.wait_ge(rstd_done, norm + 1)
                for f0, cnt in GROUPS:
                    with dve.Fori(0, cnt // 2) as i:
                        for j in range(2):
                            F = ft + f0 + j
                            bank = 4 * j
                            dve.wait_ge(w_used, at(i, 4, u + 2 * j + RING + 1))
                            dve.wait_ge(a_prod, ONE + at(i, 2, F))
                            dve.tensor_tensor(halves(t0[:, :]), ps[:, bank:bank + 2, 0:HALF], halves(rstd[:, :]),
                                              ALU.mult).then_inc(gate_scaled, 1)
                            dve.wait_ge(w_used, at(i, 4, u + 2 * j + 1 + RING + 1))
                            dve.wait_ge(a_lo, ONE + at(i, 2, F))
                            dve.tensor_tensor(halves(t1[:, :]), ps[:, bank + 2:bank + 4, 0:HALF],
                                              halves(rstd[:, :]), ALU.mult).then_inc(up_scaled, 1)
                            dve.wait_ge(silu_done, at(i, 2, F + 1))
                            dve.wait_ge(up_scaled, at(i, 2, F + 3))
                            dve.tensor_tensor(t1[:, :], t0[:, :], t1[:, :], ALU.mult).then_inc(a_prod, 1)
                            dve.wait_ge(a_prod, ONE + at(i, 2, F + 1))
                            dve.tensor_copy(ah[:, i * 2 + j, :], t1[:, :]).then_inc(a_hi, 1)
                            dve.wait_ge(a_hi, at(i, 2, F + 1))
                            dve.tensor_tensor(al[:, i * 2 + j, :], t1[:, :], ah[:, i * 2 + j, :].bitcast(F32),
                                              ALU.subtract).then_inc(a_lo, 1)
                    u += 2 * cnt
                    last = f0 == GROUPS[-1][0]
                    for d in range(KT):
                        bank = 2 * (d % 4)
                        dve.wait_ge(w_used, u + d + RING + 1)
                        dve.wait_ge(h_done, hd - KT + d + 1)
                        dve.scalar_tensor_tensor(out=halves(h[:, d, :]), in0=ps[:, bank:bank + 2, 0:HALF], scalar=0.5,
                                                 in1=halves(h[:, d, :]), op0=ALU.mult, op1=ALU.add).then_inc(h_done, 1)
                        if last:
                            prep(norm + 1, d, hd + d)
                            if number == 0:
                                prep_lo(norm + 1, d)
                    u += KT
                    hd += KT

            dve.wait_ge(vecs_turned, 1)
            dve.tensor_copy(vecs[:, :], ps[:, 7, 0:4 * KT + 3]).then_inc(vecs_kept, 1)
            for n in range(0, 10, 2):
                keep_x(dve, n)
            dve.wait_ge(x_kept, 5)
            dve.wait_ge(x_kept_act, 5)
            dve.sem_inc(h_done, KT)
            dve.wait_ge(vecs_kept, 1)
            dve.memset(ss[:, :], 0.0).then_inc(ss_zero, 1)
            for d in range(KT):
                prep_lo(0, d)
            for d in range(KT):
                dve.wait_ge(sq0_done, d + 1)
                dve.wait_ge(ss_zero, 1)
                if d:
                    dve.wait_ge(ss_done, d)
                dve.tensor_tensor(ss[:, :], ss[:, :], t01[:, 1 - d % 2, :], ALU.add).then_inc(ss_done, 1)
            dve.sem_inc(sq_done, KT)
            invert(0)
            ffn(U_FFN1, 0, 0)
            invert(1)
            dve_mixer(dve, prep, prep_lo)
            invert(2)
            ffn(U_FFN2, 1, 2)
            dve.wait_ge(norm_sum, 4)
            dve.tensor_scalar(rout, ps[:, 7, 0:4], 1.0 / D, EPS, ALU.mult, ALU.add).then_inc(var_done, 1)
            dve.wait_ge(var_done, 4)
            dve.reciprocal(rout, rout).then_inc(inv_done, 1)
            keep_y(dve, 0)

        @block.tensor
        def _(pe):
            pe.sem_inc(w_used, RING)
            pe.sem_inc(pt_done, 2)

            def product(u, bank, m, rh, rl, kts, i=None, before_k=None, tiles=range(KT)):
                slot = u % RING
                pe.wait_ge(w_split, at(i, RING, u + RING + 1))
                for k in range(kts):
                    if before_k:
                        before_k(k)
                    for n, (w, r) in enumerate(((wh, rh), (wh, rl), (wl, rh))):
                        for a in range(2):
                            mm = pe.matmul(ps[0:m, bank + a, 0:HALF], w[:, slot, k * P:k * P + m],
                                           r[:, tiles[k], a * HALF:(a + 1) * HALF], start=(k == 0 and n == 0),
                                           stop=(k == kts - 1 and n == 2))
                mm.then_inc(w_used, 1)

            def norm_product(norm):
                pe.wait_ge(ss_done, KT * (norm + 1))
                for a in range(2):
                    mm = pe.matmul(ps[:, 6 + a, 0:HALF], ones[:, :], ss[:, a * HALF:(a + 1) * HALF], start=True,
                                   stop=True)
                mm.then_inc(norm_sum, 1)

            def ffn(u0, number, norm):
                u = u0
                hd = H_FFN[number]
                ft = number * FT
                for f0, cnt in GROUPS:
                    def x_ready(k):
                        pe.wait_ge(x_lo, KT * norm + k + 1)

                    def body(i, b):
                        for j in range(2):
                            pe.wait_ge(h_done, hd - 2 + 2 * j)
                            pe.wait_ge(up_scaled, at(i, 2, ft + f0 + 2 * b + j + 1))
                            product(u + 4 * b + 2 * j, 4 * j, P, xh, xl, KT, i, x_ready if j == 0 else None)
                            if i is None and j == 0:
                                norm_product(norm)
                            if i is None and j == 1:
                                pe.wait_ge(var_done, norm + 1)
                            product(u + 4 * b + 2 * j + 1, 4 * j + 2, P, xh, xl, KT, i)

                    first = 1 if f0 == 0 else 0
                    if first:
                        body(None, 0)
                    with pe.Fori(0, cnt // 2 - first) as i:
                        body(i, first)
                    u += 2 * cnt
                    F = ft + f0

                    def a_ready(k):
                        pe.wait_ge(a_lo, ONE + F + k + 1)

                    with pe.Fori(0, KT // 4) as i:
                        for j in range(4):
                            pe.wait_ge(up_scaled, F + cnt + (1 if j == 0 else 2))
                            pe.wait_ge(h_done, at(i, 4, hd + j - 3))
                            product(u + j, 2 * j, P, ah, al, cnt, i, a_ready if j == 0 else None)
                    u += KT
                    hd += KT

            pe.wait_ge(consts, 2)
            pe.wait_ge(const_loaded, 96)
            pe.transpose(ps[:, 7, 0:4 * KT + 3], vec_rows[:, :], ident[0:4 * KT + 3, 0:4 * KT + 3]).then_inc(vecs_turned, 1)
            pe.wait_ge(vecs_kept, 1)
            for n in range(10):
                t, half = n // 2, n % 2
                w = x_cols(n)[1]
                pe.wait_ge(x_loaded[t], 16)
                if n >= 8:
                    pe.wait_ge(x_kept, 5 - 4 if n == 8 else 1)
                    pe.wait_ge(x_kept_act, 1)
                for k in range(4):
                    c = (4 * half + k) * P
                    mm = pe.transpose(ps[:, n % 8, k * w:(k + 1) * w], xin[0:w, t, c:c + P], ident[0:w, 0:w])
                mm.then_inc(x_turned, 1)
            ffn(U_FFN1, 0, 0)
            pe_mixer(pe, product, norm_product)
            ffn(U_FFN2, 1, 2)
            pe.wait_ge(h_done, H_END - 2)
            for n in range(8):
                half, t = divmod(n, 4)
                tokens = slice(META + t * P, META + (t + 1) * P)
                if n == 4:
                    pe.wait_ge(ss_done, 4 * KT)
                    for c in range(4):
                        mm = pe.matmul(ps[:, 7, c:c + 1], ss[:, META + c * P:META + (c + 1) * P], ones[:, 0:1],
                                       start=True, stop=True)
                    mm.then_inc(norm_sum, 1)
                if n == 7:
                    pe.wait_ge(var_done, 4)
                pe.wait_ge(y_done, 4 * (half + 1))
                for k in range(4):
                    mm = pe.transpose(ps[:, n, k * P:(k + 1) * P], h[:, 4 * half + k, tokens], ident[:, :])
                mm.then_inc(y_turned, 1)


INPUTS = ["x", "meta_tokens", "ffn1_norm", "ffn1_w_gate", "ffn1_w_up", "ffn1_w_down", "mix_norm", "w_in", "gla_w_a2",
          "gla_b_a", "gla_head_norm", "w_out", "ffn2_norm", "ffn2_w_gate", "ffn2_w_up", "ffn2_w_down", "final_norm"]


def rope_tables():
    import numpy as np
    f32 = np.float32
    inv = (f32(1.0) / (f32(10000.0) ** (np.arange(0, HD, 2, dtype=f32) / f32(HD)))).astype(f32)
    ang = (inv[:, None] * np.arange(TOK, dtype=f32)[None, :]).astype(f32)
    cos, sin = np.cos(ang).astype(f32), np.sin(ang).astype(f32)
    return np.concatenate([cos] * 4), np.concatenate([-sin, sin] * 2)


def kernel(**inputs):
    import numpy as np
    import concourse.bacc as bacc
    from concourse.bass_utils import run_bass_kernel_spmd as run

    nc = bacc.Bacc("TRN2", target_bir_lowering=False, num_devices=1)
    arrays, a = {}, {}
    given = {n: np.ascontiguousarray(inputs[n]) for n in INPUTS}
    given["cos_t"], given["sin_t"] = rope_tables()
    for name, v in given.items():
        if name != "meta_tokens" and v.ndim > 1 and v.shape[0] == 1:
            v = v[0]
        arrays[f"in_{name}"] = np.ascontiguousarray(v)
        a[name] = nc.dram_tensor(f"in_{name}", v.shape, F32, kind="ExternalInput").ap()
    out = nc.dram_tensor("out_0", (SEQ, D), F32, kind="ExternalOutput").ap()
    build(nc, a["x"], a["meta_tokens"],
          (a["ffn1_norm"], a["ffn1_w_gate"], a["ffn1_w_up"], a["ffn1_w_down"]),
          (a["ffn2_norm"], a["ffn2_w_gate"], a["ffn2_w_up"], a["ffn2_w_down"]),
          a["mix_norm"], a["w_in"], a["gla_w_a2"], a["gla_b_a"], a["gla_head_norm"], a["w_out"], a["final_norm"],
          a["cos_t"], a["sin_t"], out)
    r = run(nc, [arrays], core_ids=[0])
    return r.results[0]["out_0"].reshape(1, SEQ, D)
```

```python
import math
from contextlib import ExitStack

import concourse.bass as bass
from concourse import mybir

F32 = mybir.dt.float32
F32R = mybir.dt.float32r
U8 = mybir.dt.uint8
ALU = mybir.AluOpType
ACT = mybir.ActivationFunctionType
AX_X = mybir.AxisListType.X

P = 128
D = 1024
KT = D // P
META, SEQ = 16, 512
TOK = META + SEQ
HALF = TOK // 2
D_FF = 2816
FT = D_FF // P
EPS = 1e-6
GLA_HEADS, DK, DV = 4, 64, 128
HD = 64
HEADS = 8
TOPK = min(256, SEQ // 4)
GATE_NORM = 16.0
RING = 4
UNIT = KT * P
ONE = 1
NEG = -1.0e30
TAKEN = -3.0e38

GROUPS = [(0, 8), (8, 8), (16, FT - 16)]
FFN_UNITS = 2 * FT + KT * len(GROUPS)

C_GQK, C_GV, C_GR, C_GA, C_DQK, C_DV, C_IQ, C_IK = 0, 512, 1024, 1536, 1552, 2576, 3088, 3600
N_GA, N_IKW, G_COL = 16, HD + HEADS, 96

M_IQ, M_IKW, M_GV, M_RAW, M_DV, MIX_UNITS = 0, 4, 5, 9, 25, 29
R_Q, R_GR = 4, 12
U_FFN1 = 0
U_MIX = U_FFN1 + FFN_UNITS
U_OUT = U_MIX + MIX_UNITS
U_FFN2 = U_OUT + KT
U_END = U_FFN2 + FFN_UNITS

BLK = [(0, TOPK)] + [(TOPK + 100 * i, 100) for i in range((TOK - TOPK) // 100)]
SEEN = [s + n for s, n in BLK]
MASK_AT = [sum(SEEN[:b]) for b in range(len(BLK))]
WIN = [(w, min(P, TOK - w)) for w in range(0, TOK, P)]
FULL_WIN = TOK // P
LEVELS = [1, 2, 4, 8, 16, 32, 64]
NLV = len(LEVELS) + 1
R_LEVEL = 16 - NLV
ROUNDS_LEVEL = {0: 4, 2: 2, 4: 2, 6: 2}
ROUNDS_WIN = {0: 2, 1: 2, 2: 2}
RC_WIN = [0, 1, 2, 3, 9]
RC_BLK = [4, 5, 6, 7, 8]


def at(i, step, base):
    return base if i is None else i * step + base


def halves(ap):
    return ap.rearrange("p (a n) -> p a n", a=2)


def tokens_of(norm):
    return slice(0, TOK) if norm < 2 else slice(META, TOK)


def parts_of(norm):
    return [(0, 0, HALF), (1, HALF, HALF)] if norm < 2 else [(0, META, SEQ)]


def as_parts(ap, norm):
    return halves(ap) if norm < 2 else ap


def build(nc, x, meta, ffn1, ffn2, mix_norm, w_in, w_a2, b_a, head_norm, w_out, final_norm,
          cos_t, sin_t, out):
    ctx = ExitStack()
    with ctx:
        def sb(name, shape, dt=F32, scope=ctx):
            return scope.enter_context(nc.sbuf_tensor(name, shape, dt))

        def sem(name):
            return ctx.enter_context(nc.semaphore(name))

        ps = ctx.enter_context(nc.psum_tensor("ps", [P, 8, 512], F32))
        h = sb("h", [P, KT, TOK])
        xh = sb("xh", [P, KT, TOK], F32R)
        xl = sb("xl", [P, KT, TOK], F32R)
        raw = sb("raw", [P, RING, UNIT])
        wh = sb("wh", [P, RING, UNIT], F32R)
        wl = sb("wl", [P, RING, UNIT], F32R)
        rstd = sb("rstd", [P, TOK])
        ss = sb("ss", [P, TOK])
        t01 = sb("t01", [P, 2, TOK])
        t0, t1 = t01[:, 0, :], t01[:, 1, :]
        ident = sb("ident", [P, P])
        ones = sb("ones", [P, P])
        vec_rows = sb("vec_rows", [4 * KT + 3, P])
        vecs = sb("vecs", [P, 4 * KT + 3])
        gains = vecs[:, 0:4 * KT].rearrange("p (n k) -> p n k", k=KT)
        ba = vecs[:, 4 * KT:4 * KT + 2]
        hn = vecs[:, 4 * KT + 2:4 * KT + 3]
        scrap = sb("scrap", [P, 1])
        n_orow = len(WIN) * GLA_HEADS
        pick = sb("pick", [P, 2 * n_orow - 1])
        ffn_scope = ExitStack()
        ah = sb("ah", [P, KT, TOK], F32R, ffn_scope)
        al = sb("al", [P, KT, TOK], F32R, ffn_scope)
        xin = sb("xin", [P, 5, D], F32, ffn_scope)
        ffn_scope.close()
        pja = sb("pja", [P, 8, TOK])
        iq = sb("iq", [P, 4, TOK])
        sw = sb("sw", [P, 4, TOK])
        pjb = sb("pjb", [P, 8, TOK])
        dv = sb("dv", [P, 5, 512])
        mask = sb("mask", [P, sum(SEEN)])
        cosr = sb("cosr", [P, TOK])
        sinr = sb("sinr", [P, TOK])
        ikga = sb("ikga", [P, 2, TOK])
        ik, ga = ikga[:, 0, :], ikga[:, 1, :]
        gb = sb("gb", [P, 2, TOK])
        tri = sb("tri", [P, P])
        lvm = sb("lvm", [P, len(LEVELS), P], U8)
        S = t1[:, 0:GLA_HEADS * DV].rearrange("p (g n) -> p g n", g=GLA_HEADS)
        small = sb("small", [P, 112])
        rcol = small[:, 0:10]
        iwt = small[:, 16:48]
        orow = t0[0:len(WIN) * GLA_HEADS, 0:P]
        rout = small[:, 76:80]
        top8 = [small[:, 96:104], small[:, 104:112]]
        elast = small[:, 56:66]
        wa2 = sb("wa2", [N_GA, 2, P])
        iqs, iq_lo = ah, al[:, 0:4, :]
        index_scope = ExitStack()
        iks = sb("iks", [P, 2, TOK], F32R, index_scope)
        index_scope.close()
        gla_scope = ExitStack()
        xa = sb("xa", [P, 2, TOK], F32, gla_scope)
        xb = sb("xb", [P, 2, TOK], F32, gla_scope)
        gv = sb("gv", [P, 5, 512], F32, gla_scope)
        gla_scope.close()
        lg = sb("lg", [P, 2, TOK])
        pr = sb("pr", [P, 2, TOK])
        pt = sb("pt", [P, 2, 512])
        vst0 = sb("vst0", [P, 5, P])
        dg = sb("dg", [P, 2, P])
        qst = [ik, cosr]
        kst = [[gb[:, 0, :], gb[:, 1, :]], [sinr, ga]]
        vst = [vst0, t01[:, :, :].rearrange("p a n -> p (a n)")[:, 0:5 * P].rearrange("p (c n) -> p c n", c=5)]
        stat = small[:, 66:76]
        AT = iq[:, :, :].rearrange("p a n -> p (a n)")
        oT = sw

        def at_win(w):
            width = WIN[w][1]
            base = w * GLA_HEADS * P
            return AT[0:width, base:base + GLA_HEADS * width].rearrange("p (t e n) -> p t e n", t=2, e=2)

        w_in_slot = [sem(f"w_in_slot{i}") for i in range(RING)]
        w_hi = sem("w_hi")
        w_split = sem("w_split")
        w_used = sem("w_used")
        x_loaded = [sem(f"x_loaded{t}") for t in range(5)]
        const_loaded, mix_loaded = sem("const_loaded"), sem("mix_loaded")
        vecs_turned, vecs_kept = sem("vecs_turned"), sem("vecs_kept")
        c_zero, consts, lv_step = sem("c_zero"), sem("consts"), sem("lv_step")
        x_turned, x_kept = sem("x_turned"), sem("x_kept")
        h_done, sq_done, ss_zero, ss_done = sem("h_done"), sem("sq_done"), sem("ss_zero"), sem("ss_done")
        x_hi, x_lo = sem("x_hi"), sem("x_lo")
        norm_sum, var_done, inv_done, rstd_done = sem("norm_sum"), sem("var_done"), sem("inv_done"), sem("rstd_done")
        gate_scaled, up_scaled, silu_done = sem("gate_scaled"), sem("up_scaled"), sem("silu_done")
        a_prod, a_hi, a_lo = sem("a_prod"), sem("a_hi"), sem("a_lo")
        ikw_loaded = sem("ikw_loaded")
        tables_done, pj_kept = sem("tables_done"), sem("pj_kept")
        iw_scaled, ga_scaled = sem("iw_scaled"), sem("ga_scaled")
        swapped = [sem(f"swapped{i}") for i in range(13)]
        rope_sin, rope_cos, rope_done = sem("rope_sin"), sem("rope_cos"), sem("rope_done")
        kst_zero = sem("kst_zero")
        iq_his, iq_los, iqs_stacked = sem("iq_his"), sem("iq_los"), sem("iqs_stacked")
        ik_his, ik_los, iks_stacked = sem("ik_his"), sem("ik_los"), sem("iks_stacked")
        v_kept_dve = sem("v_kept_dve")
        tok_turned, tok_kept, v_kept = sem("tok_turned"), sem("tok_kept"), sem("v_kept")
        idx_done, relu_done, acc_done = sem("idx_done"), sem("relu_done"), sem("acc_done")
        top_found, top_taken, mask_done = sem("top_found"), sem("top_taken"), sem("mask_done")
        q_sin, q_cos, q_roped = sem("q_sin"), sem("q_cos"), sem("q_roped")
        z_done, gate_y, gate_abs, gate_exp, gate_ln, gate_g, gate_cum = (
            sem("z_done"), sem("gate_y"), sem("gate_abs"), sem("gate_exp"), sem("gate_ln"), sem("gate_g"),
            sem("gate_cum"))
        zq_zero, picked = sem("zq_zero"), sem("picked")
        gqk_scaled, lv_diff, lv_exp, lv_x, lv_mm, at_done = (
            sem("gqk_scaled"), sem("lv_diff"), sem("lv_exp"), sem("lv_x"), sem("lv_mm"), sem("at_done"))
        kd_turned, kd_kept, s_mm, s_new, o_mm, o_kept = (
            sem("kd_turned"), sem("kd_kept"), sem("s_mm"), sem("s_new"), sem("o_mm"), sem("o_kept"))
        o_sq, o_sum, o_var, o_inv, o_rstd, gr_scaled, gr_silu, o_spread, m_hi, m_lo = (
            sem("o_sq"), sem("o_sum"), sem("o_var"), sem("o_inv"), sem("o_rstd"), sem("gr_scaled"),
            sem("gr_silu"), sem("o_spread"), sem("m_hi"), sem("m_lo"))
        diag_done = sem("diag_done")
        staged, qk_done, lg_done, exp_done, sum_inv, pt_done, pt_kept, pv_done = (
            sem("staged"), sem("qk_done"), sem("lg_done"), sem("exp_done"), sem("sum_inv"),
            sem("pt_done"), sem("pt_kept"), sem("pv_done"))
        kd_ready, qe_ready, kd_diff, kd_exp, qe_exp, el_exp, s_zero = (
            sem("kd_ready"), sem("qe_ready"), sem("kd_diff"), sem("kd_exp"), sem("qe_exp"), sem("el_exp"),
            sem("s_zero"))
        g_hi, g_lo = sem("g_hi"), sem("g_lo")
        o_out, o_normed, tri_done, pt_first = (
            sem("o_out"), sem("o_normed"), sem("tri_done"), sem("pt_first"))
        passed = sem("passed")
        y_done, y_turned, y_kept, y_kept_act, stored = (
            sem("y_done"), sem("y_turned"), sem("y_kept"), sem("y_kept_act"), sem("stored"))

        H_FFN = [KT, KT + KT * len(GROUPS) + KT]
        H_OUT = KT + KT * len(GROUPS)
        H_END = H_FFN[1] + KT * len(GROUPS)
        FFNS = [(ffn1, U_FFN1, 0), (ffn2, U_FFN2, 1)]

        scrap_done = sem("scrap_done")

        def psum_parts(bank, norm):
            return ps[:, bank:bank + 2, 0:HALF] if norm < 2 else ps[:, bank, 0:SEQ]

        def x_cols(n):
            t = n // 2
            return (META + t * P, P) if t < 4 else (0, META)

        def keep_x(eng, n):
            c, w = x_cols(n)
            eng.wait_ge(x_turned, n + 1)
            src = ps[:, n % 8, 0:4 * w].rearrange("p (k n) -> p k n", k=4)
            dst = h[:, 4 * (n % 2):4 * (n % 2) + 4, c:c + w]
            if n % 2 == 1:
                eng.activation(dst, src, ACT.Copy).then_inc(x_kept_act, 1)
            else:
                eng.tensor_copy(dst, src).then_inc(x_kept, 1)

        x_kept_act, sq0_done = sem("x_kept_act"), sem("sq0_done")

        def keep_y(eng, half):
            eng.wait_ge(rstd_done, 4)
            for t in range(4):
                eng.wait_ge(y_turned, 4 * half + t + 1)
                src, dst = ps[:, 4 * half + t, :], xin[:, t, 512 * half:512 * half + 512]
                if half:
                    eng.activation(dst, src, ACT.Copy, scale=rout[:, t:t + 1]).then_inc(y_kept_act, 1)
                else:
                    eng.tensor_scalar(dst, src, rout[:, t:t + 1], None, ALU.mult).then_inc(y_kept, 1)

        def swap_r(sp, swap, r):
            n = r - R_Q
            sp.wait_ge(pj_kept, 5 + r + 1)
            if n < 4:
                sp.wait_ge(rope_done, 5)
            else:
                sp.wait_ge(q_roped, n - 3)
            swap(5 + n, pjb[:, n, :], sw[:, n % 4, :])

        V_BANKS = {M_GV: [4, 5, 6, 7, 2], M_DV: [3, 4, 5, 6, 7]}
        INDEX = [(b0 + c, hd) for b0 in (1, 3) for hd in range(HEADS) for c in range(2)]
        relu_buf = [gb[:, 0, :], gb[:, 1, :], xb[:, 1, :]]
        RC = [(RC_WIN[w], s, n) for w, (s, n) in enumerate(WIN)] + [(RC_BLK[b], s, n) for b, (s, n) in enumerate(BLK)]

        def lv_ap(ap, g):
            n = TOK if TOK % (2 * LEVELS[g - 1]) == 0 else FULL_WIN * P
            return ap[:, :, 0:n].rearrange("p t (m a b) -> p t m a b", a=2, b=LEVELS[g - 1])

        def lv_steps(g):
            if g == 0:
                return [[w] for w in range(len(WIN))]
            pairs = [[w, w + 1] for w in range(0, FULL_WIN, 2)]
            return pairs + [[FULL_WIN]] if LEVELS[g - 1] < WIN[-1][1] else pairs

        STEPS = [(g, ws) for g in range(NLV) for ws in lv_steps(g)]

        def steps_before(g):
            return sum(len(lv_steps(k)) for k in range(g))

        zq = [t01[:, :, :].rearrange("p t (e n) -> p t e n", e=2),
              ikga[:, :, :].rearrange("p t (e n) -> p t e n", e=2)]
        xbuf = [xa, xb]
        kdt = pja[:, 2:4, :].rearrange("p t n -> p (t n)")[:, 0:FULL_WIN * 2 * P].rearrange(
            "p (w t n) -> p w t n", w=FULL_WIN, t=2)

        def pe_mixer(pe, product, norm_product):
            for m in range(5):
                if m == 3:
                    pe.wait_ge(var_done, 2)
                if m >= 4:
                    pe.wait_ge(pj_kept, m - 3)
                rows = G_COL + N_GA if m == M_IKW else P
                product(U_MIX + m, 2 * (m % 4), rows, xh, xl, KT,
                        before_k=(lambda k: pe.wait_ge(x_lo, KT + k + 1)) if m == 0 else None)
                if m == 0:
                    norm_product(1)

            def v_unit(m0, q, blocks):
                u = U_MIX + m0 + q
                slot = u % RING
                pe.wait_ge(w_split, u + RING + 1)
                for b, (s, n) in enumerate(blocks):
                    for k in range(2):
                        for c, (xx, ww) in enumerate(((xh, wh), (xl, wh), (xh, wl))):
                            mm = pe.matmul(ps[0:n, V_BANKS[m0][b], :], xx[:, 2 * q + k, s:s + n],
                                           ww[:, slot, k * 512:(k + 1) * 512], start=(q == 0 and k == 0 and c == 0),
                                           stop=(q == 3 and k == 1 and c == 2))
                mm.then_inc(w_used, 1)

            pe.wait_ge(pj_kept, 4)
            v_unit(M_GV, 0, WIN)
            pe.wait_ge(pj_kept, 5)
            pe.wait_ge(iw_scaled, 1)
            pe.wait_ge(ga_scaled, 1)
            pe.wait_ge(rstd_done, 2)
            for c, s, n in RC:
                pe.matmul(ps[0:n, 3, c:c + 1], rstd[0:1, s:s + n], ones[0:1, 0:1], start=True, stop=True)
            for b in range(1, len(BLK)):
                s, n = BLK[b]
                mm = pe.transpose(ps[0:n, 1, 8 * b:8 * b + 8], ga[64:64 + HEADS, s:s + n],
                                  ident[64:64 + HEADS, 64:64 + HEADS])
            mm.then_inc(tok_turned, 1)
            for q in range(1, 4):
                v_unit(M_GV, q, WIN)

            pe.wait_ge(iq_his, 8)
            pe.wait_ge(iqs_stacked, 8 * 16)
            pe.wait_ge(iks_stacked, 2 * 16)
            for n, (b, hd) in enumerate(INDEX):
                q = (n + 2) % 4
                if n == 2:
                    pe.wait_ge(tok_kept, 4)
                elif n < 2:
                    pe.wait_ge([v_kept, v_kept_dve][n], 1)
                elif n == 3:
                    pe.wait_ge(v_kept, 2)
                    pe.wait_ge(v_kept_dve, 3)
                else:
                    pe.wait_ge(relu_done, n - 3)
                s, w = BLK[b]
                for a, (k0, kn) in enumerate(key_parts(b)):
                    kn = max(kn, 256)
                    for part in range(2):
                        mm = pe.matmul(ps[0:w, 2 * q + a, 0:kn], iqs[:, hd, s:s + w], iks[:, part, k0:k0 + kn],
                                       start=(part == 0), stop=(part == 1))
                mm.then_inc(idx_done, 1)
            for t in range(2):
                q = 2 + t
                pe.wait_ge(relu_done, 29 + t)
                for a in range(2):
                    mm = pe.matmul(ps[:, 2 * q + a, 0:HALF], wa2[:, t, :], ga[0:N_GA, a * HALF:(a + 1) * HALF],
                                   start=True, stop=True)
                mm.then_inc(z_done, 1)
            with pe.Fori(0, R_LEVEL // 4) as i:
                for j in range(4):
                    if j >= 2:
                        pe.wait_ge(gate_y, j - 1)
                    else:
                        pe.wait_ge(relu_done, 32)
                    pe.wait_ge(pj_kept, at(i, 4, j + 2))
                    product(U_MIX + M_RAW + j, 2 * j, P, xh, xl, KT, i)

            n = 0
            for g in range(NLV):
                pe.wait_ge(pj_kept, 5 + (R_LEVEL - 3 if g == 0 else R_LEVEL + g))
                product(U_MIX + M_RAW + R_LEVEL + g, 0, P, xh, xl, KT)
                if g == 0:
                    pe.wait_ge(pj_kept, 5 + R_LEVEL)
                    pe.wait_ge(gqk_scaled, 4)
                    pe.wait_ge(zq_zero, 4)
                else:
                    pe.wait_ge(lv_x, 3 * g)
                for ws in lv_steps(g):
                    if n >= 3:
                        pe.wait_ge(at_done, n - 2)
                    for w in ws:
                        s, width = WIN[w]
                        if g == 0:
                            for hd in range(GLA_HEADS):
                                t, e = hd // 2, 64 * (hd % 2)
                                mm = pe.matmul(ps[0:width, lv_bank(n) + hd % 2, t * width:(t + 1) * width],
                                               pja[e:e + DK, 2 + t, s:s + width], pja[e:e + DK, t, s:s + width],
                                               start=True, stop=True)
                        else:
                            for t in range(2):
                                c = 2 * P * (w - ws[0]) + t * width
                                mm = pe.matmul(ps[0:width, lv_bank(n), c:c + width], xbuf[g % 2][:, t, s:s + width],
                                               zq[g % 2][:, t, :, s // 2:(s + width) // 2], start=True, stop=True)
                    mm.then_inc(lv_mm, 1)
                    n += 1
            pe.wait_ge(at_done, len(STEPS))
            v_unit(M_DV, 0, BLK)
            pe.wait_ge(pj_kept, 5 + 16)
            pe.wait_ge(kd_ready, 2)
            for w, (s, width) in enumerate(WIN[0:FULL_WIN]):
                for t in range(2):
                    c = (2 * (w % 2) + t) * P
                    mm = pe.transpose(ps[:, w // 2, c:c + P], xb[:, t, s:s + width], ident[:, :])
                if w % 2:
                    mm.then_inc(kd_turned, 1)
            pe.wait_ge(qe_ready, 1)
            pe.wait_ge(kd_kept, 2)

            def square_sums(windows):
                for w in windows:
                    s, width = WIN[w]
                    pe.wait_ge(o_sq, 2 * (w + 1))
                    for hd in range(GLA_HEADS):
                        c = GLA_HEADS * w + hd
                        mm = pe.matmul(ps[0:n_orow, 3, 0:width], pick[:, n_orow - 1 - c:2 * n_orow - 1 - c],
                                       o_square[hd // 2][:, hd % 2, s:s + width], start=(c == 0),
                                       stop=(c == n_orow - 1))
                return mm

            pe.wait_ge(picked, 2)
            for w, (s, width) in enumerate(WIN):
                if 0 < w < 4:
                    v_unit(M_DV, w, BLK)
                if w == 4:
                    pe.wait_ge(v_kept, 7)
                    square_sums([0, 1, 2])
                if w:
                    pe.wait_ge(s_new, GLA_HEADS * w)
                if w < FULL_WIN:
                    for hd in range(GLA_HEADS):
                        t, e = hd // 2, 64 * (hd % 2)
                        mm = pe.matmul(ps[e:e + DK, 2, t * DV:(t + 1) * DV], kdt[0:width, w, t, e:e + DK],
                                       gv[0:width, w, hd * DV:(hd + 1) * DV], start=True, stop=True)
                    mm.then_inc(s_mm, 1)
                if w >= 2:
                    pe.wait_ge(o_sq, 2 * (w - 1))
                for hd in range(GLA_HEADS):
                    t, e = hd // 2, 64 * (hd % 2)
                    o = ps[:, w % 2, hd * width:(hd + 1) * width]
                    mm = pe.matmul(o, gv[0:width, w, hd * DV:(hd + 1) * DV], at_win(w)[:, t, hd % 2, :], start=True,
                                   stop=(w == 0))
                    if w:
                        mm = pe.matmul(o, S[:, hd, :], xa[:, t, s:s + width], start=False, stop=True)
                mm.then_inc(o_mm, 1)
            square_sums([3, 4]).then_inc(o_sum, 1)
            pe.wait_ge(o_rstd, 1)
            pe.wait_ge(o_kept, len(WIN))
            for w, (s, width) in enumerate(WIN):
                for hd in range(GLA_HEADS):
                    c = GLA_HEADS * w + hd
                    mm = pe.matmul(ps[:, 3 + w, hd * width:(hd + 1) * width],
                                   ident[0:n_orow, c:c + 1].broadcast_to([n_orow, P]), orow[:, 0:width],
                                   start=True, stop=True)
                mm.then_inc(o_spread, 1)

            pe.wait_ge(s_new, GLA_HEADS * FULL_WIN)
            pe.wait_ge(kst_zero, 4)
            with pe.Fori(0, HEADS // 4) as i:
                def logits(n):
                    pair, e, b, s, w = att_step(n)
                    if n % 10 == 0:
                        pe.wait_ge(staged, at(i, 10, 5 * (pair + 1)))
                    pe.wait_ge(lg_done, at(i, N_ATT, n + 1))
                    for a, (k0, kn) in enumerate(key_parts(b)):
                        mm = pe.matmul(ps[0:w, QK_BANK[b] + a, 0:kn], qst[pair][:, s:s + w],
                                       kst[pair][e][:, k0:k0 + kn], start=True, stop=True)
                    mm.then_inc(qk_done, 1)

                def values(n):
                    pair, e, b, s, w = att_step(n)
                    pe.wait_ge(pt_kept, at(i, N_ATT, n + 3))
                    pe.wait_ge(m_lo, at(i, N_ATT, n + 1))
                    for c in range(b + 1):
                        wc = BLK[c][1]
                        mm = pe.matmul(ps[HD * e:HD * (e + 1), 6 + n % 2, 0:w], vst[pair][0:wc, c, HD * e:HD * (e + 1)],
                                       pt[0:wc, n % 2, c * w:(c + 1) * w], start=(c == 0), stop=(c == b))
                    mm.then_inc(pv_done, 1)

                logits(0)
                logits(1)
                for n in range(N_ATT):
                    pair, e, b, s, w = att_step(n)
                    if n + 2 < N_ATT:
                        logits(n + 2)
                    if n == 0:
                        pe.wait_ge(o_normed, len(WIN))
                    pe.wait_ge(diag_done, at(i, N_ATT, n + 3))
                    pe.wait_ge(pt_kept, at(i, N_ATT, n + 1))
                    for c in range(b + 1):
                        sc, wc = BLK[c]
                        mm = pe.matmul(ps[0:wc, 4 + n % 2, c * w:(c + 1) * w], pr[0:w, n % 2, sc:sc + wc],
                                       dg[0:w, n % 2, 0:w], start=True, stop=True)
                    mm.then_inc(pt_done, 1)
                    if n:
                        values(n - 1)
                values(N_ATT - 1)

            pe.wait_ge(g_lo, GLA_HEADS)

            def mix_ready(k):
                if MIX_TILE[k] < 4:
                    pe.wait_ge(m_lo, 2 + HEADS // 4 * N_ATT)

            with pe.Fori(0, KT // 4) as i:
                for j in range(4):
                    pe.wait_ge(h_done, at(i, 4, H_OUT + j - 3))
                    product(U_OUT + j, 2 * j, P, ah, al, KT, i, mix_ready if j == 0 else None, MIX_TILE,
                            norm=2)

        def key_parts(b):
            n = SEEN[b]
            return [(0, n)] if n <= 512 else [(0, HALF), (HALF, n - HALF)]

        def key_view(ap, b):
            return ap if SEEN[b] <= 512 else halves(ap)

        def key_psum(b, w, bank):
            return ps[0:w, bank, 0:SEEN[b]] if SEEN[b] <= 512 else ps[0:w, bank:bank + 2, 0:HALF]

        o_square = [xb, pja[:, 0:2, :]]

        N_ATT = 4 * len(BLK)
        ATT_ORDER = [0, 3, 2, 4, 1]
        QK_BANK = [0, 2, 2, 1, 0]
        MIX_TILE = [4, 5, 6, 7, 0, 1, 2, 3]

        def att_step(n):
            pair, rest = divmod(n, 2 * len(BLK))
            e, rest = divmod(rest, len(BLK))
            b = ATT_ORDER[rest]
            return (pair, e, b) + BLK[b]

        def lv_bank(n):
            return 2 + 2 * (n % 3)

        def act_mixer(act, hi, prep_hi, root):
            def keep(bank, dst, rows, u, i=None):
                act.wait_ge(w_used, at(i, 4, u + RING + 1))
                act.activation(halves(dst), ps[0:rows, bank:bank + 2, 0:HALF], ACT.Copy).then_inc(pj_kept, 1)

            def keep_v(dst, m0, blocks, cols, first):
                act.wait_ge(w_used, U_MIX + m0 + 3 + RING + 1)
                act.wait_ge(tok_kept, 4)
                for b, (s, n) in enumerate(blocks[0:first]):
                    act.activation(dst[0:n, b, :], ps[0:n, V_BANKS[m0][b], :], ACT.Copy,
                                   scale=rcol[0:n, cols[b]:cols[b] + 1]).then_inc(v_kept, 1)

            for m in range(5):
                hi(U_MIX + m + 2)
                if m == 1:
                    root(1)
                if m < 4:
                    keep(2 * m, iq[:, m, :], P, U_MIX + m)
                elif m == 4:
                    keep(0, ik[0:HD, :], HD, U_MIX + m)
            for m in range(4):
                act.wait_ge(rope_done, m + 1)
                for e in range(2):
                    rows = slice(HD * e, HD * (e + 1))
                    act.activation(iqs[rows, 2 * m + e, :], iq[rows, m, :], ACT.Copy).then_inc(iq_his, 1)
            hi(U_MIX + M_GV + 2)
            act.wait_ge(rope_done, 5)
            act.activation(iks[0:HD, 0, :], ik[0:HD, :], ACT.Copy).then_inc(ik_his, 1)
            for q in range(1, 4):
                hi(U_MIX + M_GV + q + 2)
            keep_v(gv, M_GV, WIN, RC_WIN, 2)
            for n, (b, hd) in enumerate(INDEX):
                w = BLK[b][1]
                act.wait_ge(idx_done, n + 1)
                if n >= 3:
                    act.wait_ge(acc_done, n - 2)
                act.activation(key_view(relu_buf[n % 3][0:w, 0:SEEN[b]], b), key_psum(b, w, 2 * ((n + 2) % 4)),
                               ACT.Relu).then_inc(relu_done, 1)
            u = U_MIX + M_RAW
            hi(u + 2)
            hi(u + 3)
            act.wait_ge(gate_y, 2)
            act.activation(gb[:, :, :], xa[:, :, :], ACT.Abs).then_inc(gate_abs, 1)
            act.wait_ge(gate_abs, 1)
            act.activation(gb[:, :, :], gb[:, :, :], ACT.Exp, scale=-1.0).then_inc(gate_exp, 1)
            act.wait_ge(gate_exp, 1)
            act.activation(gb[:, :, :], gb[:, :, :], ACT.Ln, bias=1.0).then_inc(gate_ln, 1)

            def raw_tile(r):
                return pja[:, r, :] if r < R_Q else pjb[:, r - R_Q, :] if r < R_GR else pja[:, 4 + r - R_GR, :]

            def level_exp(g):
                act.wait_ge(lv_diff, 2 * g)
                part = xbuf[g % 2][:, :, 0:TOK if TOK % (2 * LEVELS[g - 1]) == 0 else FULL_WIN * P]
                act.activation(part, part, ACT.Exp, scale=1.0 / GATE_NORM).then_inc(lv_exp, 1)

            for r in range(R_LEVEL):
                if r >= 2:
                    hi(u + r + 2)
                keep(2 * (r % 4), raw_tile(r), P, u + r)
                if r == R_LEVEL - 2:
                    level_exp(1)
            for g in range(NLV + 1):
                if 1 < g < NLV:
                    level_exp(g)
                if g == NLV:
                    act.wait_ge(lv_mm, steps_before(NLV - 1))
                    act.activation(xa[:, :, :], gb[:, :, :], ACT.Exp, scale=1.0 / GATE_NORM).then_inc(qe_exp, 1)
                    act.activation(elast.rearrange("p (t w) -> p t w", t=2)[:, :, 0:FULL_WIN],
                                   gb[:, :, P - 1:FULL_WIN * P:P], ACT.Exp, scale=1.0 / GATE_NORM).then_inc(el_exp, 1)
                    act.wait_ge(kd_diff, 2)
                    act.activation(xb[:, :, 0:FULL_WIN * P], xb[:, :, 0:FULL_WIN * P], ACT.Exp,
                                   scale=1.0 / GATE_NORM).then_inc(kd_exp, 1)
                if g < NLV:
                    hi(u + R_LEVEL + g + 2)
                    keep(0, raw_tile(R_LEVEL + g), P, u + R_LEVEL + g)
            hi(U_MIX + M_DV + 2)
            hi(U_MIX + M_DV + 3)
            for w, (s, n) in enumerate(WIN):
                act.wait_ge(o_mm, w + 1)
                if w == 0:
                    act.wait_ge(q_roped, 8)
                    act.wait_ge(kd_turned, 2)
                o = ps[:, w % 2, 0:GLA_HEADS * n].rearrange("p (g n) -> p g n", g=GLA_HEADS)
                act.activation(oT[:, :, s:s + n], o, ACT.Copy).then_inc(o_kept, 1)
                for pair in range(2):
                    act.activation(o_square[pair][:, :, s:s + n], o[:, 2 * pair:2 * pair + 2, :],
                                   ACT.Square).then_inc(o_sq, 1)
                if w == 0:
                    hi(U_OUT)
                elif w == 1:
                    hi(U_OUT + 1)
                elif w == 2:
                    keep_v(dv, M_DV, BLK, RC_BLK, 5)
            act.wait_ge(o_inv, 1)
            act.activation(orow, orow, ACT.Sqrt).then_inc(o_rstd, 1)
            act.wait_ge(gr_scaled, 4)
            act.activation(pja[:, 4:8, :], pja[:, 4:8, :], ACT.Silu).then_inc(gr_silu, 1)
            act.activation(scrap[:, :], scrap[:, :], ACT.Exp).then_inc(scrap_done, 1)
            with act.Fori(0, HEADS // 4) as i:
                def probs(n):
                    pair, e, b, s, w = att_step(n)
                    act.wait_ge(lg_done, at(i, N_ATT, n + 3))
                    act.wait_ge(pt_done, at(i, N_ATT, n + 1))
                    act.activation(pr[0:w, n % 2, 0:SEEN[b]], lg[0:w, n % 2, 0:SEEN[b]], ACT.Exp, scale=-1.0,
                                   bias=stat[0:w, 4 + n % 2:5 + n % 2],
                                   accum_out=stat[0:w, 6 + n % 2:7 + n % 2]).then_inc(exp_done, 1)
                    act.wait_ge(sum_inv, at(i, N_ATT, n + 1))
                    act.activation(dg[0:w, n % 2, 0:w], ident[0:w, 0:w], ACT.Copy,
                                   scale=stat[0:w, 8 + n % 2:9 + n % 2]).then_inc(diag_done, 1)

                def keep_hi(n):
                    pair, e, b, s, w = att_step(n)
                    rows = slice(HD * e, HD * (e + 1))
                    act.wait_ge(pv_done, at(i, N_ATT, n + 3))
                    act.activation(ah[rows, 2 * i + pair, s:s + w], ps[rows, 6 + n % 2, 0:w],
                                   ACT.Copy).then_inc(m_hi, 1)

                probs(0)
                for n in range(N_ATT):
                    if n + 1 < N_ATT:
                        probs(n + 1)
                    if n:
                        keep_hi(n - 1)
                keep_hi(N_ATT - 1)
            for d in range(KT):
                hi(U_OUT + d + 2)
                prep_hi(2, d, H_OUT + d)

        def dve_mixer(dve, prep, prep_lo):
            dve.wait_ge(rstd_done, 2)
            dve.wait_ge(mix_loaded, 48)
            dve.tensor_tensor(cosr[:, :], cosr[:, :], rstd[:, :], ALU.mult).then_inc(tables_done, 1)
            dve.tensor_tensor(sinr[:, :], sinr[:, :], rstd[:, :], ALU.mult).then_inc(tables_done, 1)
            dve.wait_ge(tables_done, 2)

            def rope(n, x, s, rows):
                dve.wait_ge(swapped[n], 64 if rows == P else 32)
                dve.tensor_tensor(s[0:rows, :], s[0:rows, :], sinr[0:rows, :], ALU.mult).then_inc(rope_sin, 1)
                dve.tensor_tensor(x[0:rows, :], x[0:rows, :], cosr[0:rows, :], ALU.mult).then_inc(rope_cos, 1)
                dve.wait_ge(rope_sin, n + 1)
                dve.wait_ge(rope_cos, n + 1)
                dve.tensor_tensor(x[0:rows, :], x[0:rows, :], s[0:rows, :], ALU.add).then_inc(rope_done, 1)

            for m in range(4):
                rope(m, iq[:, m, :], sw[:, m, :], P)
            dve.wait_ge(w_used, U_MIX + M_IKW + RING + 1)
            dve.scalar_tensor_tensor(out=halves(ga[64:64 + HEADS, :]), in0=ps[64:64 + HEADS, 0:2, 0:HALF],
                                     scalar=HEADS ** -0.5 * HD ** -0.5, in1=halves(rstd[64:64 + HEADS, :]),
                                     op0=ALU.mult, op1=ALU.mult).then_inc(iw_scaled, 1)
            dve.tensor_tensor(halves(ga[0:N_GA, :]), ps[G_COL:G_COL + N_GA, 0:2, 0:HALF],
                              halves(rstd[G_COL:G_COL + N_GA, :]),
                              ALU.mult).then_inc(ga_scaled, 1)
            rope(4, ik, sw[:, 0, :], HD)
            dve.wait_ge(tok_turned, 1)
            dve.tensor_copy(rcol[:, 0:5], ps[:, 3, 0:5]).then_inc(tok_kept, 1)
            dve.tensor_copy(rcol[0:100, 5:9], ps[0:100, 3, 5:9]).then_inc(tok_kept, 1)
            dve.tensor_copy(rcol[0:WIN[-1][1], 9:10], ps[0:WIN[-1][1], 3, 9:10]).then_inc(tok_kept, 1)
            dve.tensor_copy(iwt[0:100, :], ps[0:100, 1, 8:40]).then_inc(tok_kept, 1)
            dve.wait_ge(tok_kept, 4)
            dve.wait_ge(consts, 3)
            dve.wait_ge(ik_his, 1)
            dve.tensor_tensor(iks[0:HD, 1, :], ik[0:HD, :], iks[0:HD, 0, :].bitcast(F32),
                              ALU.subtract).then_inc(ik_los, 1)
            for hd in range(HEADS):
                m, e = divmod(hd, 2)
                rows = slice(HD * e, HD * (e + 1))
                dve.wait_ge(iq_his, hd + 1)
                dve.tensor_tensor(iq_lo[rows, m, :], iq[rows, m, :], iqs[rows, hd, :].bitcast(F32),
                                  ALU.subtract).then_inc(iq_los, 1)
            dve.wait_ge(w_used, U_MIX + M_GV + 3 + RING + 1)
            for b in range(2, len(WIN)):
                n = WIN[b][1]
                dve.tensor_scalar(gv[0:n, b, :], ps[0:n, V_BANKS[M_GV][b], :], rcol[0:n, RC_WIN[b]:RC_WIN[b] + 1], None,
                                  ALU.mult).then_inc(v_kept_dve, 1)
            for n, (b, hd) in enumerate(INDEX):
                w = BLK[b][1]
                sc = mask[0:w, MASK_AT[b]:MASK_AT[b] + SEEN[b]]
                weight = iwt[0:w, 8 * (b - 1) + hd:8 * (b - 1) + hd + 1]
                r = relu_buf[n % 3][0:w, 0:SEEN[b]]
                dve.wait_ge(relu_done, n + 1)
                if hd == 0:
                    dve.tensor_scalar(sc, r, weight, None, ALU.mult).then_inc(acc_done, 1)
                else:
                    dve.wait_ge(acc_done, n - 1)
                    dve.scalar_tensor_tensor(out=sc, in0=r, scalar=weight, in1=sc, op0=ALU.mult,
                                             op1=ALU.add).then_inc(acc_done, 1)
            dve.wait_ge(acc_done, 32)
            for b in range(len(BLK)):
                s, w = BLK[b]
                own = mask[0:w, MASK_AT[b] + s:MASK_AT[b] + s + w]
                if b == 0:
                    dve.tensor_copy(own, tri[0:w, 0:w]).then_inc(mask_done, 1)
                else:
                    dve.tensor_tensor(own, own, tri[0:w, 0:w], ALU.add).then_inc(tri_done, 1)
            for t in range(2):
                dve.wait_ge(z_done, t + 1)
                dve.tensor_scalar(halves(xa[:, t, :]), ps[:, 4 + 2 * t:6 + 2 * t, 0:HALF], ba[:, t:t + 1], None,
                                  ALU.add).then_inc(gate_y, 1)
            for z in zq:
                for e in range(2):
                    dve.memset(z[64 * (1 - e):64 * (1 - e) + DK, :, e, :], 0.0).then_inc(zq_zero, 1)
            dve.wait_ge(tri_done, 4)
            rounds = TOPK // 8

            def blocks(pair):
                for c in range(2):
                    b = 1 + 2 * pair + c
                    w = BLK[b][1]
                    yield c, top8[c][0:w, :], mask[0:w, MASK_AT[b]:MASK_AT[b] + SEEN[b]]

            def select(pair, t, i=None):
                n = 2 * (pair * rounds + t)
                for c, top, sc in blocks(pair):
                    dve.wait_ge(top_taken, at(i, 8, n + c + 1))
                    dve.sem_inc(passed, 1)
                    dve.max(top, sc).then_inc(top_found, 1)
                for c, top, sc in blocks(pair):
                    dve.wait_ge(top_found, at(i, 8, n + c + 1))
                    dve.sem_inc(passed, 1)
                    dve.match_replace(sc, top, sc, TAKEN).then_inc(top_taken, 1)

            def select_end(pair):
                for c, top, sc in blocks(pair):
                    dve.wait_ge(top_taken, 2 * (pair + 1) * rounds + c + 1)
                    dve.tensor_scalar(sc, sc, TAKEN * 0.5, NEG, ALU.is_gt, ALU.mult).then_inc(mask_done, 1)

            with dve.Fori(0, rounds // 4) as i:
                for j in range(4):
                    select(0, j, i)
            select_end(0)
            selected = 0

            dve.wait_ge(pj_kept, 5 + 4)
            for t in range(4):
                dve.scalar_tensor_tensor(out=pja[:, t, :], in0=pja[:, t, :], scalar=DK ** -0.5 if t < 2 else 1.0,
                                         in1=rstd[:, :], op0=ALU.mult, op1=ALU.mult).then_inc(gqk_scaled, 1)
            dve.wait_ge(gate_ln, 1)
            dve.scalar_tensor_tensor(out=xa[:, :, :], in0=xa[:, :, :], scalar=0.0, in1=gb[:, :, :], op0=ALU.min,
                                     op1=ALU.subtract).then_inc(gate_g, 1)
            dve.wait_ge(gate_g, 1)
            for t in range(2):
                for s, w in WIN:
                    dve.tensor_tensor_scan(gb[:, t, s:s + w], ones[:, 0:w], xa[:, t, s:s + w], 0.0, ALU.mult,
                                           ALU.add).then_inc(gate_cum, 1)
            dve.wait_ge(gate_cum, 2 * len(WIN))
            dve.wait_ge(gqk_scaled, 4)

            def level_diff(g):
                if g >= 3:
                    dve.wait_ge(lv_mm, steps_before(g - 1))
                b5, x5 = lv_ap(gb, g), lv_ap(xbuf[g % 2], g)
                s = LEVELS[g - 1]
                ref = b5[:, :, :, 0, s - 1:s].broadcast_to([P, 2, b5.shape[2], s])
                dve.tensor_tensor(x5[:, :, :, 0, :], ref, b5[:, :, :, 0, :], ALU.subtract).then_inc(lv_diff, 1)
                dve.tensor_tensor(x5[:, :, :, 1, :], b5[:, :, :, 1, :], ref, ALU.subtract).then_inc(lv_diff, 1)

            def level_x(g):
                dve.wait_ge(lv_exp, g)
                x5, k5, q5 = lv_ap(xbuf[g % 2], g), lv_ap(pja[:, 2:4, :], g), lv_ap(pja[:, 0:2, :], g)
                m, b = x5.shape[2], LEVELS[g - 1]
                for e in range(2):
                    rows = slice(64 * e, 64 * e + DK)
                    z = zq[g % 2][rows, :, e, 0:m * b].rearrange("p t (m b) -> p t m b", b=b)
                    dve.tensor_tensor(z, x5[rows, :, :, 1, :], q5[rows, :, :, 1, :], ALU.mult).then_inc(lv_x, 1)
                dve.tensor_tensor(x5[:, :, :, 0, :], x5[:, :, :, 0, :], k5[:, :, :, 0, :], ALU.mult).then_inc(lv_x, 1)

            def level_take(g):
                for k, ws in enumerate(lv_steps(g)):
                    n = steps_before(g) + k
                    w, width = ws[0], WIN[ws[0]][1]
                    dve.wait_ge(lv_mm, n + 1)
                    bank = lv_bank(n)
                    if g == 0:
                        src = ps[0:width, bank:bank + 2, 0:2 * width].rearrange("p e (t n) -> p t e n", t=2)
                        sel = ident[0:width, 0:width].unsqueeze(1).unsqueeze(1).broadcast_to([width, 2, 2, width])
                        dve.tensor_tensor(at_win(w), src, sel, ALU.mult).then_inc(at_done, 1)
                    else:
                        b, g4 = LEVELS[g - 1], GLA_HEADS * len(ws)
                        dve.wait_ge(at_done, n)
                        src = ps[0:width, bank, 0:g4 * width // 2].rearrange("p (g m b) -> p g m b", g=g4, b=b)
                        sel = lvm[0:width, g - 1, 0:width].rearrange("p (m a b) -> p m a b", a=2, b=b)[:, :, 1, :]
                        sel = sel.unsqueeze(1).broadcast_to([width, g4, width // (2 * b), b])
                        c = w * GLA_HEADS * P
                        dst = AT[0:width, c:c + g4 * width].rearrange("p (g m a b) -> p g m a b", g=g4, a=2, b=b)
                        dve.copy_predicated(dst[:, :, :, 1, :], sel, src).then_inc(at_done, 1)

            dve.wait_ge(lv_step, 5 * len(LEVELS))
            level_diff(1)
            for _ in range(ROUNDS_LEVEL[0]):
                select(1, selected)
                selected += 1
            for g in range(1, NLV):
                level_x(g)
                if g + 1 < NLV:
                    level_diff(g + 1)
                level_take(g - 1)
                for _ in range(ROUNDS_LEVEL.get(g, 0)):
                    select(1, selected)
                    selected += 1
            level_take(NLV - 1)
            for t in range(2):
                b3 = gb[:, t, 0:FULL_WIN * P].rearrange("p (w n) -> p w n", n=P)
                x3 = xb[:, t, 0:FULL_WIN * P].rearrange("p (w n) -> p w n", n=P)
                dve.tensor_tensor(x3, b3[:, :, P - 1:P].broadcast_to([P, FULL_WIN, P]), b3,
                                  ALU.subtract).then_inc(kd_diff, 1)
            dve.wait_ge(qe_exp, 1)
            dve.tensor_tensor(xa[:, :, :], xa[:, :, :], pja[:, 0:2, :], ALU.mult).then_inc(qe_ready, 1)
            dve.wait_ge(kd_exp, 1)
            for t in range(2):
                dve.tensor_tensor(xb[:, t, 0:FULL_WIN * P], xb[:, t, 0:FULL_WIN * P], pja[:, 2 + t, 0:FULL_WIN * P],
                                  ALU.mult).then_inc(kd_ready, 1)
            dve.memset(S[:, :, :], 0.0).then_inc(s_zero, 1)
            dve.wait_ge(kd_ready, 2)
            for c in range(2):
                dve.wait_ge(kd_turned, c + 1)
                dve.tensor_copy(kdt[:, 2 * c:2 * c + 2, :, :], ps[:, c, :].rearrange(
                    "p (w t n) -> p w t n", w=2, t=2)).then_inc(kd_kept, 1)
            dve.wait_ge(s_zero, 1)
            dve.wait_ge(el_exp, 1)
            for w in range(FULL_WIN):
                dve.wait_ge(s_mm, w + 1)
                if w:
                    dve.wait_ge(s_new, GLA_HEADS * w)
                    dve.wait_ge(o_mm, w + 1)
                for hd in range(GLA_HEADS):
                    t, e = hd // 2, 64 * (hd % 2)
                    new, old = ps[e:e + DK, 2, t * DV:(t + 1) * DV], S[e:e + DK, hd, :]
                    if w == 0:
                        dve.tensor_copy(old, new).then_inc(s_new, 1)
                    else:
                        dve.scalar_tensor_tensor(out=old, in0=old,
                                                 scalar=elast[e:e + DK, 5 * t + w:5 * t + w + 1], in1=new,
                                                 op0=ALU.mult, op1=ALU.add).then_inc(s_new, 1)
                for _ in range(ROUNDS_WIN.get(w, 0)):
                    select(1, selected)
                    selected += 1
            assert selected == rounds
            select_end(1)
            dve.wait_ge(o_sum, 1)
            dve.tensor_scalar(orow, ps[0:n_orow, 3, 0:P], 1.0 / DV, EPS, ALU.mult, ALU.add).then_inc(o_var, 1)
            dve.wait_ge(o_var, 1)
            dve.reciprocal(orow, orow).then_inc(o_inv, 1)
            dve.wait_ge(o_kept, len(WIN))
            for w, (s, width) in enumerate(WIN):
                dve.wait_ge(o_spread, w + 1)
                o = oT[:, :, s:s + width]
                dve.scalar_tensor_tensor(out=o, in0=o, scalar=hn, in1=ps[:, 3 + w, 0:GLA_HEADS * width].rearrange(
                    "p (g n) -> p g n", g=GLA_HEADS), op0=ALU.mult, op1=ALU.mult).then_inc(o_normed, 1)
            dve.wait_ge(mask_done, 5)
            with dve.Fori(0, HEADS // 4) as i:
                def masked(n):
                    pair, e, b, s, w = att_step(n)
                    dve.wait_ge(qk_done, at(i, N_ATT, n + 1))
                    dve.wait_ge(exp_done, at(i, N_ATT, n + 1))
                    dve.sem_inc(passed, 1)
                    dve.tensor_tensor_reduce(out=key_view(lg[0:w, n % 2, 0:SEEN[b]], b),
                                             in0=key_psum(b, w, QK_BANK[b]),
                                             in1=key_view(mask[0:w, MASK_AT[b]:MASK_AT[b] + SEEN[b]], b), scale=-HD ** -0.5,
                                             scalar=3.0e38, op0=ALU.add, op1=ALU.min,
                                             accum_out=stat[0:w, 4 + n % 2:5 + n % 2]).then_inc(lg_done, 1)

                def inverse(n):
                    w = att_step(n)[-1]
                    dve.wait_ge(exp_done, at(i, N_ATT, n + 3))
                    dve.wait_ge(diag_done, at(i, N_ATT, n + 1))
                    dve.reciprocal(stat[0:w, 8 + n % 2:9 + n % 2], stat[0:w, 6 + n % 2:7 + n % 2]).then_inc(sum_inv, 1)

                def keep_pt(n):
                    pair, e, b, s, w = att_step(n)
                    dve.wait_ge(pt_done, at(i, N_ATT, n + 3))
                    dve.wait_ge(pv_done, at(i, N_ATT, n + 1))
                    if b == 0:
                        dve.tensor_copy(pt[:, n % 2, 0:w], ps[:, 4 + n % 2, 0:w]).then_inc(pt_kept, 1)
                    else:
                        dve.tensor_copy(pt[:, n % 2, 0:w], ps[:, 4 + n % 2, 0:w]).then_inc(pt_first, 1)
                        dve.tensor_copy(pt[0:100, n % 2, w:(b + 1) * w],
                                        ps[0:100, 4 + n % 2, w:(b + 1) * w]).then_inc(pt_kept, 1)

                def keep_lo(n):
                    pair, e, b, s, w = att_step(n)
                    rows = slice(HD * e, HD * (e + 1))
                    dve.wait_ge(m_hi, at(i, N_ATT, n + 1))
                    dve.tensor_tensor(al[rows, 2 * i + pair, s:s + w], ps[rows, 6 + n % 2, 0:w],
                                      ah[rows, 2 * i + pair, s:s + w].bitcast(F32), ALU.subtract).then_inc(m_lo, 1)

                masked(0)
                masked(1)
                inverse(0)
                for n in range(N_ATT):
                    if n + 1 < N_ATT:
                        inverse(n + 1)
                    if n + 2 < N_ATT:
                        masked(n + 2)
                    keep_pt(n)
                    if n:
                        keep_lo(n - 1)
                keep_lo(N_ATT - 1)
            for d in range(KT):
                bank = 2 * (d % 4)
                dve.wait_ge(w_used, U_OUT + d + RING + 1)
                dve.wait_ge(h_done, H_OUT - KT + d + 1)
                part = h[:, d, tokens_of(2)]
                dve.tensor_tensor(part, psum_parts(bank, 2), part,
                                  ALU.add).then_inc(h_done, 1)
                prep(2, d, H_OUT + d)
                prep_lo(2, d)

        block = ctx.enter_context(nc.Block())

        @block.sync
        def _(sp):
            def load(u, src, dst_view, i=None):
                slot = u % RING
                sp.wait_ge(w_split, at(i, RING, u + 1))
                sp.dma_start(dst_view(raw[:, slot, :]), src).then_inc(w_in_slot[slot], 16)

            def cols(n=P):
                return lambda s: s.rearrange("p (k n) -> p k n", k=KT)[:, :, 0:n]

            def load_x(t):
                sp.dma_start(xin[:, t, :], x[t * P:(t + 1) * P, :]).then_inc(x_loaded[t], 16)

            load_x(0)
            load_x(1)
            sp.dma_start(xin[0:META, 4, :], meta).then_inc(x_loaded[4], 16)
            for n, g in enumerate([ffn1[0], mix_norm, ffn2[0], final_norm]):
                sp.dma_start(vec_rows[KT * n:KT * (n + 1), :], g.rearrange("(k p) -> k p", p=P)).then_inc(const_loaded, 16)
            sp.dma_start(vec_rows[4 * KT:4 * KT + 2, :], b_a.rearrange("(k p) -> k p", p=P)).then_inc(const_loaded, 16)
            sp.dma_start(vec_rows[4 * KT + 2:4 * KT + 3, :], head_norm.rearrange("(k p) -> k p", p=P)).then_inc(const_loaded, 16)

            load_x(2)
            load_x(3)

            def ffn_loads(weights, u0):
                _, w_gate, w_up, w_down = weights
                gate_v = w_gate.rearrange("(k p) f -> p k f", p=P)
                up_v = w_up.rearrange("(k p) f -> p k f", p=P)
                down_v = w_down.rearrange("(k p) d -> p k d", p=P)
                u = u0
                for f0, cnt in GROUPS:
                    with sp.Fori(0, cnt // 2) as i:
                        for j in range(2):
                            c = (i * 2 + (f0 + j)) * P
                            load(u + 2 * j, gate_v[:, :, bass.ds(c, P)], cols(), i)
                            load(u + 2 * j + 1, up_v[:, :, bass.ds(c, P)], cols(), i)
                    u += 2 * cnt
                    with sp.Fori(0, KT // RING) as i:
                        for j in range(RING):
                            c = (i * RING + j) * P
                            load(u + j, down_v[:, f0:f0 + cnt, bass.ds(c, P)],
                                 lambda s: s.rearrange("p (k n) -> p k n", k=KT)[:, 0:cnt, :], i)
                    u += KT

            ffn_loads(ffn1, U_FFN1)
            win_v = w_in.rearrange("(k p) n -> p k n", p=P)

            def load_mix(m):
                u = U_MIX + m
                if m < M_IKW:
                    load(u, win_v[:, :, C_IQ + m * P:C_IQ + (m + 1) * P], cols())
                elif m == M_IKW:
                    slot = u % RING
                    sp.wait_ge(w_split, u + 1)
                    for c, src, n in ((0, C_IK, N_IKW), (G_COL, C_GA, N_GA)):
                        dst = raw[:, slot, :].rearrange("p (k n) -> p k n", k=KT)[:, :, c:c + n]
                        sp.dma_start(dst, win_v[:, :, src:src + n]).then_inc(ikw_loaded if c == 0 else w_in_slot[slot], 16)
                elif M_RAW <= m < M_DV:
                    r = m - M_RAW
                    c = (C_GQK + r * P if r < R_Q else C_DQK + (r - R_Q) * P if r < R_GR
                         else C_GR + (r - R_GR) * P)
                    load(u, win_v[:, :, c:c + P], cols())
                else:
                    c, q = (C_GV, m - M_GV) if m < M_RAW else (C_DV, m - M_DV)
                    load(u, win_v[:, 2 * q:2 * q + 2, c:c + 512], lambda s: s.rearrange("p (k n) -> p k n", k=2))

            def swap(n, tile, dst, rows=P):
                for a in range(0, rows, 32):
                    b = a ^ 32
                    sp.dma_start(dst[a:a + 32, :], tile[b:b + 32, :]).then_inc(swapped[n], 16)

            for m in range(4):
                load_mix(m)
            sp.wait_ge(h_done, H_OUT)
            for dst, src in ((cosr, cos_t), (sinr, sin_t)):
                sp.dma_start(dst[:, :], src).then_inc(mix_loaded, 16)
            sp.dma_start(wa2[:, :, :], w_a2.rearrange("k (t n) -> k t n", n=P)).then_inc(mix_loaded, 16)
            load_mix(4)
            load_mix(5)
            for m in range(5):
                sp.wait_ge(pj_kept, m + 1)
                if m < 4:
                    swap(m, iq[:, m, :], sw[:, m, :])
                else:
                    sp.wait_ge(rope_done, 1)
                    swap(m, ik[:, :], sw[:, 0, :], HD)
                load_mix(6 + m)
            sp.wait_ge(rope_done, 5)
            sp.wait_ge(ik_his, 1)
            sp.dma_start(iks[HD:2 * HD, 0, :].bitcast(F32), iks[0:HD, 0, :].bitcast(F32)).then_inc(iks_stacked, 16)
            sp.wait_ge(ik_los, 1)
            sp.dma_start(iks[HD:2 * HD, 1, :].bitcast(F32), iks[0:HD, 1, :].bitcast(F32)).then_inc(iks_stacked, 16)
            for hd in range(HEADS):
                m, e = divmod(hd, 2)
                sp.wait_ge(iq_los, hd + 1)
                sp.dma_start(iqs[HD * (1 - e):HD * (2 - e), hd, :].bitcast(F32),
                             iq_lo[HD * e:HD * (e + 1), m, :].bitcast(F32)).then_inc(iqs_stacked, 16)
            for m in range(11, MIX_UNITS):
                load_mix(m)
                r = m - M_RAW - 5
                if R_Q <= r < R_GR:
                    swap_r(sp, swap, r)
            out_v = w_out.rearrange("(k p) d -> p k d", p=P)
            with sp.Fori(0, KT // RING) as i:
                for j in range(RING):
                    load(U_OUT + j, out_v[:, :, bass.ds((i * RING + j) * P, P)], cols(), i)
            ffn_loads(ffn2, U_FFN2)
            for t in range(SEQ // P):
                sp.wait_ge(y_kept, t + 1)
                sp.wait_ge(y_kept_act, t + 1)
                sp.dma_start(out[t * P:(t + 1) * P, :], xin[:, t, :]).then_inc(stored, 16)
            sp.wait_ge(stored, 16 * (SEQ // P))

        @block.gpsimd
        def _(pool):
            pool.sem_inc(w_split, RING)
            pool.memset(ident[:, :], 0.0).then_inc(c_zero, 1)
            pool.memset(ones[:, :], 1.0).then_inc(consts, 1)
            pool.memset(pick[:, :], 0.0).then_inc(picked, 1)
            pool.wait_ge(picked, 1)
            pool.memset(pick[:, n_orow - 1:n_orow], 1.0).then_inc(picked, 1)
            pool.wait_ge(c_zero, 1)
            pool.affine_select(out=ident[:, :], in_=ident[:, :], compare_op=ALU.not_equal, fill=1.0, base=0,
                               pattern=[[-1, P]], channel_multiplier=1).then_inc(consts, 1)

            def lo(u, i=None):
                slot = u % RING
                pool.wait_ge(w_hi, at(i, RING, u + 1))
                pool.tensor_tensor(wl[:, slot, :], raw[:, slot, :], wh[:, slot, :].bitcast(F32),
                                   ALU.subtract).then_inc(w_split, 1)

            def run(u0, n):
                if n >= RING:
                    with pool.Fori(0, n // RING) as i:
                        for j in range(RING):
                            lo(u0 + j, i)
                for j in range(n - n % RING, n):
                    lo(u0 + j)

            run(0, U_MIX)
            run(U_MIX, 6)
            pool.wait_ge(h_done, H_OUT)
            pool.memset(tri[:, :], 0.0).then_inc(c_zero, 1)
            pool.wait_ge(c_zero, 2)
            pool.affine_select(out=tri[:, :], in_=tri[:, :], compare_op=ALU.is_ge, fill=NEG, base=0,
                               pattern=[[-1, P]], channel_multiplier=1).then_inc(consts, 1)
            run(U_MIX + 6, M_RAW - 6)
            steps = 0
            for n, s in enumerate(LEVELS):
                scratch = xb[:, 0, 0:P]
                blk = scratch.rearrange("p (m a b) -> p m a b", a=2, b=s)
                if n:
                    pool.wait_ge(lv_step, steps)
                pool.memset(scratch, 0.0).then_inc(lv_step, 1)
                steps += 1
                pool.wait_ge(lv_step, steps)
                pool.memset(blk[:, :, 1, :], 1.0).then_inc(lv_step, 1)
                steps += 1
                pool.wait_ge(lv_step, steps)
                pool.affine_select(out=blk[:, :, 1, :], in_=blk[:, :, 1, :], compare_op=ALU.is_ge, fill=0.0,
                                   base=0, pattern=[[-2 * s, P // (2 * s)], [0, s]],
                                   channel_multiplier=1).then_inc(lv_step, 1)
                steps += 1
                pool.wait_ge(lv_step, steps)
                pool.affine_select(out=blk[:, :, 1, :], in_=blk[:, :, 1, :], compare_op=ALU.is_ge, fill=0.0,
                                   base=s - 1, pattern=[[2 * s, P // (2 * s)], [0, s]],
                                   channel_multiplier=-1).then_inc(lv_step, 1)
                steps += 1
                pool.wait_ge(lv_step, steps)
                pool.tensor_copy(lvm[:, n, :], scratch).then_inc(lv_step, 1)
                steps += 1
            run(U_MIX + M_RAW, 8)
            for n in range(8):
                lo(U_MIX + M_RAW + 8 + n)
                pool.wait_ge(swapped[5 + n], 64)
                s = sw[:, n % 4, :]
                pool.tensor_tensor(s, s, sinr[:, :], ALU.mult).then_inc(q_sin, 1)
                pool.tensor_tensor(pjb[:, n, :], pjb[:, n, :], cosr[:, :], ALU.mult).then_inc(q_cos, 1)
                pool.wait_ge(q_sin, n + 1)
                pool.wait_ge(q_cos, n + 1)
                pool.tensor_tensor(pjb[:, n, :], pjb[:, n, :], s, ALU.add).then_inc(q_roped, 1)
            for q in range(4):
                lo(U_MIX + M_DV + q)
            pool.wait_ge(pj_kept, 5 + 16)
            for t in range(4):
                pool.tensor_tensor(pja[:, 4 + t, :], pja[:, 4 + t, :], rstd[:, :], ALU.mult).then_inc(gr_scaled, 1)
            pool.wait_ge(q_roped, 8)
            pool.wait_ge(w_split, U_OUT + RING)
            pool.wait_ge(gr_scaled, 4)
            pool.wait_ge(lv_mm, len(STEPS))
            pool.wait_ge(kd_diff, 2)
            pool.wait_ge(el_exp, 1)
            pool.wait_ge(qe_exp, 1)
            for n, (pair, e) in enumerate(((0, 0), (0, 1), (1, 0), (1, 1))):
                pool.memset(kst[pair][e][64 * (1 - e):64 * (1 - e) + HD, :], 0.0).then_inc(kst_zero, 1)
                pool.wait_ge(kst_zero, n + 1)
            lo(U_OUT)
            lo(U_OUT + 1)
            pool.wait_ge(w_split, U_OUT + 2 + RING)

            def stage(p):
                k = p % 2
                if p >= 2:
                    pool.wait_ge(qk_done, 10 * (p - 1))
                pool.tensor_copy(qst[k][:, :], pjb[:, p, :]).then_inc(staged, 1)
                for e in range(2):
                    rows = slice(HD * e, HD * (e + 1))
                    pool.wait_ge(staged, 5 * p + 1 + e)
                    pool.tensor_copy(kst[k][e][rows, :], pjb[rows, p + 4, :]).then_inc(staged, 1)
                if p >= 2:
                    pool.wait_ge(pv_done, 2 + 10 * (p - 1))
                else:
                    pool.wait_ge(v_kept, 7)
                    pool.wait_ge(o_mm, len(WIN))
                if p == 1:
                    pool.wait_ge(o_normed, len(WIN))
                pool.wait_ge(staged, 5 * p + 3)
                pool.tensor_copy(vst[k][:, 0, :], dv[:, 0, p * P:(p + 1) * P]).then_inc(staged, 1)
                pool.wait_ge(staged, 5 * p + 4)
                pool.tensor_copy(vst[k][0:100, 1:5, :], dv[0:100, 1:5, p * P:(p + 1) * P]).then_inc(staged, 1)
                pool.wait_ge(staged, 5 * p + 5)

            stage(0)
            stage(1)
            pool.wait_ge(o_normed, len(WIN))
            pool.wait_ge(gr_silu, 1)
            for hd in range(GLA_HEADS):
                pool.tensor_tensor(oT[:, hd, :], oT[:, hd, :], pja[:, 4 + hd, :], ALU.mult).then_inc(o_out, 1)
            for hd in range(GLA_HEADS):
                pool.wait_ge(o_out, hd + 1)
                pool.tensor_copy(ah[:, 4 + hd, :], oT[:, hd, :]).then_inc(g_hi, 1)
            for hd in range(GLA_HEADS):
                pool.wait_ge(g_hi, hd + 1)
                pool.tensor_tensor(al[:, 4 + hd, :], oT[:, hd, :], ah[:, 4 + hd, :].bitcast(F32),
                                   ALU.subtract).then_inc(g_lo, 1)
            pool.wait_ge(g_lo, GLA_HEADS)
            stage(2)
            stage(3)
            run(U_OUT + 2, U_END - U_OUT - 2)

        @block.scalar
        def _(act):
            def hi(u, i=None):
                slot = u % RING
                if u == U_MIX + M_IKW:
                    act.wait_ge(ikw_loaded, 16)
                if i is None and u >= U_END:
                    return
                act.wait_ge(w_in_slot[slot], at(i, 16, 16 * (u // RING + 1)))
                act.wait_ge(w_used, at(i, RING, u + 1))
                act.activation(wh[:, slot, :], raw[:, slot, :], ACT.Copy).then_inc(w_hi, 1)

            act.sem_inc(exp_done, 2)

            def prep_hi(norm, d, h_count):
                act.wait_ge(h_done, h_count + 1)
                tk = tokens_of(norm)
                act.activation(xh[:, d, tk], h[:, d, tk], ACT.Copy, scale=gains[:, norm, d:d + 1]).then_inc(x_hi, 1)

            def root(norm):
                act.wait_ge(inv_done, norm + 1)
                part = rstd[:, tokens_of(norm)]
                act.activation(part, part, ACT.Sqrt).then_inc(rstd_done, 1)

            def ffn(u0, number, norm):
                u = u0
                hd = H_FFN[number]
                ft = number * FT
                tk = tokens_of(norm)
                for f0, cnt in GROUPS:
                    def body(i, b):
                        for j in range(2):
                            hi(u + 4 * b + 2 * j + 2, i)
                            hi(u + 4 * b + 2 * j + 3, i)
                            if i is None and j == 0:
                                root(norm)
                            act.wait_ge(gate_scaled, at(i, 2, ft + f0 + 2 * b + j + 1))
                            act.activation(t0[:, tk], t0[:, tk], ACT.Silu).then_inc(silu_done, 1)

                    first = 1 if f0 == 0 else 0
                    if first:
                        body(None, 0)
                    else:
                        act.activation(scrap[:, :], scrap[:, :], ACT.Silu).then_inc(scrap_done, 1)
                        scrap_n[0] += 1
                        act.wait_ge(scrap_done, scrap_n[0])
                    with act.Fori(0, cnt // 2 - first) as i:
                        body(i, first)
                    u += 2 * cnt
                    last = f0 == GROUPS[-1][0]
                    for d in range(KT):
                        hi(u + d + 2)
                        if last and number == 0:
                            prep_hi(1, d, hd + d)
                        elif last:
                            act.wait_ge(sq_done, 3 * KT + d + 1)
                            act.activation(h[:, d, tk], h[:, d, tk], ACT.Copy,
                                           scale=gains[:, 3, d:d + 1]).then_inc(y_done, 1)
                    u += KT
                    hd += KT

            scrap_n = [1]
            act.wait_ge(scrap_done, 1)

            for n in range(1, 10, 2):
                keep_x(act, n)
                if n == 5:
                    hi(0)
            act.wait_ge(vecs_kept, 1)
            for d in range(KT):
                prep_hi(0, d, d)
                if d == 3:
                    hi(1)
            for d in range(KT):
                if d >= 2:
                    act.wait_ge(ss_done, d - 1)
                act.activation(t01[:, 1 - d % 2, :], h[:, d, :], ACT.Square).then_inc(sq0_done, 1)
            ffn(U_FFN1, 0, 0)
            act_mixer(act, hi, prep_hi, root)
            ffn(U_FFN2, 1, 2)
            act.wait_ge(inv_done, 4)
            act.activation(rout, rout, ACT.Sqrt).then_inc(rstd_done, 1)
            keep_y(act, 1)

        @block.vector
        def _(dve):
            dve.memset(scrap[:, :], 0.0).then_inc(scrap_done, 1)
            for free in (up_scaled, lg_done, pt_kept, m_lo, diag_done, pv_done):
                dve.sem_inc(free, 2)
            dve.sem_inc(top_taken, 2)
            for start in (a_prod, a_lo):
                dve.sem_inc(start, ONE)

            def prep(norm, d, h_count):
                n = norm * KT + d
                if d == 0:
                    if norm:
                        dve.wait_ge(var_done, norm)
                    dve.memset(ss[:, :], 0.0).then_inc(ss_zero, 1)
                tk = tokens_of(norm)
                dve.wait_ge(h_done, h_count + 1)
                if n:
                    dve.wait_ge(ss_done, n)
                dve.tensor_tensor(t1[:, tk], h[:, d, tk], h[:, d, tk], ALU.mult).then_inc(sq_done, 1)
                dve.wait_ge(sq_done, n + 1)
                dve.wait_ge(ss_zero, norm + 1)
                dve.tensor_tensor(ss[:, tk], ss[:, tk], t1[:, tk], ALU.add).then_inc(ss_done, 1)

            def prep_lo(norm, d):
                n = norm * KT + d
                dve.wait_ge(x_hi, n + 1)
                tk = tokens_of(norm)
                dve.scalar_tensor_tensor(out=xl[:, d, tk], in0=h[:, d, tk], scalar=gains[:, norm, d:d + 1],
                                         in1=xh[:, d, tk].bitcast(F32), op0=ALU.mult,
                                         op1=ALU.subtract).then_inc(x_lo, 1)

            def invert(norm):
                dve.wait_ge(norm_sum, norm + 1)
                part = rstd[:, tokens_of(norm)]
                dve.tensor_scalar(as_parts(part, norm), psum_parts(6, norm), 1.0 / D, EPS, ALU.mult,
                                  ALU.add).then_inc(var_done, 1)
                dve.wait_ge(var_done, norm + 1)
                dve.reciprocal(part, part).then_inc(inv_done, 1)

            def ffn(u0, number, norm):
                u = u0
                hd = H_FFN[number]
                ft = number * FT
                tk = tokens_of(norm)
                dve.wait_ge(rstd_done, norm + 1)
                for f0, cnt in GROUPS:
                    with dve.Fori(0, cnt // 2) as i:
                        for j in range(2):
                            F = ft + f0 + j
                            bank = 4 * j
                            dve.wait_ge(w_used, at(i, 4, u + 2 * j + RING + 1))
                            dve.wait_ge(a_prod, ONE + at(i, 2, F))
                            dve.tensor_tensor(as_parts(t0[:, tk], norm), psum_parts(bank, norm), as_parts(rstd[:, tk], norm),
                                              ALU.mult).then_inc(gate_scaled, 1)
                            dve.wait_ge(w_used, at(i, 4, u + 2 * j + 1 + RING + 1))
                            dve.wait_ge(a_lo, ONE + at(i, 2, F))
                            dve.tensor_tensor(as_parts(t1[:, tk], norm), psum_parts(bank + 2, norm),
                                              as_parts(rstd[:, tk], norm), ALU.mult).then_inc(up_scaled, 1)
                            dve.wait_ge(silu_done, at(i, 2, F + 1))
                            dve.wait_ge(up_scaled, at(i, 2, F + 3))
                            dve.tensor_tensor(t1[:, tk], t0[:, tk], t1[:, tk], ALU.mult).then_inc(a_prod, 1)
                            dve.wait_ge(a_prod, ONE + at(i, 2, F + 1))
                            dve.tensor_copy(ah[:, i * 2 + j, tk], t1[:, tk]).then_inc(a_hi, 1)
                            dve.wait_ge(a_hi, at(i, 2, F + 1))
                            dve.tensor_tensor(al[:, i * 2 + j, tk], t1[:, tk], ah[:, i * 2 + j, tk].bitcast(F32),
                                              ALU.subtract).then_inc(a_lo, 1)
                    u += 2 * cnt
                    last = f0 == GROUPS[-1][0]
                    for d in range(KT):
                        bank = 2 * (d % 4)
                        dve.wait_ge(w_used, u + d + RING + 1)
                        dve.wait_ge(h_done, hd - KT + d + 1)
                        dve.scalar_tensor_tensor(out=as_parts(h[:, d, tk], norm), in0=psum_parts(bank, norm), scalar=0.5,
                                                 in1=as_parts(h[:, d, tk], norm), op0=ALU.mult, op1=ALU.add).then_inc(h_done, 1)
                        if last:
                            prep(norm + 1, d, hd + d)
                            if number == 0:
                                prep_lo(norm + 1, d)
                    u += KT
                    hd += KT

            for n in range(0, 10, 2):
                if n == 4:
                    dve.wait_ge(vecs_turned, 1)
                    dve.tensor_copy(vecs[:, :], ps[:, 7, 0:4 * KT + 3]).then_inc(vecs_kept, 1)
                keep_x(dve, n)
            dve.wait_ge(x_kept, 5)
            dve.wait_ge(x_kept_act, 5)
            dve.sem_inc(h_done, KT)
            dve.wait_ge(vecs_kept, 1)
            dve.memset(ss[:, :], 0.0).then_inc(ss_zero, 1)
            for d in range(KT):
                prep_lo(0, d)
            for d in range(KT):
                dve.wait_ge(sq0_done, d + 1)
                dve.wait_ge(ss_zero, 1)
                if d:
                    dve.wait_ge(ss_done, d)
                dve.tensor_tensor(ss[:, :], ss[:, :], t01[:, 1 - d % 2, :], ALU.add).then_inc(ss_done, 1)
            dve.sem_inc(sq_done, KT)
            invert(0)
            ffn(U_FFN1, 0, 0)
            invert(1)
            dve_mixer(dve, prep, prep_lo)
            invert(2)
            ffn(U_FFN2, 1, 2)
            dve.wait_ge(norm_sum, 4)
            dve.tensor_scalar(rout, ps[:, 7, 0:4], 1.0 / D, EPS, ALU.mult, ALU.add).then_inc(var_done, 1)
            dve.wait_ge(var_done, 4)
            dve.reciprocal(rout, rout).then_inc(inv_done, 1)
            keep_y(dve, 0)

        @block.tensor
        def _(pe):
            pe.sem_inc(w_used, RING)
            pe.sem_inc(pt_done, 2)

            def product(u, bank, m, rh, rl, kts, i=None, before_k=None, tiles=range(KT), norm=1):
                slot = u % RING
                pe.wait_ge(w_split, at(i, RING, u + RING + 1))
                for k in range(kts):
                    if before_k:
                        before_k(k)
                    for n, (w, r) in enumerate(((wh, rh), (wh, rl), (wl, rh))):
                        for a, t, width in parts_of(norm):
                            mm = pe.matmul(ps[0:m, bank + a, 0:width], w[:, slot, k * P:k * P + m],
                                           r[:, tiles[k], t:t + width], start=(k == 0 and n == 0),
                                           stop=(k == kts - 1 and n == 2))
                mm.then_inc(w_used, 1)

            def norm_product(norm):
                pe.wait_ge(ss_done, KT * (norm + 1))
                for a, t, width in parts_of(norm):
                    mm = pe.matmul(ps[:, 6 + a, 0:width], ones[:, :], ss[:, t:t + width], start=True,
                                   stop=True)
                mm.then_inc(norm_sum, 1)

            def ffn(u0, number, norm):
                u = u0
                hd = H_FFN[number]
                ft = number * FT
                tk = tokens_of(norm)
                for f0, cnt in GROUPS:
                    def x_ready(k):
                        pe.wait_ge(x_lo, KT * norm + k + 1)

                    def body(i, b):
                        for j in range(2):
                            pe.wait_ge(h_done, hd - 2 + 2 * j)
                            pe.wait_ge(up_scaled, at(i, 2, ft + f0 + 2 * b + j + 1))
                            product(u + 4 * b + 2 * j, 4 * j, P, xh, xl, KT, i, x_ready if j == 0 else None,
                                    norm=norm)
                            if i is None and j == 0 and norm:
                                norm_product(norm)
                            if i is None and j == 1:
                                pe.wait_ge(var_done, norm + 1)
                            product(u + 4 * b + 2 * j + 1, 4 * j + 2, P, xh, xl, KT, i, norm=norm)
                            if i is None and j == 0 and not norm:
                                norm_product(norm)

                    first = 1 if f0 == 0 else 0
                    if first:
                        body(None, 0)
                    with pe.Fori(0, cnt // 2 - first) as i:
                        body(i, first)
                    u += 2 * cnt
                    F = ft + f0

                    def a_ready(k):
                        pe.wait_ge(a_lo, ONE + F + k + 1)

                    with pe.Fori(0, KT // 4) as i:
                        for j in range(4):
                            pe.wait_ge(up_scaled, F + cnt + (1 if j == 0 else 2))
                            pe.wait_ge(h_done, at(i, 4, hd + j - 3))
                            product(u + j, 2 * j, P, ah, al, cnt, i, a_ready if j == 0 else None, norm=norm)
                    u += KT
                    hd += KT

            pe.wait_ge(consts, 2)
            for n in range(10):
                t, half = n // 2, n % 2
                w = x_cols(n)[1]
                if n == 4:
                    pe.wait_ge(const_loaded, 96)
                    pe.transpose(ps[:, 7, 0:4 * KT + 3], vec_rows[:, :],
                                 ident[0:4 * KT + 3, 0:4 * KT + 3]).then_inc(vecs_turned, 1)
                if n == 7:
                    pe.wait_ge(vecs_kept, 1)
                pe.wait_ge(x_loaded[t], 16)
                if n >= 8:
                    pe.wait_ge(x_kept, 5 - 4 if n == 8 else 1)
                    pe.wait_ge(x_kept_act, 1)
                for k in range(4):
                    c = (4 * half + k) * P
                    mm = pe.transpose(ps[:, n % 8, k * w:(k + 1) * w], xin[0:w, t, c:c + P], ident[0:w, 0:w])
                mm.then_inc(x_turned, 1)
            ffn(U_FFN1, 0, 0)
            pe_mixer(pe, product, norm_product)
            ffn(U_FFN2, 1, 2)
            pe.wait_ge(h_done, H_END - 2)
            for n in range(8):
                half, t = divmod(n, 4)
                tokens = slice(META + t * P, META + (t + 1) * P)
                if n == 4:
                    pe.wait_ge(ss_done, 4 * KT)
                    for c in range(4):
                        mm = pe.matmul(ps[:, 7, c:c + 1], ss[:, META + c * P:META + (c + 1) * P], ones[:, 0:1],
                                       start=True, stop=True)
                    mm.then_inc(norm_sum, 1)
                if n == 7:
                    pe.wait_ge(var_done, 4)
                pe.wait_ge(y_done, 4 * (half + 1))
                for k in range(4):
                    mm = pe.transpose(ps[:, n, k * P:(k + 1) * P], h[:, 4 * half + k, tokens], ident[:, :])
                mm.then_inc(y_turned, 1)


INPUTS = ["x", "meta_tokens", "ffn1_norm", "ffn1_w_gate", "ffn1_w_up", "ffn1_w_down", "mix_norm", "w_in", "gla_w_a2",
          "gla_b_a", "gla_head_norm", "w_out", "ffn2_norm", "ffn2_w_gate", "ffn2_w_up", "ffn2_w_down", "final_norm"]


def rope_tables():
    import numpy as np
    f32 = np.float32
    inv = (f32(1.0) / (f32(10000.0) ** (np.arange(0, HD, 2, dtype=f32) / f32(HD)))).astype(f32)
    ang = (inv[:, None] * np.arange(TOK, dtype=f32)[None, :]).astype(f32)
    cos, sin = np.cos(ang).astype(f32), np.sin(ang).astype(f32)
    return np.concatenate([cos] * 4), np.concatenate([-sin, sin] * 2)


def kernel(**inputs):
    import numpy as np
    import concourse.bacc as bacc
    from concourse.bass_utils import run_bass_kernel_spmd as run

    nc = bacc.Bacc("TRN2", target_bir_lowering=False, num_devices=1)
    arrays, a = {}, {}
    given = {n: np.ascontiguousarray(inputs[n]) for n in INPUTS}
    given["cos_t"], given["sin_t"] = rope_tables()
    for name, v in given.items():
        if name != "meta_tokens" and v.ndim > 1 and v.shape[0] == 1:
            v = v[0]
        arrays[f"in_{name}"] = np.ascontiguousarray(v)
        a[name] = nc.dram_tensor(f"in_{name}", v.shape, F32, kind="ExternalInput").ap()
    out = nc.dram_tensor("out_0", (SEQ, D), F32, kind="ExternalOutput").ap()
    build(nc, a["x"], a["meta_tokens"],
          (a["ffn1_norm"], a["ffn1_w_gate"], a["ffn1_w_up"], a["ffn1_w_down"]),
          (a["ffn2_norm"], a["ffn2_w_gate"], a["ffn2_w_up"], a["ffn2_w_down"]),
          a["mix_norm"], a["w_in"], a["gla_w_a2"], a["gla_b_a"], a["gla_head_norm"], a["w_out"], a["final_norm"],
          a["cos_t"], a["sin_t"], out)
    r = run(nc, [arrays], core_ids=[0])
    return r.results[0]["out_0"].reshape(1, SEQ, D)
```
